# Optimizing a Trainium2 kernel written in Bass

```python
import jax, jax.numpy as jnp
from jax import lax
import numpy as np

D_MODEL = 1024
BATCH = 1
SEQ = 512
DEPTH = 1

HEAD_DIM = 64
N_HEADS = D_MODEL // HEAD_DIM
NSA_HEADS = N_HEADS // 2
SWA_HEADS = N_HEADS - NSA_HEADS
NSA_KV = 2
NSA_GROUP = NSA_HEADS // NSA_KV
SWA_KV = 2
SWA_GROUP = SWA_HEADS // SWA_KV
MIX_WIDTH = (NSA_HEADS + SWA_HEADS) * HEAD_DIM
SWA_WINDOW = 128
NSA_WINDOW = 512
CMP_LEN = 32
CMP_STRIDE = 16
CMP_HIDDEN = 256
SLC_BLOCK = 64
SLC_TOPK = 16
NSA_BRANCHES = 3
BAND_QBLOCK = 128
SLC_QCHUNK = 64
D_FF = 2816
CONV_WIDTH = 3
ROPE_THETA = 10000.0
RMS_EPS = 1e-6
NEG = -1e30
BIG = 1e9

IN_SIZES = [
    NSA_HEADS * HEAD_DIM,
    NSA_KV * HEAD_DIM, NSA_KV * HEAD_DIM,
    NSA_KV * HEAD_DIM, NSA_KV * HEAD_DIM,
    NSA_KV * HEAD_DIM, NSA_KV * HEAD_DIM,
    NSA_HEADS * NSA_BRANCHES,
    SWA_HEADS * HEAD_DIM,
    SWA_KV * HEAD_DIM, SWA_KV * HEAD_DIM,
]
IN_WIDTH = int(sum(IN_SIZES))
IN_SPLITS = [int(v) for v in np.cumsum(IN_SIZES)[:-1]]


def rms_norm(x, g):
    xf = x.astype(jnp.float32)
    y = xf * lax.rsqrt(jnp.mean(xf * xf, axis=-1, keepdims=True) + RMS_EPS)
    return (y * g.astype(jnp.float32)).astype(x.dtype)

def rope(x, pos):
    half = HEAD_DIM // 2
    inv = ROPE_THETA ** (-jnp.arange(half, dtype=jnp.float32) / half)
    ang = pos.astype(jnp.float32)[:, None] * inv[None, :]
    cos = jnp.cos(ang)[None, :, None, :]
    sin = jnp.sin(ang)[None, :, None, :]
    xf = x.astype(jnp.float32)
    x1, x2 = xf[..., :half], xf[..., half:]
    return jnp.concatenate([x1 * cos - x2 * sin, x2 * cos + x1 * sin], axis=-1).astype(x.dtype)

def compress(kv, pe, w1, w2):
    B, S, H, D = kv.shape
    ch = kv.reshape(B, S // CMP_STRIDE, CMP_STRIDE, H, D)
    blocks = jnp.concatenate([ch[:, :-1], ch[:, 1:]], axis=2)
    blocks = blocks + pe[None, None, :, None, :]
    nc = blocks.shape[1]
    flat = blocks.transpose(0, 1, 3, 2, 4).reshape(B, nc, H, CMP_LEN * D)
    return jax.nn.gelu(flat @ w1) @ w2

def compressed_attention(q, kc, vc, t):
    nc = kc.shape[1]
    s = jnp.einsum('bthgd,bchd->bhgtc', q, kc).astype(jnp.float32) * (HEAD_DIM ** -0.5)
    ends = jnp.arange(nc) * CMP_STRIDE + CMP_LEN - 1
    valid = ends[None, :] <= t[:, None]
    s = jnp.where(valid, s, NEG)
    m = jnp.max(s, axis=-1, keepdims=True)
    e = jnp.where(valid, jnp.exp(s - m), 0.0)
    p = e / jnp.maximum(jnp.sum(e, axis=-1, keepdims=True), 1e-30)
    o = jnp.einsum('bhgtc,bchd->bthgd', p.astype(vc.dtype), vc)
    return o, p

def overlap_matrix(nc, nsb):
    i = np.arange(nc)[:, None]
    j = np.arange(nsb)[None, :]
    cs, ce = i * CMP_STRIDE, i * CMP_STRIDE + CMP_LEN - 1
    bs, be = j * SLC_BLOCK, j * SLC_BLOCK + SLC_BLOCK - 1
    return jnp.asarray(((cs <= be) & (ce >= bs)).astype(np.float32))

def select_blocks(p_cmp, t, nsb):
    p_grp = jnp.sum(p_cmp, axis=2)
    imp = jnp.einsum('bhtc,cj->bhtj', p_grp, overlap_matrix(p_cmp.shape[-1], nsb))
    jb = jnp.arange(nsb)[None, :]
    tb = (t // SLC_BLOCK)[:, None]
    forced = (jb == 0) | (jb == tb) | (jb == tb - 1)
    causal = jb * SLC_BLOCK <= t[:, None]
    score = jnp.where(forced, BIG, jnp.where(causal, imp, NEG))
    _, idx = lax.top_k(score, min(SLC_TOPK, nsb))
    return idx

def selected_attention(q, k, v, idx, t):
    B, S, Hkv, G, D = q.shape
    nsb = S // SLC_BLOCK
    K = idx.shape[-1]
    nqc = S // SLC_QCHUNK
    kb = k.reshape(B, nsb, SLC_BLOCK, Hkv, D).transpose(0, 3, 1, 2, 4)
    vb = v.reshape(B, nsb, SLC_BLOCK, Hkv, D).transpose(0, 3, 1, 2, 4)
    qc = q.reshape(B, nqc, SLC_QCHUNK, Hkv, G, D).transpose(1, 0, 2, 3, 4, 5)
    ic = idx.reshape(B, Hkv, nqc, SLC_QCHUNK, K).transpose(2, 0, 1, 3, 4)
    tc = t.reshape(nqc, SLC_QCHUNK)
    gather = jax.vmap(jax.vmap(lambda blk, ix: blk[ix]))
    offs = jnp.arange(SLC_BLOCK)

    def chunk(args):
        qx, ix, tx = args
        kg = gather(kb, ix)
        vg = gather(vb, ix)
        s = jnp.einsum('bqhgd,bhqnkd->bhgqnk', qx, kg).astype(jnp.float32) * (HEAD_DIM ** -0.5)
        pos = ix[..., None] * SLC_BLOCK + offs
        mask = pos <= tx[None, None, :, None, None]
        s = jnp.where(mask[:, :, None], s, NEG)
        p = jax.nn.softmax(s.reshape(B, Hkv, G, SLC_QCHUNK, K * SLC_BLOCK), axis=-1)
        p = p.reshape(B, Hkv, G, SLC_QCHUNK, K, SLC_BLOCK).astype(vg.dtype)
        return jnp.einsum('bhgqnk,bhqnkd->bqhgd', p, vg)

    o = lax.map(chunk, (qc, ic, tc))
    return o.transpose(1, 0, 2, 3, 4, 5).reshape(B, S, Hkv, G, D)

def banded_attention(q, k, v, window, sinks):
    B, S, Hkv, G, D = q.shape
    QB = BAND_QBLOCK
    span = window + QB
    kp = jnp.pad(k, ((0, 0), (window, 0), (0, 0), (0, 0)))
    vp = jnp.pad(v, ((0, 0), (window, 0), (0, 0), (0, 0)))
    a = jnp.arange(QB)[:, None]
    j = jnp.arange(span)[None, :]
    band = (j > a) & (j <= a + window)
    scale = HEAD_DIM ** -0.5

    def block(i):
        start = i * QB
        qb = lax.dynamic_slice_in_dim(q, start, QB, axis=1)
        kb = lax.dynamic_slice_in_dim(kp, start, span, axis=1)
        vb = lax.dynamic_slice_in_dim(vp, start, span, axis=1)
        s = jnp.einsum('bqhgd,bkhd->bhgqk', qb, kb).astype(jnp.float32) * scale
        mask = band & (start + j - window >= 0)
        s = jnp.where(mask, s, NEG)
        m = jnp.max(s, axis=-1, keepdims=True)
        if sinks is not None:
            sk = sinks.astype(jnp.float32)[None, :, :, None, None]
            m = jnp.maximum(m, sk)
            e = jnp.exp(s - m)
            den = jnp.sum(e, axis=-1, keepdims=True) + jnp.exp(sk - m)
        else:
            e = jnp.exp(s - m)
            den = jnp.sum(e, axis=-1, keepdims=True)
        p = (e / den).astype(vb.dtype)
        return jnp.einsum('bhgqk,bkhd->bqhgd', p, vb)

    o = lax.map(block, jnp.arange(S // QB))
    return o.transpose(1, 0, 2, 3, 4, 5).reshape(B, S, Hkv, G, D)

def causal_dwconv(x, w, b):
    C = x.shape[-1]
    y = lax.conv_general_dilated(
        x, w[:, None, :].astype(x.dtype), window_strides=(1,),
        padding=[(CONV_WIDTH - 1, 0)], dimension_numbers=('NWC', 'WIO', 'NWC'),
        feature_group_count=C)
    return y + b

def hybrid_layer(h, w_in, w_out, attn_pre_norm, attn_post_norm, nsa_out_norm, swa_out_norm,
                 cmp_pos, cmp_w1, cmp_w2, swa_sinks, ffn_pre_norm, ffn_post_norm,
                 w_up, conv_w, conv_b, w_down):
    B, S, _ = h.shape
    t = jnp.arange(S)
    hn = rms_norm(h, attn_pre_norm)
    proj = hn @ w_in
    (q_n, k_c, v_c, k_s, v_s, k_w, v_w, g_n, q_w, k_sw, v_sw) = jnp.split(proj, IN_SPLITS, axis=-1)
    kvh = lambda z, n: z.reshape(B, S, n, HEAD_DIM)

    qn = rope(kvh(q_n, NSA_HEADS), t).reshape(B, S, NSA_KV, NSA_GROUP, HEAD_DIM)
    k_c, k_s, k_w = (rope(kvh(z, NSA_KV), t) for z in (k_c, k_s, k_w))
    v_c, v_s, v_w = (kvh(z, NSA_KV) for z in (v_c, v_s, v_w))
    ckv = jax.vmap(compress)(jnp.stack([k_c, v_c]), cmp_pos, cmp_w1, cmp_w2)
    o_cmp, p_cmp = compressed_attention(qn, ckv[0], ckv[1], t)
    idx = select_blocks(p_cmp, t, S // SLC_BLOCK)
    o_slc = selected_attention(qn, k_s, v_s, idx, t)
    o_win = banded_attention(qn, k_w, v_w, NSA_WINDOW, None)
    gates = jax.nn.sigmoid(g_n).reshape(B, S, NSA_KV, NSA_GROUP, NSA_BRANCHES)
    o_nsa = gates[..., 0:1] * o_cmp + gates[..., 1:2] * o_slc + gates[..., 2:3] * o_win
    o_nsa = rms_norm(o_nsa.reshape(B, S, NSA_HEADS * HEAD_DIM), nsa_out_norm)

    qw = rope(kvh(q_w, SWA_HEADS), t).reshape(B, S, SWA_KV, SWA_GROUP, HEAD_DIM)
    kw = rope(kvh(k_sw, SWA_KV), t)
    o_swa = banded_attention(qw, kw, kvh(v_sw, SWA_KV), SWA_WINDOW,
                             swa_sinks.reshape(SWA_KV, SWA_GROUP))
    o_swa = rms_norm(o_swa.reshape(B, S, SWA_HEADS * HEAD_DIM), swa_out_norm)

    mixed = jnp.concatenate([o_nsa, o_swa], axis=-1) @ w_out
    h = h + rms_norm(mixed, attn_post_norm)

    hn = rms_norm(h, ffn_pre_norm)
    u = causal_dwconv(hn @ w_up, conv_w, conv_b)
    gate, up = jnp.split(u, 2, axis=-1)
    y = (jax.nn.gelu(gate, approximate=True) * up) @ w_down
    return h + rms_norm(y, ffn_post_norm)

def first_inputs(seed: int = 0) -> dict:
    key = jax.random.key(seed)
    ks = jax.random.split(key, 17)
    f = jnp.float32
    L = DEPTH
    nrm = lambda k, shape, sc: jax.random.normal(k, shape, f) * sc
    gain = lambda k, shape: 1.0 + 0.05 * jax.random.normal(k, shape, f)
    return {
        "x": nrm(ks[0], (BATCH, SEQ, D_MODEL), 1.0),
        "w_in": nrm(ks[1], (L, D_MODEL, IN_WIDTH), D_MODEL ** -0.5),
        "w_out": nrm(ks[2], (L, MIX_WIDTH, D_MODEL), MIX_WIDTH ** -0.5),
        "attn_pre_norm": gain(ks[3], (L, D_MODEL)),
        "attn_post_norm": gain(ks[4], (L, D_MODEL)),
        "nsa_out_norm": gain(ks[5], (L, NSA_HEADS * HEAD_DIM)),
        "swa_out_norm": gain(ks[6], (L, SWA_HEADS * HEAD_DIM)),
        "cmp_pos": nrm(ks[7], (L, 2, CMP_LEN, HEAD_DIM), 0.1),
        "cmp_w1": nrm(ks[8], (L, 2, CMP_LEN * HEAD_DIM, CMP_HIDDEN), (CMP_LEN * HEAD_DIM) ** -0.5),
        "cmp_w2": nrm(ks[9], (L, 2, CMP_HIDDEN, HEAD_DIM), CMP_HIDDEN ** -0.5),
        "swa_sinks": nrm(ks[10], (L, SWA_HEADS), 0.5),
        "ffn_pre_norm": gain(ks[11], (L, D_MODEL)),
        "ffn_post_norm": gain(ks[12], (L, D_MODEL)),
        "w_up": nrm(ks[13], (L, D_MODEL, 2 * D_FF), D_MODEL ** -0.5),
        "conv_w": nrm(ks[14], (L, CONV_WIDTH, 2 * D_FF), CONV_WIDTH ** -0.5),
        "conv_b": nrm(ks[15], (L, 2 * D_FF), 0.02),
        "w_down": nrm(ks[16], (L, D_FF, D_MODEL), D_FF ** -0.5),
    }

def first_block(x, w_in, w_out, attn_pre_norm, attn_post_norm, nsa_out_norm, swa_out_norm,
              cmp_pos, cmp_w1, cmp_w2, swa_sinks, ffn_pre_norm, ffn_post_norm,
              w_up, conv_w, conv_b, w_down):
    h = x
    for l in range(DEPTH):
        h = hybrid_layer(h, w_in[l], w_out[l], attn_pre_norm[l], attn_post_norm[l],
                         nsa_out_norm[l], swa_out_norm[l], cmp_pos[l], cmp_w1[l], cmp_w2[l],
                         swa_sinks[l], ffn_pre_norm[l], ffn_post_norm[l],
                         w_up[l], conv_w[l], conv_b[l], w_down[l])
    return h


DEPTH_2 = 2

BLOCK_Q = 128
EPS = 1e-6
NEG_INF = -1e30

MLA_HEADS = 8
MLA_Q_RANK = 256
MLA_KV_RANK = 128
MLA_NOPE = 64
MLA_ROPE = 32
MLA_QK = MLA_NOPE + MLA_ROPE
MLA_V = 64
SB_HEADS = 8
SB_DIM = 64
SB_WIDTH = SB_HEADS * SB_DIM
FOX_HEADS = 16
FOX_DIM = 64
FOX_WIDTH = FOX_HEADS * FOX_DIM
D_FF_2 = ((8 * D_MODEL // 3 + 255) // 256) * 256

EVEN_IN = MLA_Q_RANK + MLA_KV_RANK + MLA_ROPE + 3 * SB_WIDTH
EVEN_OUT = MLA_HEADS * MLA_V + SB_WIDTH
ODD_IN = 3 * FOX_WIDTH + FOX_HEADS
ODD_OUT = FOX_WIDTH


def rms_norm_2(x, g):
    xf = x.astype(jnp.float32)
    y = xf * lax.rsqrt(jnp.mean(xf * xf, axis=-1, keepdims=True) + EPS)
    return (y * g.astype(jnp.float32)).astype(x.dtype)

def split_last(x, sizes):
    return jnp.split(x, [int(v) for v in np.cumsum(sizes)[:-1]], axis=-1)

def heads_first(x):
    return x.transpose(0, 2, 1, 3)

def merge_heads(x):
    b, h, s, d = x.shape
    return x.transpose(0, 2, 1, 3).reshape(b, s, h * d)

def rope_tail(x, positions):
    nope, r = x[..., :-MLA_ROPE], x[..., -MLA_ROPE:]
    half = MLA_ROPE // 2
    inv_freq = ROPE_THETA ** (-jnp.arange(half, dtype=jnp.float32) / half)
    ang = positions.astype(jnp.float32)[..., None] * inv_freq
    cos, sin = jnp.cos(ang)[:, :, None, :], jnp.sin(ang)[:, :, None, :]
    r1, r2 = r[..., :half].astype(jnp.float32), r[..., half:].astype(jnp.float32)
    rot = jnp.concatenate([r1 * cos - r2 * sin, r2 * cos + r1 * sin], axis=-1)
    return jnp.concatenate([nope, rot.astype(x.dtype)], axis=-1)

def sweep_query_blocks(block_fn, q):
    b, h, s, _ = q.shape
    out = lax.map(block_fn, jnp.arange(s // BLOCK_Q))
    nb, _, _, bq, dv = out.shape
    return out.transpose(1, 2, 0, 3, 4).reshape(b, h, nb * bq, dv)

def causal_softmax_attention(q, k, v, scale, decay=None):
    s = k.shape[2]
    k_idx = jnp.arange(s)

    def block(i):
        start = i * BLOCK_Q
        qb = lax.dynamic_slice_in_dim(q, start, BLOCK_Q, axis=2)
        logits = jnp.einsum('bhqd,bhkd->bhqk', qb, k).astype(jnp.float32) * scale
        if decay is not None:
            cq = lax.dynamic_slice_in_dim(decay, start, BLOCK_Q, axis=2)
            logits = logits + cq[..., :, None] - decay[..., None, :]
        q_idx = start + jnp.arange(BLOCK_Q)
        mask = k_idx[None, :] <= q_idx[:, None]
        p = jax.nn.softmax(jnp.where(mask, logits, NEG_INF), axis=-1)
        return jnp.einsum('bhqk,bhkd->bhqd', p.astype(v.dtype), v)

    return sweep_query_blocks(block, q)

def stick_breaking_attention(q, k, v):
    s = k.shape[2]
    scale = q.shape[-1] ** -0.5
    k_idx = jnp.arange(s)

    def block(i):
        start = i * BLOCK_Q
        qb = lax.dynamic_slice_in_dim(q, start, BLOCK_Q, axis=2)
        z = jnp.einsum('bhqd,bhkd->bhqk', qb, k).astype(jnp.float32) * scale
        q_idx = start + jnp.arange(BLOCK_Q)
        mask = k_idx[None, :] < q_idx[:, None]
        log_beta = jax.nn.log_sigmoid(z)
        log_1m_beta = jnp.where(mask, jax.nn.log_sigmoid(-z), 0.0)
        suffix = lax.cumsum(log_1m_beta, axis=3, reverse=True) - log_1m_beta
        a = jnp.where(mask, jnp.exp(log_beta + suffix), 0.0)
        return jnp.einsum('bhqk,bhkd->bhqd', a.astype(v.dtype), v)

    return sweep_query_blocks(block, q)

def even_mixer(h, positions, w_in, q_a_norm, w_q_up, kv_a_norm, w_kv_up, q_norm, k_norm, w_o):
    b, s, _ = h.shape
    proj = h @ w_in
    cq, ckv, k_rope, sb_qkv = split_last(proj, [MLA_Q_RANK, MLA_KV_RANK, MLA_ROPE, 3 * SB_WIDTH])
    q = (rms_norm_2(cq, q_a_norm) @ w_q_up).reshape(b, s, MLA_HEADS, MLA_QK)
    kv = (rms_norm_2(ckv, kv_a_norm) @ w_kv_up).reshape(b, s, MLA_HEADS, MLA_NOPE + MLA_V)
    k_nope, v = kv[..., :MLA_NOPE], kv[..., MLA_NOPE:]
    k_rope = jnp.broadcast_to(k_rope[:, :, None, :], (b, s, MLA_HEADS, MLA_ROPE))
    k = jnp.concatenate([k_nope, k_rope], axis=-1)
    q = rope_tail(rms_norm_2(q, q_norm), positions)
    k = rope_tail(rms_norm_2(k, k_norm), positions)
    mla = causal_softmax_attention(heads_first(q), heads_first(k), heads_first(v), MLA_QK ** -0.5)
    sq, sk, sv = [heads_first(t.reshape(b, s, SB_HEADS, SB_DIM)) for t in jnp.split(sb_qkv, 3, axis=-1)]
    sb = stick_breaking_attention(sq, sk, sv)
    o = jnp.concatenate([merge_heads(mla), merge_heads(sb)], axis=-1)
    return o @ w_o

def odd_mixer(h, w_in, f_bias, q_norm, k_norm, w_o):
    b, s, _ = h.shape
    proj = h @ w_in
    q, k, v, f_logit = split_last(proj, [FOX_WIDTH, FOX_WIDTH, FOX_WIDTH, FOX_HEADS])
    q = rms_norm_2(q.reshape(b, s, FOX_HEADS, FOX_DIM), q_norm)
    k = rms_norm_2(k.reshape(b, s, FOX_HEADS, FOX_DIM), k_norm)
    v = v.reshape(b, s, FOX_HEADS, FOX_DIM)
    log_f = jax.nn.log_sigmoid(f_logit.astype(jnp.float32) + f_bias.astype(jnp.float32))
    decay = lax.cumsum(log_f, axis=1).transpose(0, 2, 1)
    o = causal_softmax_attention(heads_first(q), heads_first(k), heads_first(v), FOX_DIM ** -0.5, decay)
    return merge_heads(o) @ w_o

def swiglu(h, w_gate, w_up, w_down):
    return (jax.nn.silu(h @ w_gate) * (h @ w_up)) @ w_down

def second_inputs(seed: int = 0) -> dict:
    key = jax.random.key(seed)
    ks = iter(jax.random.split(key, 32))

    def dense(shape):
        return jax.random.normal(next(ks), shape, jnp.float32) * shape[0] ** -0.5

    def gain(n):
        return 1.0 + 0.1 * jax.random.normal(next(ks), (n,), jnp.float32)

    x = jax.random.normal(next(ks), (BATCH, SEQ, D_MODEL), jnp.float32)
    offsets = jax.random.randint(next(ks), (BATCH, 1), 0, SEQ, dtype=jnp.int32)
    positions = (offsets + jnp.arange(SEQ, dtype=jnp.int32)[None, :]).astype(jnp.int32)
    return {
        'x': x,
        'positions': positions,
        'l0_attn_norm': gain(D_MODEL),
        'l0_w_in': dense((D_MODEL, EVEN_IN)),
        'l0_mla_q_a_norm': gain(MLA_Q_RANK),
        'l0_mla_w_q_up': dense((MLA_Q_RANK, MLA_HEADS * MLA_QK)),
        'l0_mla_kv_a_norm': gain(MLA_KV_RANK),
        'l0_mla_w_kv_up': dense((MLA_KV_RANK, MLA_HEADS * (MLA_NOPE + MLA_V))),
        'l0_mla_q_norm': gain(MLA_QK),
        'l0_mla_k_norm': gain(MLA_QK),
        'l0_w_o': dense((EVEN_OUT, D_MODEL)),
        'l0_ffn_norm': gain(D_MODEL),
        'l0_w_gate': dense((D_MODEL, D_FF_2)),
        'l0_w_up': dense((D_MODEL, D_FF_2)),
        'l0_w_down': dense((D_FF_2, D_MODEL)),
        'l1_attn_norm': gain(D_MODEL),
        'l1_w_in': dense((D_MODEL, ODD_IN)),
        'l1_fox_f_bias': 3.0 + 0.5 * jax.random.normal(next(ks), (FOX_HEADS,), jnp.float32),
        'l1_fox_q_norm': gain(FOX_DIM),
        'l1_fox_k_norm': gain(FOX_DIM),
        'l1_w_o': dense((ODD_OUT, D_MODEL)),
        'l1_ffn_norm': gain(D_MODEL),
        'l1_w_gate': dense((D_MODEL, D_FF_2)),
        'l1_w_up': dense((D_MODEL, D_FF_2)),
        'l1_w_down': dense((D_FF_2, D_MODEL)),
    }

def second_block(x, positions,
              l0_attn_norm, l0_w_in, l0_mla_q_a_norm, l0_mla_w_q_up, l0_mla_kv_a_norm,
              l0_mla_w_kv_up, l0_mla_q_norm, l0_mla_k_norm, l0_w_o,
              l0_ffn_norm, l0_w_gate, l0_w_up, l0_w_down,
              l1_attn_norm, l1_w_in, l1_fox_f_bias, l1_fox_q_norm, l1_fox_k_norm, l1_w_o,
              l1_ffn_norm, l1_w_gate, l1_w_up, l1_w_down):
    mixer_params = (
        (l0_attn_norm, l0_w_in, l0_mla_q_a_norm, l0_mla_w_q_up, l0_mla_kv_a_norm,
         l0_mla_w_kv_up, l0_mla_q_norm, l0_mla_k_norm, l0_w_o),
        (l1_attn_norm, l1_w_in, l1_fox_f_bias, l1_fox_q_norm, l1_fox_k_norm, l1_w_o),
    )
    ffn_params = (
        (l0_ffn_norm, l0_w_gate, l0_w_up, l0_w_down),
        (l1_ffn_norm, l1_w_gate, l1_w_up, l1_w_down),
    )
    for layer in range(DEPTH_2):
        norm_g, *mp = mixer_params[layer]
        h = rms_norm_2(x, norm_g)
        if layer % 2 == 0:
            x = x + even_mixer(h, positions, *mp)
        else:
            x = x + odd_mixer(h, *mp)
        f_norm, w_gate, w_up, w_down = ffn_params[layer]
        x = x + swiglu(rms_norm_2(x, f_norm), w_gate, w_up, w_down)
    return x


def setup_inputs(seed=0):
    out = dict(first_inputs(seed))
    for name, value in second_inputs(seed + 1).items():
        if name != "x":
            out[name + "_2"] = value
    return out


def reference(
    x, w_in, w_out, attn_pre_norm, attn_post_norm, nsa_out_norm, swa_out_norm, cmp_pos, cmp_w1,
    cmp_w2, swa_sinks, ffn_pre_norm, ffn_post_norm, w_up, conv_w, conv_b, w_down, positions_2,
    l0_attn_norm_2, l0_w_in_2, l0_mla_q_a_norm_2, l0_mla_w_q_up_2, l0_mla_kv_a_norm_2,
    l0_mla_w_kv_up_2, l0_mla_q_norm_2, l0_mla_k_norm_2, l0_w_o_2, l0_ffn_norm_2, l0_w_gate_2,
    l0_w_up_2, l0_w_down_2, l1_attn_norm_2, l1_w_in_2, l1_fox_f_bias_2, l1_fox_q_norm_2,
    l1_fox_k_norm_2, l1_w_o_2, l1_ffn_norm_2, l1_w_gate_2, l1_w_up_2, l1_w_down_2,
):
    x = first_block(
        x, w_in, w_out, attn_pre_norm, attn_post_norm, nsa_out_norm, swa_out_norm, cmp_pos,
        cmp_w1, cmp_w2, swa_sinks, ffn_pre_norm, ffn_post_norm, w_up, conv_w, conv_b, w_down,
    )
    return second_block(
        x, positions_2, l0_attn_norm_2, l0_w_in_2, l0_mla_q_a_norm_2, l0_mla_w_q_up_2,
        l0_mla_kv_a_norm_2, l0_mla_w_kv_up_2, l0_mla_q_norm_2, l0_mla_k_norm_2, l0_w_o_2,
        l0_ffn_norm_2, l0_w_gate_2, l0_w_up_2, l0_w_down_2, l1_attn_norm_2, l1_w_in_2,
        l1_fox_f_bias_2, l1_fox_q_norm_2, l1_fox_k_norm_2, l1_w_o_2, l1_ffn_norm_2, l1_w_gate_2,
        l1_w_up_2, l1_w_down_2,
    )


_drawn_inputs = setup_inputs


def setup_inputs(seed=0):
    import zlib

    import numpy as np

    out = dict(_drawn_inputs(seed))
    spreads = {}
    factors = {'swa_sinks': 6.745,
     'conv_b': 2.997,
     'l0_mla_q_a_norm_2': 8.0,
     'l0_mla_kv_a_norm_2': 2.849,
     'l0_mla_q_norm_2': 8.0,
     'l0_mla_k_norm_2': 8.0,
     'l1_fox_q_norm_2': 4.805,
     'l1_fox_k_norm_2': 5.897}
    for name, (base, spread) in spreads.items():
        noise = np.random.default_rng([zlib.crc32(name.encode()), seed]).standard_normal(out[name].shape)
        drawn = base * np.exp(spread * noise) if base else spread * noise
        out[name] = __import__('jax').numpy.asarray(drawn.astype(out[name].dtype))
    for name, factor in factors.items():
        out[name] = (out[name] * factor).astype(out[name].dtype)
    return out
```

```python
from contextlib import ExitStack

import concourse.bass as bass
from concourse import mybir

P = 128
SEQ = 512
D = 1024
NT = SEQ // P
KD = D // P
DFF = 2816
KF = DFF // P
HD = 64
EPS = 1e-6
NEG = -1e30
W = 512
SLAB = 1024
TOKW = 528
QR, KVR, ROPE = 256, 128, 32
MQK = 96
CMP, CMPS = 32, 16
SMALLS = 16
NCB = SEQ // CMPS - 1

F32 = mybir.dt.float32
F32R = mybir.dt.float32r
BF16 = mybir.dt.bfloat16
I32 = mybir.dt.int32
ALU = mybir.AluOpType
ACT = mybir.ActivationFunctionType
AX = mybir.AxisListType
EXP_LN = "natural_log_exp_and_others"

TWO_PI_HI = 6.28125
TWO_PI_MID = 0.0019350051879882812
TWO_PI_LO = 3.019916050561e-07
PI = 3.1415925


class Order:

    def __init__(self, sem):
        self.sem, self.n, self.base, self.before, self.newest = sem, 0, 0, 0, None

    def own(self):
        self.n += 1
        self.newest = (self.sem, self.base + self.n)
        return self.sem, 1

    def done(self, sem, value):
        self.newest = (sem, value)
        return sem, 1

    def latest(self):
        return self.newest

    def enter(self, j, per):
        self.before, self.n = self.n, 0
        self.base = self.before + j * per

    def leave(self, count, per):
        assert self.n == per, f"{self.n} steps in the loop's body"
        self.n, self.base = self.before + count * per, 0


def build(nc, A, out):
    top = ExitStack()
    sems = {}

    def sem(name):
        name = shared.get(name, (name, 0))[0]
        if name not in sems:
            sems[name] = top.enter_context(nc.semaphore(name))
        return sems[name]

    shared = {}

    def share(kind, what, counts, start=0):
        for phase, n in counts:
            shared[f"{phase}_{what}"] = (f"{kind}_{what}", start)
            start += n

    NORMS = ["n0", "n1", "n3", "n5", "x2", "n6", "n7", "x3", "n8"]
    RMS = [p for p in NORMS if p[0] == "n"]
    for what in ("tp", "hi", "lo"):
        share("norm", what, [(p, 2 * NT) for p in NORMS])
    share("norm", "sq", [(p, 4 if p == "n1" else 2) for p in RMS])
    share("norm", "var", [(p, 1) for p in RMS])
    share("norm", "y", [(p, 1) for p in RMS])
    share("norm", "xn", [(p, NT) for p in RMS])
    UPS, OUTS = ["up1", "up2", "up3"], ["out1", "down1", "out2", "down2", "out3", "down3"]
    share("up", "acc", [(p, 33) for p in UPS])
    share("up", "s", [(p, 4 * 11 if p == "up1" else 2 * 11) for p in UPS])
    share("up", "h", [(p, KF) for p in UPS], 2)
    for what in ("hi", "lo"):
        share("up", what, [(p, KF) for p in UPS])
    share("out", "acc", [(p, 6) for p in OUTS])
    share("out", "res", [(p, NT) for p in OUTS])
    share("out", "sq", [(p, NT) for p in ("out1", "down1")])
    share("out", "var", [(p, 1) for p in ("out1", "down1")])
    share("out", "y", [(p, 1) for p in ("out1", "down1")])

    def at(name, value):
        name, start = shared.get(name, (name, 0))
        return sem(name), value + start

    def sb(name, shape, dt=F32, ctx=top):
        return ctx.enter_context(nc.sbuf_tensor(name, shape, dt))

    ps = top.enter_context(nc.psum_tensor("ps", [P, 8 * W], F32))

    def bank(b, n=W, at=0, rows=P):
        return ps[0:rows, b * W + at:b * W + at + n]

    h = sb("h", [P, NT, D])
    raw = sb("raw", [P, 2, SLAB])
    w_hi = sb("w_hi", [P, 4, SLAB], F32R)
    w_lo = sb("w_lo", [P, 4, SLAB], F32R)
    gains = sb("gains", [P, 2, D])
    tok = sb("tok", [P, NT * TOKW])
    scratch = sb("scratch", [P, 2, W])
    ident = sb("ident", [P, P])
    ident_b = sb("ident_b", [P, P], BF16)
    causal = sb("causal", [P, P], BF16)
    strict = sb("strict", [P, P], BF16)
    band = sb("band", [P, P], BF16)
    one = sb("one", [P, 1])
    conv = sb("conv", [P, 4, 2 * KF])
    pe_t = sb("pe_t", [HD, 2, 2, CMPS])
    sink = sb("sink", [P, 8])
    neg_sink = sb("neg_sink", [P, 8])
    g_qa = sb("g_qa", [P, QR])
    g_kva = sb("g_kva", [P, KVR])
    g_mq = sb("g_mq", [P, MQK])
    g_mk = sb("g_mk", [P, MQK])
    g_fq = sb("g_fq", [P, HD])
    g_fk = sb("g_fk", [P, HD])
    f_bias = sb("f_bias", [P, 16])
    k_rope = sb("k_rope", [P, NT, ROPE])
    m_cos = sb("m_cos", [P, NT, ROPE])
    m_sin = sb("m_sin", [P, NT, ROPE])
    ss = sb("ss", [P, 32])
    var = sb("var", [P, 32])
    rstd = sb("rstd", [P, 32])
    sq_a = sb("sq_a", [P, 32])
    nmax = sb("nmax", [P, 4])
    den = sb("den", [P, 4])
    esink = sb("esink", [P, 4])
    rg = sb("rg", [P, 2])

    lay = ExitStack()
    xt_hi = sb("xt_hi", [P, KD, SEQ], F32R, lay)
    xt_lo = sb("xt_lo", [P, KD, SEQ], F32R, lay)
    lay.close()
    lay = ExitStack()
    q_st = sb("q_st", [P, 2, SEQ], F32, lay)
    prob = sb("prob", [P, 4, SEQ], F32, lay)
    prob_t = sb("prob_t", [P, 2, SEQ], F32, lay)
    sb_ln = sb("sb_ln", [P, 4, SEQ], F32, lay)
    lay.close()
    lay = ExitStack()
    f_hi = sb("f_hi", [P, 2, CMPS, 62], F32R, lay)
    f_lo = sb("f_lo", [P, 2, CMPS, 62], F32R, lay)
    f_raw = sb("f_raw", [P, 2, CMPS, 62], F32, lay)
    lay.close()
    lay = ExitStack()
    x_hold = sb("x_hold", [P, 2 * KD, SEQ], F32, lay)
    u = ExitStack()
    hid_hi = sb("hid_hi", [P, KF, SEQ], F32R, u)
    hid_lo = sb("hid_lo", [P, KF, SEQ], F32R, u)
    u.close()
    u = ExitStack()
    qt1 = sb("qt1", [HD, 16, SEQ], F32, u)
    kt1 = sb("kt1", [HD, 8, SEQ], F32, u)
    vct = sb("vct", [HD, 2, SEQ], F32, u)
    v1 = sb("v1", [P, NT, 6 * HD], F32, u)
    o1 = sb("o1", [P, NT, D], F32, u)
    rope_c = sb("rope_c", [P, NT, HD], F32, u)
    rope_s = sb("rope_s", [P, NT, HD], F32, u)
    gate = sb("gate", [P, NT, 24], F32, u)
    c_add = sb("c_add", [P, NT, CMP], F32, u)
    c_01 = sb("c_01", [P, NT, CMP], F32, u)
    w2_sb = sb("w2_sb", [P, 2, 2, HD], F32, u)
    kct = sb("kct", [HD, 2, CMP], F32, u)
    vbd = sb("vbd", [P, 2, 4 * HD], F32, u)
    chid = sb("chid", [P, 2, 256], F32, u)
    chid_t = sb("chid_t", [P, 2, 2, 62], F32, u)
    u.close()
    u = ExitStack()
    qm = sb("qm", [MQK, 8, SEQ], F32, u)
    qs = sb("qs", [HD, 8, SEQ], F32, u)
    ksb = sb("ksb", [HD, 8, SEQ], F32, u)
    v2 = sb("v2", [P, NT, D], F32, u)
    ckv_hi = sb("ckv_hi", [P, SEQ], F32R, u)
    ckv_lo = sb("ckv_lo", [P, SEQ], F32R, u)
    kk = ExitStack()
    km = sb("km", [MQK, 8, SEQ], F32, kk)
    kk.close()
    cq_hi = sb("cq_hi", [P, 2, SEQ], F32R, kk)
    cq_lo = sb("cq_lo", [P, 2, SEQ], F32R, kk)
    kk.close()
    u.close()
    u = ExitStack()
    qf = sb("qf", [HD + 2, 16, SEQ], F32, u)
    kf = sb("kf", [HD + 2, 16, SEQ], F32, u)
    v3 = sb("v3", [P, NT, D], F32, u)
    tri = sb("tri", [P, P], F32, u)
    ones = sb("ones", [P, P], F32, u)
    logf = sb("logf", [P, NT, 16], F32, u)
    decay = sb("decay", [P, NT, 16], F32, u)
    u.close()
    u = ExitStack()
    c_raw = sb("c_raw", [2 * KF, 4, P], F32, u)
    pe_raw = sb("pe_raw", [CMPS, 2, P], F32, u)
    pos_i = sb("pos_i", [P, NT], I32, u)
    pos_f = sb("pos_f", [P, NT], F32, u)
    inv_f = sb("inv_f", [P, ROPE // 2], F32, u)
    ang = sb("ang", [P, NT, ROPE // 2], F32, u)
    turn = sb("turn", [P, NT, ROPE // 2], F32, u)
    turn_i = sb("turn_i", [P, NT, ROPE // 2], I32, u)
    red = sb("red", [P, NT, ROPE // 2], F32, u)
    u.close()
    u_hold = sb("u_hold", [P, 2 * KF * SEQ], F32, lay)
    top.push(lay.pop_all())

    tok3 = tok[:, :].rearrange("p (t n) -> p t n", t=NT)
    xn = tok[:, 0:2 * D].rearrange("p (s n) -> p s n", s=2)
    half_u = tok[:, 0:4 * W].rearrange("p (s n) -> p s n", s=4)

    def cols(w, c0, n, kts):
        return w.rearrange("(k p) c -> p k c", p=P)[:, kts, c0:c0 + n] if isinstance(c0, int) else \
            w.rearrange("(k p) c -> p k c", p=P)[:, kts, bass.ds(c0, n)]

    class Phase:

        def __init__(self, name, g0, groups):
            self.name, self.g0, self.groups = name, g0, groups

    IN1 = [(0, 512), (512, 512), (1024, 280), (1304, 512), (1816, 256)]
    IN2 = [(0, 416), (416, 512), (928, 512), (1440, 512)]
    g = 0
    phases = {}
    for name, n in (("in1", 5), ("cmp", 2), ("out1", 2), ("up1", 11), ("down1", 6), ("in2", 4), ("mla", 1),
                    ("out2", 2), ("up2", 11), ("down2", 6), ("in3", 7), ("out3", 2), ("up3", 11), ("down3", 6)):
        phases[name] = Phase(name, g, n)
        g += n
    split, slab_used = sem("split"), sem("slab_used")
    raw_full = [sem(f"raw_full{i}") for i in range(2)]

    block = top.enter_context(nc.Block())

    def sp_slab(e, n, parts):
        if not isinstance(n, int) or n >= 2:
            e.wait_ge(split, 2 * n - 2)
        for off, src in parts:
            k, c = src.shape[1], src.shape[2]
            dst = raw[:, n_slot(n), off:off + (k - 1) * STRIDE[0] + c]
            if k > 1:
                dst = raw[:, n_slot(n), :].rearrange("p (k c) -> p k c", c=STRIDE[0])[:, 0:k, off:off + c]
            else:
                dst = raw[:, n_slot(n), off:off + c].rearrange("p (k c) -> p k c", k=1)
            e.dma_start(dst, src).then_inc(raw_full[n_slot(n)], 32 // len(parts))

    STRIDE = [W]
    SLOT = [0]

    def n_slot(n):
        return SLOT[0] % 2

    def sp_group(e, grp, slabs, stride=W):
        STRIDE[0] = stride
        for s, parts in enumerate(slabs):
            SLOT[0] = s
            sp_slab(e, 4 * grp + s, parts)

    def gain_load(e, n, wait=None):
        if wait:
            e.wait_ge(*wait)
        rows = GAINS[n]
        col = 0
        for r in rows:
            w = r.shape[-1]
            e.dma_start(gains[:, n % 2, col:col + w], r.partition_broadcast(P)).then_inc(
                sem(f"gain_full{n % 2}"), 32 // len(rows))
            col += w

    GAINS = [[A["attn_pre_norm"][0]], [A["nsa_out_norm"][0], A["swa_out_norm"][0]], [A["attn_post_norm"][0]],
             [A["ffn_pre_norm"][0]], [A["ffn_post_norm"][0]], [A["l0_attn_norm_2"]], [A["l0_ffn_norm_2"]],
             [A["l1_attn_norm_2"]], [A["l1_ffn_norm_2"]]]

    def wait_apart(e, s, value):
        e.wait_ge(s, value)
        e.sem_inc(sem("passed"), 1)

    def gain_ready(e, n):
        e.wait_ge(*at(f"gain_full{n % 2}", 32 * (n // 2 + 1)))

    def two_kt(w, c0, n):
        return [[(0, cols(w, c0, n, slice(2 * s, 2 * s + 2)))] for s in range(4)]

    def up_slabs(wg, wu, off_u, gi):
        return [[(0, cols(wg, gi * 256, 256, slice(2 * s, 2 * s + 2))),
                 (256, cols(wu, gi * 256 + off_u, 256, slice(2 * s, 2 * s + 2)))] for s in range(4)]

    def down_slabs(w, c0):
        kts = [slice(2 * s, 2 * s + 2) for s in range(10)] + [slice(20, 21), slice(21, 22)]
        return [[(0, cols(w, c0, W, k))] for k in kts]

    def sp_ffn(e, up, down, wg, wu, off_u, wd, mid):
        with e.Fori(0, up.groups) as gi:
            sp_group(e, gi + up.g0, up_slabs(wg, wu, off_u, gi))
        mid()
        with e.Fori(0, 2) as c:
            slabs = down_slabs(wd, c * W)
            for q in range(3):
                sp_group(e, 3 * c + (down.g0 + q), slabs[4 * q:4 * q + 4])

    @block.sync
    def _(e):
        ph = phases
        for t in range(NT):
            e.dma_start(h[:, t, :], A["x"][0, t * P:(t + 1) * P, :]).then_inc(sem("h_full"), 16)
        gain_load(e, 0)
        for i, (c0, n) in enumerate(IN1):
            sp_group(e, ph["in1"].g0 + i, two_kt(A["w_in"][0], c0, n))
            if i == 0:
                gain_load(e, 1)
        gain_load(e, 2, at("n0_xn", NT))
        for kv in range(2):
            w1 = A["cmp_w1"][0, kv]
            sp_group(e, ph["cmp"].g0 + kv,
                     [[(0, cols(w1, 0, 256, slice(4 * s, 4 * s + 4)))] for s in range(4)], 256)
        with e.Fori(0, 2) as c:
            sp_group(e, c + ph["out1"].g0, two_kt(A["w_out"][0], c * W, W))
        gain_load(e, 3, at("n1_xn", NT))

        def mid1():
            gain_load(e, 4, at("out1_res", NT))
            gain_load(e, 5, at("n3_xn", NT))

        sp_ffn(e, ph["up1"], ph["down1"], A["w_up"][0], A["w_up"][0], DFF, A["w_down"][0], mid1)
        for i, (c0, n) in enumerate(IN2):
            sp_group(e, ph["in2"].g0 + i, two_kt(A["l0_w_in_2"], c0, n))
        gain_load(e, 6, at("down1_res", NT))
        gain_load(e, 7, at("n5_xn", NT))
        qw, kw = A["l0_mla_w_q_up_2"], A["l0_mla_w_kv_up_2"]
        sp_group(e, ph["mla"].g0, [[(0, cols(qw, 0, 384, slice(0, 2)))], [(0, cols(qw, 384, 384, slice(0, 2)))],
                                   [(0, cols(kw, 0, W, slice(0, 1)))], [(0, cols(kw, W, W, slice(0, 1)))]])
        with e.Fori(0, 2) as c:
            sp_group(e, c + ph["out2"].g0, two_kt(A["l0_w_o_2"], c * W, W))
        sp_ffn(e, ph["up2"], ph["down2"], A["l0_w_gate_2"], A["l0_w_up_2"], 0, A["l0_w_down_2"], lambda: None)
        sp_group(e, ph["in3"].g0, two_kt(A["l1_w_in_2"], 3 * D, 16))
        with e.Fori(0, 6) as c:
            sp_group(e, c + (ph["in3"].g0 + 1), two_kt(A["l1_w_in_2"], c * W, W))
        gain_load(e, 8, at("n6_xn", NT))
        with e.Fori(0, 2) as c:
            sp_group(e, c + ph["out3"].g0, two_kt(A["l1_w_o_2"], c * W, W))
        sp_ffn(e, ph["up3"], ph["down3"], A["l1_w_gate_2"], A["l1_w_up_2"], 0, A["l1_w_down_2"], lambda: None)
        for t in range(NT):
            e.wait_ge(*at("down3_res", t + 1))
            e.dma_start(out[0, t * P:(t + 1) * P, :], h[:, t, :]).then_inc(sem("stored"), 16)
        e.wait_ge(*at("stored", 16 * NT))

    def split_slab(e, grp, s, width):
        n = 4 * grp + s
        e.wait_ge(raw_full[s % 2], 64 * grp + 32 * (s // 2 + 1))
        free = n - 3
        wait_apart(e, slab_used, free)
        r = raw[:, s % 2, 0:width]
        e.tensor_scalar(w_hi[:, s, 0:width], r, 1.0, 0.0, ALU.mult, ALU.add).then_inc(split, 1)
        e.wait_ge(split, 2 * n + 1)
        e.tensor_tensor(w_lo[:, s, 0:width], r, w_hi[:, s, 0:width].bitcast(F32), ALU.subtract).then_inc(split, 1)

    def split_cols(e, grp, s, k, n):
        m = 4 * grp + s
        e.wait_ge(raw_full[s % 2], 64 * grp + 32 * (s // 2 + 1))
        if grp > 0:
            e.wait_ge(slab_used, m - 3)

        def view(x):
            return x.rearrange("p (k c) -> p k c", c=W)[:, 0:k, 0:n]

        e.tensor_scalar(view(w_hi[:, s, :]), view(raw[:, s % 2, :]), 1.0, 0.0, ALU.mult, ALU.add).then_inc(split, 1)
        e.wait_ge(split, 2 * m + 1)
        e.tensor_tensor(view(w_lo[:, s, :]), view(raw[:, s % 2, :]), view(w_hi[:, s, :].bitcast(F32)),
                        ALU.subtract).then_inc(split, 1)

    def split_all(e, phase, first=0, widths=(SLAB,) * 4):
        with e.Fori(first, phase.groups) as gi:
            for s in range(4):
                split_slab(e, gi + phase.g0, s, widths[s])

    def split_down(e, phase):
        with e.Fori(0, 2) as c:
            for q in range(3):
                for s in range(4):
                    split_slab(e, 3 * c + (phase.g0 + q), s, W if q == 2 and s >= 2 else SLAB)

    def stage_queries(e, ph, q_src, rows, iters, ready, h0=0):
        for s, v in ready:
            e.wait_ge(s, v)

        def one_head(hd, hh):
            e.tensor_copy(q_st[0:rows, hh, :], q_src(hd)).then_inc(sem(f"{ph}_q"), 1)

        for hh in range(2):
            one_head(hh, hh)
        with e.Fori(1, iters) as j:
            for hh in range(2):
                e.wait_ge(*at(f"{ph}_qk", 8 * j + (4 * hh - 4)))
                one_head(2 * j + hh, hh)

    def heads(t, hd, off=0, m=None):
        if isinstance(hd, int):
            return t[:, hd, :]
        return t[:, bass.ds(hd, 1), :].rearrange("p a s -> p (a s)")

    @block.gpsimd
    def _(e):
        consts = sem("consts")
        e.memset(ident[:, :], 0.0).then_inc(consts, 1)
        e.memset(one[:, :], 1.0).then_inc(consts, 1)
        for m in (causal, strict, band):
            e.memset(m[:, :], 0.0).then_inc(consts, 1)
        e.memset(c_add[:, :, :], 0.0).then_inc(consts, 1)
        e.memset(c_01[:, :, :], 1.0).then_inc(consts, 1)
        e.memset(kct[:, :, :], 0.0).then_inc(consts, 1)
        e.memset(vbd[:, :, :], 0.0).then_inc(consts, 1)
        e.wait_ge(consts, 9)
        sel = lambda t, op, fill, base, pat, ch: e.affine_select(
            out=t, in_=t, compare_op=op, fill=fill, base=base, pattern=pat, channel_multiplier=ch).then_inc(consts, 1)
        sel(ident[:, :], ALU.not_equal, 1.0, 0, [[-1, P]], 1)
        sel(causal[:, :], ALU.is_ge, NEG, 0, [[-1, P]], 1)
        sel(strict[:, :], ALU.is_ge, NEG, -1, [[-1, P]], 1)
        sel(band[:, :], ALU.is_ge, NEG, -1, [[1, P]], -1)
        sel(c_add[:, :, :], ALU.is_ge, NEG, -(CMP - 1), [[P, NT], [-CMPS, CMP]], 1)
        sel(c_01[:, :, :], ALU.is_ge, 0.0, -(CMP - 1), [[P, NT], [-CMPS, CMP]], 1)
        e.wait_ge(consts, 10)
        e.tensor_copy(ident_b[:, :], ident[:, :]).then_inc(consts, 1)
        ph = phases
        for i, (c0, n) in enumerate(IN1):
            for s in range(4):
                split_cols(e, ph["in1"].g0 + i, s, 2, n)
        split_all(e, ph["cmp"])
        stage_queries(e, "nsa", lambda hd: heads(qt1, hd if isinstance(hd, int) else hd % 8), HD, 8,
                      [at("in1_tpa", 13), at("in1_tpd", 13), at("cat_fin", NT)])
        stage_queries(e, "swa", lambda hd: heads(qt1, hd + 8), HD, 4, [at("nsa_ofree", 66)])
        split_all(e, ph["out1"])
        split_all(e, ph["up1"])
        split_down(e, ph["down1"])
        for i, (c0, n) in enumerate(IN2):
            for s in range(4):
                split_cols(e, ph["in2"].g0 + i, s, 2, n)
        for s, (k, n) in enumerate(((2, 384), (2, 384), (1, W), (1, W))):
            split_cols(e, ph["mla"].g0, s, k, n)
        stage_queries(e, "att2", lambda hd: heads(qm, hd), MQK, 4,
                      [at("mla_tpa", 8), at("mla_tpd", 8)])
        stage_queries(e, "stk", lambda hd: heads(qs, hd), HD, 4, [at("att2_ofree", 34)])
        split_all(e, ph["out2"])
        split_all(e, ph["up2"])
        split_down(e, ph["down2"])
        for s in range(4):
            split_cols(e, ph["in3"].g0, s, 2, 16)
        e.memset(tri[:, :], 1.0).then_inc(consts, 1)
        e.memset(ones[:, :], 1.0).then_inc(consts, 1)
        e.wait_ge(consts, 18)
        sel(tri[:, :], ALU.is_ge, 0.0, 0, [[1, P]], -1)
        split_all(e, ph["in3"], 1)
        stage_queries(e, "fox", lambda hd: heads(qf, hd), HD + 2, 8,
                      [at("in3_tpa", 16), at("in3_tpd", 16), (slab_used, 4 * (ph["in3"].g0 + 7))])
        split_all(e, ph["out3"])
        split_all(e, ph["up3"])
        split_down(e, ph["down3"])

    def dst_of(t, i):
        return lambda: t[:, i, :]

    def alternate(items):
        return [(off, w, dst, "ad"[i % 2]) for i, (off, w, dst) in enumerate(items)]

    T_IN1 = [
        alternate([(64 * i, HD, qt1[:, i, :]) for i in range(8)]),
        alternate([(0, HD, kt1[:, 0, :]), (64, HD, kt1[:, 1, :]), (128, HD, vct[:, 0, :]), (192, HD, vct[:, 1, :]),
                   (256, HD, kt1[:, 2, :]), (320, HD, kt1[:, 3, :])]),
        alternate([(64 * i, HD, kt1[:, 4 + i, :]) for i in range(2)]),
        alternate([(64 * i, HD, qt1[:, 8 + i, :]) for i in range(8)]),
        alternate([(64 * i, HD, kt1[:, 6 + i, :]) for i in range(2)]),
    ]
    T_IN2 = [
        [(0, P, (cq_hi[:, 0, :], cq_lo[:, 0, :]), "s"), (P, P, (cq_hi[:, 1, :], cq_lo[:, 1, :]), "s"),
         (QR, P, (ckv_hi[:, :], ckv_lo[:, :]), "s")],
        alternate([(64 * i, HD, qs[:, i, :]) for i in range(8)]),
        alternate([(64 * i, HD, ksb[:, i, :]) for i in range(8)]),
        [],
    ]
    T_MLA = [alternate([(MQK * i, MQK, (qm, km)[c // 2][:, 4 * (c % 2) + i, :]) for i in range(4)]) for c in range(4)]
    T_IN3 = [[]] + [alternate([(66 * i, 66, (qf, kf)[c // 2][:, 8 * (c % 2) + i, :]) for i in range(8)])
                    for c in range(4)] + [[], []]

    def t_plan(t_lists):
        plan, n = [], {"a": 0, "d": 0}
        for c, units in enumerate(t_lists):
            for un in units:
                k = "a" if un[3] == "a" else "d"
                n[k] += 1
                plan.append((c, un, k, n[k]))
        return plan

    def emptied(e, name, plan, i):
        _, _, k, count = plan[i]
        e.wait_ge(*at(f"{name}_tp{k}", count))

    def mm3(e, o, s_hi, s_lo, m_hi, m_lo, start, stop):
        e.matmul(o, s_hi, m_hi, start=start, stop=False)
        e.matmul(o, s_hi, m_lo, start=False, stop=False)
        return e.matmul(o, s_lo, m_hi, start=False, stop=stop)

    def pe_turn(e, name, plan, c, tok_waits):
        if any(p[0] == c for p in plan):
            for s, v in tok_waits:
                e.wait_ge(s, v)
        for i, (cc, (off, w, _, _), _, _) in enumerate(plan):
            if cc != c:
                continue
            if i >= 4:
                emptied(e, name, plan, i - 4)
            for t in range(NT):
                m = e.transpose(bank(4 + i % 4, P, t * P, w), tok3[:, t, off:off + w], ident[:, :])
            m.then_inc(sem(f"{name}_tp"), 1)

    def pe_project(e, name, chunks, plan, x_of, kts, tok_waits, xt_wait=None):
        g0 = phases[name].g0
        for c, n in enumerate(chunks):
            for s in range(4):
                e.wait_ge(split, 2 * (4 * (g0 + c) + s + 1))
                for t in range(NT):
                    if c == 0 and s == 0 and xt_wait:
                        e.wait_ge(*at(xt_wait, 2 * t + 2))
                    if c > 0 and s == 0:
                        e.wait_ge(*at(f"{name}_copy", 4 * c - 3 + t))
                    for k in range(2):
                        hi, lo = x_of(2 * s + k, t)
                        m = mm3(e, bank(t, n), hi, lo, w_hi[:, s, k * W:k * W + n], w_lo[:, s, k * W:k * W + n],
                                s == 0 and k == 0, s == 3 and k == 1)
                    if s == 3 and t < 3:
                        m.then_inc(sem(f"{name}_acc"), 1)
                m.then_inc(slab_used, 1)
                if s == 2 and c > 0:
                    pe_turn(e, name, plan, c - 1, tok_waits(c - 1))
        pe_turn(e, name, plan, len(chunks) - 1, tok_waits(len(chunks) - 1))

    def x_model(k, t):
        return xt_hi[:, k, t * P:(t + 1) * P], xt_lo[:, k, t * P:(t + 1) * P]

    def x_hidden(k, t):
        return hid_hi[:, k, t * P:(t + 1) * P], hid_lo[:, k, t * P:(t + 1) * P]

    def tile_done(e, name, c, t, slabs_end):
        if t == 3:
            e.wait_ge(slab_used, slabs_end)
        else:
            e.wait_ge(*at(f"{name}_acc", 3 * c + t + 1))

    def turn_bank(name, i):
        return (0 if name in ("n3", "n6", "n8") else 4) + i % 4

    def pe_to_xt(e, name, src, ready):
        for t in range(NT):
            e.wait_ge(*ready(t))
            for q in range(2):
                i = 2 * t + q
                if i >= 4:
                    e.wait_ge(*at(f"{name}_lo", i - 3))
                for k in range(4):
                    m = e.transpose(bank(turn_bank(name, i), P, k * P), src(t)[:, (4 * q + k) * P:(4 * q + k + 1) * P],
                                    ident[:, :])
                m.then_inc(sem(f"{name}_tp"), 1)

    def pe_out(e, name, x_of, kts, xt_wait, hid=None):
        phase = phases[name]
        per = phase.groups // 2
        last_k = kts[-1][-1]
        if hid:
            e.wait_ge(*at(f"{hid}_h", 20))
        with e.Fori(0, 2) as c:
            for s, kt in enumerate(kts):
                n = 4 * per * c + (4 * phase.g0 + s)
                e.wait_ge(split, 2 * n + 2)
                if hid:
                    e.wait_ge(*at(f"{hid}_lo", 2 * (kt[-1] // 2) + 2))
                for t in range(NT):
                    if xt_wait and s == 0:
                        e.wait_ge(*at(xt_wait, 2 * t + 2))
                    o = ps[:, bass.ds(c * (4 * W) + t * W, W)]
                    for i, k in enumerate(kt):
                        hi, lo = x_of(k, t)
                        m = mm3(e, o, hi, lo, w_hi[:, s % 4, i * W:(i + 1) * W], w_lo[:, s % 4, i * W:(i + 1) * W],
                                k == 0, k == last_k)
                    if s == len(kts) - 1 and t < 3:
                        m.then_inc(sem(f"{name}_acc"), 1)
                m.then_inc(slab_used, 1)

    OUT_KTS = [(2 * s, 2 * s + 1) for s in range(4)]
    DOWN_KTS = [(2 * s, 2 * s + 1) for s in range(10)] + [(20,), (21,)]

    def pe_up(e, name, xt):
        g0 = phases[name].g0

        def chunk(gi, even):
            for s in range(4):
                e.wait_ge(split, 8 * (gi + g0) + (2 * s + 2))
                for j in range(4):
                    if s == 0 and not (isinstance(gi, int) and gi == 0) and j == 0:
                        e.wait_ge(*at(f"{name}_h", 2 * (gi - 1)))
                    for k in range(2):
                        kt = 2 * s + k
                        m = mm3(e, bank(4 * even + j), w_hi[:, s, k * W + j * P:k * W + (j + 1) * P],
                                w_lo[:, s, k * W + j * P:k * W + (j + 1) * P], xt_hi[:, kt, :], xt_lo[:, kt, :],
                                kt == 0, kt == KD - 1)
                    if s == 3 and j < 3:
                        m.then_inc(sem(f"{name}_acc"), 1)
                m.then_inc(slab_used, 1)

        e.wait_ge(*at(f"{xt}_lo", 8))
        chunk(0, 1)
        with e.Fori(0, 5) as j:
            chunk(2 * j + 1, 0)
            chunk(2 * j + 2, 1)

    def columns(ap3, hd):
        return lambda kt: (ap3[:, kt, hd * HD:(hd + 1) * HD] if isinstance(hd, int)
                           else ap3[:, kt, bass.ds(hd * HD, HD)])

    def span(cfg, i):
        return (max(0, i - 1) if cfg["band"] else 0), i + 1

    def pe_attend(e, cfg):
        name, iters, look = cfg["name"], cfg["iters"], cfg["look"]

        def scores(j, k):
            hh, i = k // 4, 3 - k % 4
            k0, k1 = span(cfg, i)
            n = (k1 - k0) * P
            if k % 4 == 0:
                e.wait_ge(*at(f"{name}_q", 2 * j + (hh + 1)))
            o = bank(k % 4, n)
            e.matmul(o, q_st[0:cfg["dh"], hh, i * P:(i + 1) * P], cfg["k"](2 * j + hh)[:, k0 * P:k1 * P],
                     start=True, stop=False)
            last = k1 - k0 - 1
            if cfg["band"] and i > 0:
                e.matmul(bank(k % 4, P), ident_b[:, :], band[:, :], start=False, stop=False)
            e.matmul(bank(k % 4, P, last * P), ident_b[:, :], cfg["mask"][:, :], start=False, stop=True).then_inc(
                sem(f"{name}_qk"), 1)

        def turn_probs(j, k):
            k0, k1 = span(cfg, 3 - k % 4)
            e.wait_ge(*at(f"{name}_p", 8 * j + (k + 1)))
            for x in range(k1 - k0):
                m = e.transpose(bank(4 + k % 2, P, x * P), prob[:, k % 4, x * P:(x + 1) * P], ident[:, :])
            m.then_inc(sem(f"{name}_tp"), 1)

        def values(j, k):
            k0, k1 = span(cfg, 3 - k % 4)
            v = cfg["v"](2 * j + k // 4)
            e.wait_ge(*at(f"{name}_pt", 8 * j + (k + 1)))
            e.wait_ge(*at(f"{name}_ofree", 8 * j + (k + 1)))
            for x in range(k1 - k0):
                m = e.matmul(bank(6 + k % 2, HD), prob_t[:, k % 2, x * P:(x + 1) * P], v(k0 + x),
                             start=x == 0, stop=x == k1 - k0 - 1)
            m.then_inc(sem(f"{name}_pv"), 1)

        for s, v in cfg["start"]:
            e.wait_ge(s, v)
        if name == "stk":
            e.sem_inc(sem("stk_pv"), 2)
        for k in range(look):
            scores(0, k)

        def body(j, last):
            for k in range(8):
                if k + look < 8:
                    scores(j, k + look)
                elif not last:
                    scores(j + 1, k + look - 8)
                turn_probs(j, k)
                if k > 0:
                    values(j, k - 1)
            values(j, 7)

        with e.Fori(0, iters - 1) as j:
            body(j, False)
        body(iters - 1, True)

    att = {
        "nsa": dict(name="nsa", iters=8, look=2, dh=HD, band=False, mask=causal,
                    k=lambda hd: heads(kt1, hd // 4 + 2), v=lambda hd: columns(v1, hd // 4),
                    start=[at("cat_fin", NT), at("in1_tpa", 13), at("in1_tpd", 13), at("in1_copy", 20)]),
        "swa": dict(name="swa", iters=4, look=2, dh=HD, band=True, mask=causal,
                    k=lambda hd: heads(kt1, hd // 4 + 6), v=lambda hd: columns(v1, hd // 4 + 4),
                    start=[at("nsa_ofree", 66)]),
        "att2": dict(name="att2", iters=4, look=2, dh=MQK, band=False, mask=causal,
                     k=lambda hd: heads(km, hd), v=lambda hd: columns(v2, hd),
                     start=[at("mla_tpa", 8), at("mla_tpd", 8), at("mla_copy", 16)]),
        "stk": dict(name="stk", iters=4, look=3, dh=HD, band=False, mask=strict,
                    k=lambda hd: heads(ksb, hd), v=lambda hd: columns(v2, hd + 8),
                    start=[at("att2_ofree", 34)]),
        "fox": dict(name="fox", iters=8, look=2, dh=HD + 2, band=False, mask=causal,
                    k=lambda hd: heads(kf, hd), v=lambda hd: columns(v3, hd),
                    start=[at("in3_tpa", 16), at("in3_tpd", 16), at("in3_copy", 28)]),
    }

    @block.tensor
    def _(e):
        e.wait_ge(*at("consts", 16))
        e.wait_ge(*at("small_full", 16 * SMALLS))
        for w in range(4):
            e.transpose(bank(7, 2 * KF, w * 2 * KF), c_raw[:, w, :], ident[0:2 * KF, 0:2 * KF])
        for kv in range(2):
            for par in range(2):
                m = e.transpose(bank(6, CMPS, (2 * kv + par) * CMPS, HD), pe_raw[:, kv, par * HD:(par + 1) * HD],
                                ident[0:CMPS, 0:CMPS])
        m.then_inc(sem("pre_tp"), 1)
        e.wait_ge(*at("pre_out", 1))

        xn_ready = lambda name: lambda t: at(f"{name}_xn", t + 1)
        xn_of = lambda t: xn[:, t % 2, :]
        pe_to_xt(e, "n0", xn_of, xn_ready("n0"))
        tokd = {0: 4, 1: 8, 2: 12, 3: 16, 4: 20}
        pe_project(e, "in1", [n for _, n in IN1], t_plan(T_IN1), x_model, KD,
                   lambda c: [at("in1_copy", 4 * c + 4), at("in1_tok", tokd[c])], "n0_lo")
        e.wait_ge(*at("in1_copy", 20))
        e.wait_ge(*at("in1_tpa", 13))
        e.wait_ge(*at("in1_tpd", 13))
        g0 = phases["cmp"].g0
        for kv in range(2):
            for s in range(4):
                e.wait_ge(split, 2 * (4 * (g0 + kv) + s + 1))
                if s == 0:
                    e.wait_ge(*at("cmp_f", kv + 1))
                for k in range(4):
                    pp = 4 * s + k
                    m = mm3(e, bank(kv, 256, 0, 62), f_hi[:, kv, pp, :], f_lo[:, kv, pp, :],
                            w_hi[:, s, k * 256:(k + 1) * 256], w_lo[:, s, k * 256:(k + 1) * 256],
                            pp == 0, pp == CMPS - 1)
                m.then_inc(slab_used, 1)
        for kv in range(2):
            e.wait_ge(*at("cmp_gelu", kv + 1))
            for x in range(2):
                m = e.transpose(bank(2, 62, (2 * kv + x) * 62), chid[0:62, kv, x * P:(x + 1) * P],
                                ident[0:62, 0:62])
            m.then_inc(sem("cmp_tp"), 1)
        e.wait_ge(*at("cmp_ht", 1))
        for x in range(2):
            m = e.matmul(bank(3, 62, 0, HD), w2_sb[:, 0, x, :], chid_t[:, 0, x, :], start=x == 0, stop=x == 1)
        m.then_inc(sem("cmp_kv"), 1)
        for hd in range(2):
            for x in range(2):
                m = e.matmul(bank(hd, HD, 0, NCB), chid_t[:, 1, x, hd * NCB:(hd + 1) * NCB], w2_sb[:, 1, x, :],
                             start=x == 0, stop=x == 1)
        m.then_inc(sem("cmp_kv"), 1)
        e.wait_ge(*at("cmp_out", 1))
        for i in range(NT):
            for hd in range(8):
                m = e.matmul(bank(4, CMP, hd * CMP), qt1[:, hd, i * P:(i + 1) * P], kct[:, hd // 4, :],
                             start=True, stop=True)
            m.then_inc(sem("cat_s"), 1)
            e.wait_ge(*at("cat_p", i + 1))
            for x in range(2):
                m = e.transpose(bank(5, P, x * P), scratch[:, 0, x * P:(x + 1) * P], ident[:, :])
            m.then_inc(sem("cat_tp"), 1)
            e.wait_ge(*at("cat_pt", i + 1))
            for x in range(2):
                m = e.matmul(bank(6, 4 * HD, x * 4 * HD), scratch[:, 1, x * P:(x + 1) * P], vbd[:, x, :],
                             start=True, stop=True)
            m.then_inc(sem("cat_o"), 1)
        pe_attend(e, att["nsa"])
        pe_attend(e, att["swa"])
        pe_to_xt(e, "n1", xn_of, xn_ready("n1"))
        pe_out(e, "out1", x_model, OUT_KTS, "n1_lo")
        pe_to_xt(e, "n3", xn_of, xn_ready("n3"))
        pe_up(e, "up1", "n3")
        pe_out(e, "down1", x_hidden, DOWN_KTS, None, "up1")

        pe_to_xt(e, "n5", xn_of, xn_ready("n5"))
        pe_project(e, "in2", [n for _, n in IN2], t_plan(T_IN2), x_model, KD,
                   lambda c: [at("in2_copy", 4 * c + 4)] + [at("in2_tok", 4)] * (c == 0), "n5_lo")
        plan = t_plan(T_MLA)
        for i in (-1, -2, -3, -4):
            emptied(e, "in2", t_plan(T_IN2), i)
        gm = phases["mla"].g0
        for c in range(4):
            e.wait_ge(split, 2 * (4 * gm + c + 1))
            n = 384 if c < 2 else W
            for t in range(NT):
                if c > 0:
                    e.wait_ge(*at("mla_copy", 4 * c - 3 + t))
                elif t == 0:
                    e.wait_ge(*at("in2_copy", 16))
                    emptied(e, "in2", t_plan(T_IN2), 2)
                T = slice(t * P, (t + 1) * P)
                if c < 2:
                    for x in range(2):
                        m = mm3(e, bank(t, n), cq_hi[:, x, T], cq_lo[:, x, T], w_hi[:, c, x * W:x * W + n],
                                w_lo[:, c, x * W:x * W + n], x == 0, x == 1)
                else:
                    m = mm3(e, bank(t, n), ckv_hi[:, T], ckv_lo[:, T], w_hi[:, c, 0:n], w_lo[:, c, 0:n], True, True)
                if t < 3:
                    m.then_inc(sem("mla_acc"), 1)
            m.then_inc(slab_used, 1)
            if c > 0:
                pe_turn(e, "mla", plan, c - 1, [at("mla_tok", 4 * c)])
        pe_turn(e, "mla", plan, 3, [at("mla_tok", 16)])
        pe_attend(e, att["att2"])
        pe_attend(e, att["stk"])
        pe_to_xt(e, "x2", lambda t: v2[:, t, :], lambda t: at("stk_ofree", 34))
        pe_out(e, "out2", x_model, OUT_KTS, "x2_lo")
        pe_to_xt(e, "n6", xn_of, xn_ready("n6"))
        pe_up(e, "up2", "n6")
        pe_out(e, "down2", x_hidden, DOWN_KTS, None, "up2")

        pe_to_xt(e, "n7", xn_of, xn_ready("n7"))
        g3 = phases["in3"].g0
        plan = t_plan(T_IN3)

        def decays():
            e.wait_ge(*at("consts", 19))
            e.wait_ge(*at("fox_logf", 1))
            for t in range(NT):
                for x in range(t + 1):
                    m = e.matmul(bank(7, 16, t * 16), (tri if x == t else ones)[:, :], logf[:, x, :],
                                 start=x == 0, stop=x == t)
            m.then_inc(sem("fox_decay"), 1)
            e.wait_ge(*at("fox_dec_out", 1))

        def tok3_waits(c):
            if c == 0:
                decays()
                return []
            return [at("in3_copy", 4 * c + 4), at("in3_tok", 4 * c)]

        T_IN3[0] = []
        pe_project(e, "in3", [16] + [W] * 6, plan, x_model, KD, tok3_waits, "n7_lo")
        pe_attend(e, att["fox"])
        pe_to_xt(e, "x3", lambda t: v3[:, t, :], lambda t: at("fox_ofree", 66))
        pe_out(e, "out3", x_model, OUT_KTS, "x3_lo")
        pe_to_xt(e, "n8", xn_of, xn_ready("n8"))
        pe_up(e, "up3", "n8")
        pe_out(e, "down3", x_hidden, DOWN_KTS, None, "up3")


    def small_loads(e):
        full = sem("small_full")
        ld = lambda dst, src: e.dma_start(dst, src).then_inc(full, 16)
        ld(c_raw[:, 0:3, :], A["conv_w"][0].rearrange("w (t p) -> t w p", p=P))
        ld(c_raw[:, 3, :], A["conv_b"][0].rearrange("(t p) -> t p", p=P))
        ld(pe_raw[:, :, :], A["cmp_pos"][0].rearrange("k (s r) d -> s k (r d)", r=2))
        ld(rope_c[:, :, :], A["rope_cos"].rearrange("(t p) d -> p t d", p=P))
        ld(rope_s[:, :, :], A["rope_sin"].rearrange("(t p) d -> p t d", p=P))
        with nc.allow_non_contiguous_dma(reason="512 positions"):
            ld(pos_i[:, :], A["positions_2"][0].rearrange("(t p) -> p t", p=P))
        for dst, src in ((inv_f, A["inv_freq"]), (sink, A["swa_sinks"][0]), (g_qa, A["l0_mla_q_a_norm_2"]),
                         (g_kva, A["l0_mla_kv_a_norm_2"]), (g_mq, A["l0_mla_q_norm_2"]),
                         (g_mk, A["l0_mla_k_norm_2"]), (g_fq, A["l1_fox_q_norm_2"]), (g_fk, A["l1_fox_k_norm_2"]),
                         (f_bias, A["l1_fox_f_bias_2"])):
            ld(dst[:, :], src.partition_broadcast(P))
        ld(w2_sb[:, :, :, :].rearrange("p k x d -> p (k x) d"),
           A["cmp_w2"][0].rearrange("k (x p) d -> p (k x) d", p=P))

    def act_rstd(e, od, name, k, n):
        e.wait_ge(*at(f"{name}_var", k))
        e.activation(sq_a[:, 0:n], var[:, 0:n], ACT.Ln).then_inc(*od.own())
        e.wait_ge(*od.latest())
        e.activation(rstd[:, 0:n], sq_a[:, 0:n], ACT.Exp, scale=-0.5).then_inc(*od.done(*at(f"{name}_y", k)))

    def act_norm(e, od, name, src, parts, ready):
        width = D // parts
        for t in range(2):
            e.wait_ge(*ready(t))
            for x in range(parts):
                if od.newest:
                    e.wait_ge(*od.latest())
                e.activation(scratch[:, :, :].rearrange("p a b -> p (a b)")[:, 0:width],
                             src(t)[:, x * width:(x + 1) * width], ACT.Square,
                             accum_out=ss[:, t * parts + x:t * parts + x + 1]).then_inc(
                    *od.done(*at(f"{name}_sq", t * parts + x + 1)))
        act_rstd(e, od, name, 1, NT * parts)

    def act_to_xt(e, od, name):
        for i in range(8):
            t, q = i // 2, i % 2
            e.wait_ge(*at(f"{name}_tp", i + 1))
            e.activation(xt_hi[:, 4 * q:4 * q + 4, t * P:(t + 1) * P],
                         bank(turn_bank(name, i)).rearrange("p (k s) -> p k s", k=4), ACT.Copy).then_inc(
                *od.done(*at(f"{name}_hi", i + 1)))

    def out_tile(name, t):
        banks = ps[:, :].rearrange("p (b n) -> p b n", n=W)
        return banks[:, t::4, :]

    def out_done(e, name, t):
        phase = phases[name]
        tile_done(e, name, 1, t, 4 * (phase.g0 + phase.groups))

    def act_post(e, od, name):
        for t in range(NT):
            out_done(e, name, t)
            e.wait_ge(*od.latest())
            e.activation(scratch[:, :, :], out_tile(name, t), ACT.Square, accum_out=ss[:, t:t + 1]).then_inc(
                *od.done(*at(f"{name}_sq", t + 1)))
        act_rstd(e, od, name, 1, NT)

    def act_turned(e, od, name, plan, c):
        for i, (cc, (off, w, dst, kind), _, count) in enumerate(plan):
            if cc != c or kind == "d":
                continue
            e.wait_ge(*at(f"{name}_tp", i + 1))
            if kind == "s":
                e.activation(dst[0], bank(4 + i % 4), ACT.Copy).then_inc(*od.done(*at(f"{name}_tph", i + 1)))
            else:
                e.activation(dst, bank(4 + i % 4, W, 0, w), ACT.Copy).then_inc(*od.done(*at(f"{name}_tpa", count)))

    def act_copies(e, od, name, c, ends, copy, plan, uses_tok):
        for t in range(NT):
            tile_done(e, name, c, t, ends)
            if t == 0 and uses_tok:
                before = sum(p[0] < c for p in plan)
                if before:
                    e.wait_ge(*at(f"{name}_tp", before))
            copy(t)

    def act_up(e, od, name, conv_layer):
        g0 = phases[name].g0

        def chunk(gi, even):
            first = isinstance(gi, int) and gi == 0
            for j in range(4):
                if j == 3:
                    e.wait_ge(slab_used, 4 * (gi + g0) + 4)
                elif conv_layer or j < 2:
                    e.wait_ge(*at(f"{name}_acc", 3 * gi + (j + 1)))
                if conv_layer:
                    tile = 2 * gi + (j % 2 + (j // 2) * KF)
                    tap = (lambda w: conv[:, w, tile:tile + 1]) if isinstance(gi, int) else \
                        (lambda w: conv[:, w, bass.ds(tile, 1)])
                    scale, bias = tap(2), tap(3)
                    if not first:
                        wait_apart(e, *at(f"{name}_lo", 2 * gi + (j % 2 - 1)))
                    e.activation(half_u[:, 2 * (j % 2) + j // 2, :], bank(4 * even + j), ACT.Identity,
                                 scale=scale, bias=bias).then_inc(*od.done(*at(f"{name}_s", 4 * gi + (j + 1))))
                elif j < 2:
                    e.activation(half_u[:, 2 * j, :], bank(4 * even + j), ACT.Silu).then_inc(
                        *od.done(*at(f"{name}_s", 2 * gi + (j + 1))))
            if conv_layer:
                for k in range(2):
                    e.wait_ge(*at(f"{name}_c", 4 * gi + (k + 1)))
                    e.activation(half_u[:, 2 * k, :], half_u[:, 2 * k, :], ACT.Gelu_apprx_tanh).then_inc(
                        *od.done(*at(f"{name}_g", 2 * gi + (k + 1))))
            for k in range(2):
                src = half_u[:, 2 * k + (0 if conv_layer else 1), :]
                high = hid_tile(hid_hi, 2 * gi + k)
                wait_apart(e, *at(f"{name}_h", 2 * gi + (k + 1)))
                e.activation(high, src, ACT.Copy).then_inc(*od.done(*at(f"{name}_hi", 2 * gi + (k + 1))))

        e.preload_act_table(ACT.Gelu_apprx_tanh if conv_layer else ACT.Silu)
        chunk(0, 1)
        with e.Fori(0, 5) as j:
            chunk(2 * j + 1, 0)
            chunk(2 * j + 2, 1)
        e.preload_act_table_set(EXP_LN)

    def hid_tile(t, i):
        return t[:, i, :] if isinstance(i, int) else t[:, bass.ds(i, 1), :].rearrange("p a s -> p (a s)")

    def column(t, hd):
        return t[:, hd:hd + 1] if isinstance(hd, int) else t[:, bass.ds(hd, 1)]

    def steps(e, od, cfg, before, body, per):
        before()
        iters = cfg["iters"]
        with e.Fori(0, iters - 1) as j:
            od.enter(j, per)
            body(j, False)
        od.leave(iters - 1, per)
        body(iters - 1, True)

    def act_attend(e, od, cfg):
        name = cfg["name"]

        def probs(j, k):
            k0, k1 = span(cfg, 3 - k % 4)
            n = (k1 - k0) * P
            c = k % 4
            if cfg["band"]:
                its_sink = column(sink, 2 * j + k // 4)
                wait_apart(e, *at(f"{name}_nm", 8 * j + (k + 1)))
                e.activation(esink[:, c:c + 1], its_sink, ACT.Exp, bias=nmax[:, c:c + 1]).then_inc(*od.own())
            else:
                e.wait_ge(*at(f"{name}_nm", 8 * j + (k + 1)))
            e.activation(prob[:, c, 0:n], bank(c, n), ACT.Exp, bias=nmax[:, c:c + 1],
                         accum_out=den[:, c:c + 1]).then_inc(*od.done(*at(f"{name}_p", 8 * j + (k + 1))))

        def body(j, last):
            for k in range(8):
                if k < 6:
                    probs(j, k + 2)
                elif not last:
                    probs(j + 1, k - 6)

        steps(e, od, cfg, lambda: (probs(0, 0), probs(0, 1)), body, 8 if cfg["band"] else 0)

    def act_stick(e, od, cfg):
        name = cfg["name"]

        def logs(j, k):
            n = (4 - k % 4) * P
            e.wait_ge(*at(f"{name}_qk", 8 * j + (k + 1)))
            a = sb_ln[:, k % 4, 0:n]
            e.activation(a, bank(k % 4, n), ACT.Abs).then_inc(*od.own())
            e.wait_ge(*od.latest())
            e.activation(a, a, ACT.Exp, scale=-1.0).then_inc(*od.own())
            e.wait_ge(*od.latest())
            e.activation(a, a, ACT.Ln, bias=1.0).then_inc(*od.done(*at(f"{name}_ln", 8 * j + (k + 1))))

        def probs(j, k):
            n = (4 - k % 4) * P
            e.wait_ge(*at(f"{name}_w", 8 * j + (k + 1)))
            a = prob[:, k % 4, 0:n]
            e.activation(a, a, ACT.Exp).then_inc(*od.done(*at(f"{name}_p", 8 * j + (k + 1))))

        def fin(j, k):
            o = cfg["v"](2 * j + k // 4)(3 - k % 4)
            wait_apart(e, *at(f"{name}_pv", 8 * j + (k + 3)))
            e.activation(o, bank(6 + k % 2, HD), ACT.Copy).then_inc(*od.done(*at(f"{name}_ofree", 8 * j + (k + 3))))

        def body(j, last):
            for k in range(8):
                if k < 5:
                    logs(j, k + 3)
                elif not last:
                    logs(j + 1, k - 5)
                if k < 6:
                    probs(j, k + 2)
                elif not last:
                    probs(j + 1, k - 6)
                if k > 0:
                    fin(j, k - 1)
            fin(j, 7)

        def before():
            e.sem_inc(*at(f"{name}_ofree", 2))
            for k in range(3):
                logs(0, k)
            probs(0, 0)
            probs(0, 1)

        steps(e, od, cfg, before, body, 16)

    @block.scalar
    def _(e):
        od = Order(sem("act_own"))
        small_loads(e)
        e.preload_act_table_set(EXP_LN)
        act_norm(e, od, "n0", lambda t: h[:, t, :], 1, lambda t: at("h_full", 64))
        act_to_xt(e, od, "n0")
        for k in range(2):
            e.wait_ge(*at("angle", k + 1))
            halves = ((-1.0, 0), (1.0, 1)) if k == 0 else ((1.0, 0), (1.0, 1))
            dst = (m_sin, m_cos)[k]
            for sign, x in halves:
                op = e.activation(dst[:, :, 16 * x:16 * x + 16], red[:, :, :], ACT.Sin, scale=sign)
                if x:
                    op.then_inc(*od.done(*at("angle_out", k + 1)))
                else:
                    op.then_inc(*od.own())
        e.preload_act_table_set(EXP_LN)

        plan = t_plan(T_IN1)
        g0 = phases["in1"].g0

        def copy1(c):
            cp = sem("in1_copy")

            def put(t):
                last = 4 * c + t + 1
                if c in (0, 3):
                    e.activation(tok3[:, t, 0:W], bank(t), ACT.Copy, scale=0.125).then_inc(*od.done(cp, last))
                elif c == 1:
                    e.activation(tok3[:, t, 0:384], bank(t, 384), ACT.Copy).then_inc(*od.own())
                    e.activation(v1[:, t, 0:P], bank(t, P, 384), ACT.Copy).then_inc(*od.done(cp, last))
                else:
                    e.activation(tok3[:, t, 0:P], bank(t, P), ACT.Copy).then_inc(*od.own())
                    if c == 2:
                        e.activation(gate[:, t, :], bank(t, 24, 256), ACT.Exp, scale=-1.0).then_inc(*od.own())
                    v_at = P if c == 2 else 2 * P
                    e.activation(v1[:, t, v_at:v_at + P], bank(t, P, P), ACT.Copy).then_inc(*od.done(cp, last))
            return put

        for c in range(5):
            act_copies(e, od, "in1", c, 4 * (g0 + c + 1), copy1(c), plan, True)
            act_turned(e, od, "in1", plan, c)
        for kv in range(2):
            e.wait_ge(*at("cmp_raw", kv + 1))
            e.activation(f_hi[:, kv, :, :], f_raw[:, kv, :, :], ACT.Copy).then_inc(*od.done(*at("cmp_fh", kv + 1)))
        for kv in range(2):
            e.wait_ge(slab_used, 4 * (phases["cmp"].g0 + kv + 1))
            e.activation(chid[0:62, kv, :], bank(kv, 256, 0, 62), ACT.Gelu_apprx_tanh).then_inc(
                *od.done(*at("cmp_gelu", kv + 1)))
        e.preload_act_table_set(EXP_LN)
        for i in range(NT):
            e.wait_ge(*at("cat_e", i + 1))
            a = scratch[:, 0, 0:8 * CMP]
            e.activation(a, a, ACT.Exp).then_inc(*od.done(*at("cat_x", i + 1)))
        act_attend(e, od, att["nsa"])
        act_attend(e, od, att["swa"])
        act_norm(e, od, "n1", lambda t: o1[:, t, :], 2, lambda t: at("swa_ofree", 34))
        act_to_xt(e, od, "n1")
        act_post(e, od, "out1")
        act_norm(e, od, "n3", lambda t: h[:, t, :], 1, lambda t: at("out1_res", t + 1))
        act_to_xt(e, od, "n3")
        act_up(e, od, "up1", True)
        act_post(e, od, "down1")

        act_norm(e, od, "n5", lambda t: h[:, t, :], 1, lambda t: at("down1_res", t + 1))
        act_to_xt(e, od, "n5")
        plan = t_plan(T_IN2)
        g2 = phases["in2"].g0

        def copy2(c):
            cp = sem("in2_copy")

            def put(t):
                last = 4 * c + t + 1
                if c == 0:
                    e.activation(tok3[:, t, 0:384], bank(t, 384), ACT.Copy).then_inc(*od.own())
                    e.activation(k_rope[:, t, :], bank(t, ROPE, 384), ACT.Copy).then_inc(*od.own())
                    if t:
                        e.wait_ge(*od.latest())
                    e.activation(scratch[:, 0, 0:QR], bank(t, QR), ACT.Square, accum_out=ss[:, t:t + 1]).then_inc(
                        *od.own())
                    e.activation(scratch[:, 0, QR:QR + KVR], bank(t, KVR, QR), ACT.Square,
                                 accum_out=ss[:, 4 + t:5 + t]).then_inc(*od.done(cp, last))
                elif c < 3:
                    e.activation(tok3[:, t, 0:W], bank(t), ACT.Copy, scale=0.125 if c == 1 else 1.0).then_inc(
                        *od.done(cp, last))
                else:
                    e.activation(v2[:, t, W:D], bank(t), ACT.Copy).then_inc(*od.done(cp, last))
            return put

        for c in range(4):
            act_copies(e, od, "in2", c, 4 * (g2 + c + 1), copy2(c), plan, c < 3)
            if c == 0:
                act_rstd(e, od, "in2", 1, 8)
            act_turned(e, od, "in2", plan, c)
        plan = t_plan(T_MLA)
        gm = phases["mla"].g0

        def copy_m(c):
            cp = sem("mla_copy")

            def put(t):
                last = 4 * c + t + 1
                if c < 2:
                    e.activation(tok3[:, t, 0:384], bank(t, 384), ACT.Copy).then_inc(*od.done(cp, last))
                    return
                rows = tok3[:, t, 0:384].rearrange("p (h d) -> p h d", d=MQK)
                kv = bank(t).rearrange("p (h d) -> p h d", d=P)
                e.activation(rows[:, :, 0:HD], kv[:, :, 0:HD], ACT.Copy).then_inc(*od.own())
                e.activation(rows[:, :, HD:MQK], k_rope[:, t, :].unsqueeze(1).broadcast_to([P, 4, ROPE]),
                             ACT.Copy).then_inc(*od.own())
                a = (c - 2) * 4 * HD
                e.activation(v2[:, t, a:a + 4 * HD].rearrange("p (h d) -> p h d", d=HD), kv[:, :, HD:P],
                             ACT.Copy).then_inc(*od.done(cp, last))
            return put

        for c in range(4):
            act_copies(e, od, "mla", c, 4 * gm + c + 1, copy_m(c), plan, True)
            act_rstd(e, od, "mla", c + 1, 16)
            act_turned(e, od, "mla", plan, c)
        act_attend(e, od, att["att2"])
        act_stick(e, od, att["stk"])
        act_to_xt(e, od, "x2")
        act_norm(e, od, "n6", lambda t: h[:, t, :], 1, lambda t: at("out2_res", t + 1))
        act_to_xt(e, od, "n6")
        act_up(e, od, "up2", False)

        act_norm(e, od, "n7", lambda t: h[:, t, :], 1, lambda t: at("down2_res", t + 1))
        act_to_xt(e, od, "n7")
        plan = t_plan(T_IN3)
        g3 = phases["in3"].g0

        def copy3(c):
            cp = sem("in3_copy")

            def put(t):
                last = 4 * c + t + 1
                if c == 0:
                    e.activation(logf[:, t, :], bank(t, 16), ACT.Copy).then_inc(*od.done(cp, last))
                elif c < 5:
                    e.activation(tok3[:, t, :].rearrange("p (h d) -> p h d", d=66)[:, :, 0:HD],
                                 bank(t).rearrange("p (h d) -> p h d", d=HD), ACT.Copy).then_inc(*od.done(cp, last))
                else:
                    e.activation(v3[:, t, (c - 5) * W:(c - 4) * W], bank(t), ACT.Copy).then_inc(*od.done(cp, last))
            return put

        for c in range(7):
            act_copies(e, od, "in3", c, 4 * (g3 + c + 1), copy3(c), plan, 0 < c < 5)
            if c == 0:
                e.wait_ge(*at("fox_abs", 1))
                a = logf[:, :, :]
                e.activation(a, a, ACT.Exp, scale=-1.0).then_inc(*od.own())
                e.wait_ge(*od.latest())
                e.activation(a, a, ACT.Ln, bias=1.0).then_inc(*od.done(*at("fox_ln", 1)))
            elif c < 5:
                act_rstd(e, od, "in3", c, 32)
            act_turned(e, od, "in3", plan, c)
        act_attend(e, od, att["fox"])
        act_to_xt(e, od, "x3")
        act_norm(e, od, "n8", lambda t: h[:, t, :], 1, lambda t: at("out3_res", t + 1))
        act_to_xt(e, od, "n8")
        act_up(e, od, "up3", False)

    def dve_refine(e, od, name, k, n):
        e.wait_ge(*at(f"{name}_y", k))
        e.tensor_tensor(sq_a[:, 0:n], rstd[:, 0:n], rstd[:, 0:n], ALU.mult).then_inc(*od.own())
        e.wait_ge(*od.latest())
        e.scalar_tensor_tensor(out=sq_a[:, 0:n], in0=sq_a[:, 0:n], scalar=-0.5, in1=var[:, 0:n],
                               op0=ALU.mult, op1=ALU.mult).then_inc(*od.own())
        e.wait_ge(*od.latest())
        e.scalar_tensor_tensor(out=rstd[:, 0:n], in0=sq_a[:, 0:n], scalar=1.5, in1=rstd[:, 0:n],
                               op0=ALU.add, op1=ALU.mult).then_inc(*od.own())
        e.wait_ge(*od.latest())

    def dve_rstd(e, od, name, k, n, count):
        e.tensor_scalar(var[:, 0:n], ss[:, 0:n], 1.0 / count, EPS, ALU.mult, ALU.add).then_inc(
            *od.done(*at(f"{name}_var", k)))
        dve_refine(e, od, name, k, n)

    def dve_low(e, od, name, i):
        t, q = i // 2, i % 2
        e.wait_ge(*at(f"{name}_hi", i + 1))
        hi = xt_hi[:, 4 * q:4 * q + 4, t * P:(t + 1) * P].bitcast(F32)
        e.tensor_tensor(xt_lo[:, 4 * q:4 * q + 4, t * P:(t + 1) * P],
                        bank(turn_bank(name, i)).rearrange("p (k s) -> p k s", k=4), hi, ALU.subtract).then_inc(
            *od.done(*at(f"{name}_lo", i + 1)))

    def dve_norm(e, od, name, gain, src, parts, ready):
        width = D // parts
        for t in range(2, NT):
            e.wait_ge(*ready(t))
            for x in range(parts):
                if od.newest:
                    e.wait_ge(*od.latest())
                a = src(t)[:, x * width:(x + 1) * width]
                e.tensor_tensor_reduce(xn[:, 1, 0:width], a, a, 1.0, 0.0, ALU.mult, ALU.add,
                                       ss[:, t * parts + x:t * parts + x + 1]).then_inc(*od.own())
        e.wait_ge(*at(f"{name}_sq", 2 * parts))
        e.wait_ge(*od.latest())
        dve_rstd(e, od, name, 1, NT * parts, width)
        gain_ready(e, gain)

        def rows(t):
            if t >= 2:
                e.wait_ge(*at(f"{name}_tp", 2 * t - 2))
            for x in range(parts):
                cs = slice(x * width, (x + 1) * width)
                i = t * parts + x
                op = e.scalar_tensor_tensor(out=xn[:, t % 2, cs], in0=src(t)[:, cs], scalar=rstd[:, i:i + 1],
                                            in1=gains[:, gain % 2, cs], op0=ALU.mult, op1=ALU.mult)
                if x == parts - 1:
                    op.then_inc(*od.done(*at(f"{name}_xn", t + 1)))
                else:
                    op.then_inc(*od.own())

        rows(0)
        rows(1)
        for t in range(NT):
            dve_low(e, od, name, 2 * t)
            dve_low(e, od, name, 2 * t + 1)
            if t < 2:
                rows(t + 2)

    def dve_post(e, od, name, gain):
        e.wait_ge(*at(f"{name}_sq", NT))
        dve_rstd(e, od, name, 1, NT, D)
        gain_ready(e, gain)
        for t in range(NT):
            y = xn[:, t % 2, :].rearrange("p (a b) -> p a b", a=2)
            e.scalar_tensor_tensor(out=y, in0=out_tile(name, t), scalar=rstd[:, t:t + 1],
                                   in1=gains[:, gain % 2, :].rearrange("p (a b) -> p a b", a=2),
                                   op0=ALU.mult, op1=ALU.mult).then_inc(*od.own())
            e.wait_ge(*od.latest())
            e.tensor_tensor(h[:, t, :], h[:, t, :], xn[:, t % 2, :], ALU.add).then_inc(
                *od.done(*at(f"{name}_res", t + 1)))

    def dve_residual(e, od, name):
        for t in range(NT):
            out_done(e, name, t)
            a = h[:, t, :].rearrange("p (a b) -> p a b", a=2)
            e.tensor_tensor(a, out_tile(name, t), a, ALU.add).then_inc(*od.done(*at(f"{name}_res", t + 1)))

    def dve_turned(e, od, name, plan, c):
        for i, (cc, (off, w, dst, kind), _, count) in enumerate(plan):
            if cc != c or kind == "a":
                continue
            if kind == "s":
                e.wait_ge(*at(f"{name}_tph", i + 1))
                e.tensor_tensor(dst[1], bank(4 + i % 4), dst[0].bitcast(F32), ALU.subtract).then_inc(
                    *od.done(*at(f"{name}_tpd", count)))
            else:
                e.wait_ge(*at(f"{name}_tp", i + 1))
                e.tensor_copy(dst, bank(4 + i % 4, W, 0, w)).then_inc(*od.done(*at(f"{name}_tpd", count)))

    def swapped_halves(e, od, x, nh, half, cos, sin, done):
        v = x if len(x.shape) == 3 else x.rearrange("p (h d) -> p h d", h=nh)
        v4 = v.rearrange("p h (a b) -> p h a b", a=2)
        s = scratch[:, 1, 0:nh * 2 * half].rearrange("p (h d) -> p h d", h=nh)
        s4 = s.rearrange("p h (a b) -> p h a b", a=2)
        sn = sin.rearrange("p (a b) -> p a b", a=2).unsqueeze(1).broadcast_to([P, nh, 2, half])
        e.tensor_tensor(s4, v4[:, :, ::-1, :], sn, ALU.mult).then_inc(*od.own())
        e.wait_ge(*od.latest())
        e.tensor_tensor(v, v, cos.unsqueeze(1).broadcast_to([P, nh, 2 * half]), ALU.mult).then_inc(*od.own())
        e.wait_ge(*od.latest())
        e.tensor_tensor(v, v, s, ALU.add).then_inc(*done())

    def head_norms(e, od, name, c, k, nh, dh, stride, gain, after):
        def view(t):
            return tok3[:, t, 0:nh * stride].rearrange("p (h d) -> p h d", d=stride)[:, :, 0:dh]
        for t in range(NT):
            e.wait_ge(*at(f"{name}_copy", 4 * c + t + 1))
            s = scratch[:, 0, 0:nh * dh].rearrange("p (h d) -> p h d", h=nh)
            e.tensor_tensor(s, view(t), view(t), ALU.mult).then_inc(*od.own())
            e.wait_ge(*od.latest())
            e.tensor_reduce(ss[:, nh * t:nh * (t + 1)], s, AX.X, ALU.add).then_inc(*od.own())
            e.wait_ge(*od.latest())
        dve_rstd(e, od, name, k, nh * NT, dh)
        for t in range(NT):
            r = rstd[:, nh * t:nh * (t + 1)].unsqueeze(2).broadcast_to([P, nh, dh])
            e.tensor_tensor(view(t), view(t), r, ALU.mult).then_inc(*od.own())
            e.wait_ge(*od.latest())
            e.tensor_tensor(view(t), view(t), gain[:, 0:dh].unsqueeze(1).broadcast_to([P, nh, dh]), ALU.mult).then_inc(
                *od.own())
            e.wait_ge(*od.latest())
            after(t, view(t))

    def dve_up(e, od, name, conv_layer):
        g0 = phases[name].g0
        per = 4 if conv_layer else 0

        def chunk(gi, even):
            if conv_layer:
                for j in range(4):
                    tile = 2 * gi + (j % 2 + (j // 2) * KF)
                    tap = (lambda w: conv[:, w, tile:tile + 1]) if isinstance(gi, int) else \
                        (lambda w: conv[:, w, bass.ds(tile, 1)])
                    y = half_u[:, 2 * (j % 2) + j // 2, :]
                    e.wait_ge(*at(f"{name}_s", 4 * gi + (j + 1)))
                    e.scalar_tensor_tensor(out=y[:, 1:], in0=bank(4 * even + j, W - 1), scalar=tap(1),
                                           in1=y[:, 1:], op0=ALU.mult, op1=ALU.add).then_inc(*od.own())
                    e.wait_ge(*od.latest())
                    e.scalar_tensor_tensor(out=y[:, 2:], in0=bank(4 * even + j, W - 2), scalar=tap(0),
                                           in1=y[:, 2:], op0=ALU.mult, op1=ALU.add).then_inc(
                        *od.done(*at(f"{name}_c", 4 * gi + (j + 1))))
                e.wait_ge(*od.latest())
                for k in range(2):
                    e.wait_ge(*at(f"{name}_g", 2 * gi + (k + 1)))
                    e.tensor_tensor(half_u[:, 2 * k, :], half_u[:, 2 * k, :], half_u[:, 2 * k + 1, :],
                                    ALU.mult).then_inc(*od.done(*at(f"{name}_h", 2 * gi + (k + 1))))
            else:
                for k in range(2):
                    e.wait_ge(*at(f"{name}_s", 2 * gi + (k + 1)))
                    if not (isinstance(gi, int) and gi == 0):
                        e.wait_ge(*at(f"{name}_lo", 2 * gi + (k - 1)))
                    if k == 1:
                        e.wait_ge(slab_used, 4 * (gi + g0) + 4)
                    else:
                        e.wait_ge(*at(f"{name}_acc", 3 * gi + 3))
                    e.tensor_tensor(half_u[:, 2 * k + 1, :], bank(4 * even + 2 + k), half_u[:, 2 * k, :],
                                    ALU.mult).then_inc(*od.done(*at(f"{name}_h", 2 * gi + (k + 1))))
            for k in range(2):
                e.wait_ge(*at(f"{name}_hi", 2 * gi + (k + 1)))
                src = half_u[:, 2 * k + (0 if conv_layer else 1), :]
                e.tensor_tensor(hid_tile(hid_lo, 2 * gi + k), src,
                                hid_tile(hid_hi, 2 * gi + k).bitcast(F32), ALU.subtract).then_inc(
                    *od.done(*at(f"{name}_lo", 2 * gi + (k + 1))))

        chunk(0, 1)
        with e.Fori(0, 5) as j:
            od.enter(j, 2 * per)
            chunk(2 * j + 1, 0)
            chunk(2 * j + 2, 1)
        od.leave(5, 2 * per)
        od.newest = at(f"{name}_lo", 22)

    def dve_attend(e, od, cfg, fin_steps, per):
        name = cfg["name"]

        def maxima(j, k):
            k0, k1 = span(cfg, 3 - k % 4)
            c = k % 4
            e.wait_ge(*at(f"{name}_qk", 8 * j + (k + 1)))
            op = e.tensor_reduce(nmax[:, c:c + 1], bank(c, (k1 - k0) * P), AX.X, ALU.max, negate=True)
            if cfg["band"]:
                op.then_inc(*od.own())
                e.wait_ge(*od.latest())
                op = e.tensor_tensor(nmax[:, c:c + 1], nmax[:, c:c + 1], column(neg_sink, 2 * j + k // 4), ALU.min)
            op.then_inc(*od.done(*at(f"{name}_nm", 8 * j + (k + 1))))

        def body(j, last):
            for k in range(8):
                if k < 6:
                    maxima(j, k + 2)
                elif not last:
                    maxima(j + 1, k - 6)
                k0, k1 = span(cfg, 3 - k % 4)
                n = (k1 - k0) * P
                e.wait_ge(*at(f"{name}_tp", 8 * j + (k + 1)))
                e.tensor_copy(prob_t[:, k % 2, 0:n], bank(4 + k % 2, n)).then_inc(
                    *od.done(*at(f"{name}_pt", 8 * j + (k + 1))))
                if k > 0:
                    fin(j, k - 1)
            fin(j, 7)

        def fin(j, k):
            e.wait_ge(*at(f"{name}_pv", 8 * j + (k + 1)))
            c = k % 4
            r = rg[:, k % 2:k % 2 + 1]
            if cfg["band"]:
                e.tensor_tensor(r, den[:, c:c + 1], esink[:, c:c + 1], ALU.add).then_inc(*od.own())
                e.wait_ge(*od.latest())
                e.reciprocal(r, r).then_inc(*od.own())
            else:
                e.reciprocal(r, den[:, c:c + 1]).then_inc(*od.own())
            e.wait_ge(*od.latest())
            fin_steps(j, k, r, *at(f"{name}_ofree", 8 * j + (k + 3)))

        def before():
            e.sem_inc(*at(f"{name}_ofree", 2))
            maxima(0, 0)
            maxima(0, 1)

        steps(e, od, cfg, before, body, per)

    def dve_stick(e, od, cfg):
        name = cfg["name"]

        def weights(j, k):
            n = (4 - k % 4) * P
            e.wait_ge(*at(f"{name}_ln", 8 * j + (k + 1)))
            sp, r, z = sb_ln[:, k % 4, 0:n], prob[:, k % 4, 0:n], bank(k % 4, n)
            e.scalar_tensor_tensor(out=sp, in0=z, scalar=0.0, in1=sp, op0=ALU.max, op1=ALU.add).then_inc(*od.own())
            e.wait_ge(*od.latest())
            e.tensor_tensor_scan(r[:, ::-1], one[:, 0:1].broadcast_to([P, n]), sp[:, ::-1], 0.0,
                                 ALU.mult, ALU.add).then_inc(*od.own())
            e.wait_ge(*od.latest())
            e.tensor_tensor(r, z, r, ALU.subtract).then_inc(*od.done(*at(f"{name}_w", 8 * j + (k + 1))))

        def body(j, last):
            for k in range(8):
                if k < 6:
                    weights(j, k + 2)
                elif not last:
                    weights(j + 1, k - 6)
                n = (4 - k % 4) * P
                e.wait_ge(*at(f"{name}_tp", 8 * j + (k + 1)))
                e.wait_ge(*at(f"{name}_pv", 8 * j + (k + 1)))
                e.tensor_copy(prob_t[:, k % 2, 0:n], bank(4 + k % 2, n)).then_inc(
                    *od.done(*at(f"{name}_pt", 8 * j + (k + 1))))

        steps(e, od, cfg, lambda: (weights(0, 0), weights(0, 1)), body, 16)

    @block.vector
    def _(e):
        od = Order(sem("dve_own"))
        e.sem_inc(sem("up1_h"), 2)
        e.wait_ge(*at("small_full", 16 * SMALLS))
        e.wait_ge(*at("consts", 16))
        e.wait_ge(*at("pre_tp", 1))
        e.tensor_copy(conv[:, :, :].rearrange("p a b -> p (a b)"), bank(7, 8 * KF)).then_inc(*od.own())
        e.tensor_copy(pe_t[:, :, :, :].rearrange("p a b c -> p (a b c)"), bank(6, 4 * CMPS, 0, HD)).then_inc(
            *od.done(*at("pre_out", 1)))
        dve_norm(e, od, "n0", 0, lambda t: h[:, t, :], 1, lambda t: at("h_full", 64))
        e.tensor_scalar(neg_sink[:, :], sink[:, :], -1.0, None, ALU.mult).then_inc(*od.own())
        e.tensor_scalar(g_fq[:, :], g_fq[:, :], 0.125, None, ALU.mult).then_inc(*od.own())
        e.tensor_scalar(g_mq[:, :], g_mq[:, :], MQK ** -0.5, None, ALU.mult).then_inc(*od.own())
        e.tensor_copy(pos_f[:, :], pos_i[:, :]).then_inc(*od.own())
        e.wait_ge(*od.latest())
        for t in range(NT):
            e.tensor_scalar(ang[:, t, :], inv_f[:, :], pos_f[:, t:t + 1], None, ALU.mult).then_inc(*od.own())
        e.wait_ge(*od.latest())
        for k in range(2):
            e.tensor_scalar(turn[:, :, :], ang[:, :, :], 0.15915494309189535, 0.25 * k, ALU.mult, ALU.add).then_inc(
                *od.own())
            e.wait_ge(*od.latest())
            e.tensor_copy(turn_i[:, :, :], turn[:, :, :]).then_inc(*od.own())
            e.wait_ge(*od.latest())
            e.tensor_copy(turn[:, :, :], turn_i[:, :, :]).then_inc(*od.own())
            e.wait_ge(*od.latest())
            if k:
                e.wait_ge(*at("angle_out", 1))
            for part, src in ((TWO_PI_HI, ang), (TWO_PI_MID, red), (TWO_PI_LO, red)):
                e.scalar_tensor_tensor(out=red[:, :, :], in0=turn[:, :, :], scalar=-part, in1=src[:, :, :],
                                       op0=ALU.mult, op1=ALU.add).then_inc(*od.own())
                e.wait_ge(*od.latest())
            if k:
                e.tensor_scalar(red[:, :, :], red[:, :, :], 1.5707963267948966, None, ALU.add).then_inc(*od.own())
                e.wait_ge(*od.latest())
            e.tensor_scalar(red[:, :, :], red[:, :, :], PI, -PI, ALU.min, ALU.max).then_inc(
                *od.done(*at("angle", k + 1)))
        e.wait_ge(*at("angle_out", 2))

        plan = t_plan(T_IN1)
        for c in range(5):
            for t in range(NT):
                e.wait_ge(*at("in1_copy", 4 * c + t + 1))
                pieces = {0: [(0, 8)], 1: [(0, 2), (256, 2)], 2: [(0, 2)], 3: [(0, 8)], 4: [(0, 2)]}[c]
                for x, (off, nh) in enumerate(pieces):
                    if x or t:
                        e.wait_ge(*od.latest())
                    done = (lambda: od.done(*at("in1_tok", 4 * c + t + 1))) if x == len(pieces) - 1 else od.own
                    swapped_halves(e, od, tok3[:, t, off:off + nh * HD], nh, HD // 2, rope_c[:, t, :],
                                   rope_s[:, t, :], done)
            if c == 2:
                e.tensor_scalar(gate[:, :, :], gate[:, :, :], 1.0, None, ALU.add).then_inc(*od.own())
                e.wait_ge(*od.latest())
                e.reciprocal(gate[:, :, :], gate[:, :, :]).then_inc(*od.own())
            dve_turned(e, od, "in1", plan, c)

        e.wait_ge(*at("in1_tpa", 13))
        e.wait_ge(*at("in1_tpd", 13))
        for kv in range(2):
            for hd in range(2):
                src = (vct[:, hd, :] if kv else kt1[:, hd, :]).rearrange("d (c s) -> d c s", s=CMPS)
                for par in range(2):
                    for hf in range(2):
                        op = e.tensor_tensor(
                            f_raw[par * HD:(par + 1) * HD, kv, 8 * hf:8 * hf + 8, hd * NCB:(hd + 1) * NCB],
                            src[:, hf:hf + NCB, par::2].rearrange("d c s -> d s c"),
                            pe_t[:, kv, par, 8 * hf:8 * hf + 8].unsqueeze(2).broadcast_to([HD, 8, NCB]), ALU.add)
                        if hd and par and hf:
                            op.then_inc(*od.done(*at("cmp_raw", kv + 1)))
                        else:
                            op.then_inc(*od.own())
        for kv in range(2):
            e.wait_ge(*at("cmp_fh", kv + 1))
            e.tensor_tensor(f_lo[:, kv, :, :], f_raw[:, kv, :, :], f_hi[:, kv, :, :].bitcast(F32),
                            ALU.subtract).then_inc(*od.done(*at("cmp_f", kv + 1)))
        e.wait_ge(*at("cmp_tp", 2))
        e.tensor_copy(chid_t[:, :, :, :].rearrange("p a b c -> p (a b c)"), bank(2, 4 * 62)).then_inc(
            *od.done(*at("cmp_ht", 1)))
        e.wait_ge(*at("cmp_kv", 2))
        e.tensor_copy(kct[:, :, 0:NCB], bank(3, 62, 0, HD).rearrange("p (h c) -> p h c", h=2)).then_inc(*od.own())
        for gq in range(2):
            for x in range(4):
                op = e.tensor_copy(vbd[32 * x:32 * x + NCB, gq, HD * x:HD * (x + 1)], bank(gq, HD, 0, NCB))
                if gq and x == 3:
                    op.then_inc(*od.done(*at("cmp_out", 1)))
                else:
                    op.then_inc(*od.own())
        for i in range(NT):
            a = scratch[:, 0, 0:8 * CMP].rearrange("p (h c) -> p h c", h=8)
            e.wait_ge(*at("cat_s", i + 1))
            e.wait_ge(*od.latest())
            e.tensor_tensor(a, bank(4, 8 * CMP).rearrange("p (h c) -> p h c", h=8),
                            c_add[:, i, :].unsqueeze(1).broadcast_to([P, 8, CMP]), ALU.add).then_inc(*od.own())
            e.wait_ge(*od.latest())
            e.tensor_reduce(ss[:, 0:8], a, AX.X, ALU.max).then_inc(*od.own())
            e.wait_ge(*od.latest())
            e.tensor_tensor(a, a, ss[:, 0:8].unsqueeze(2).broadcast_to([P, 8, CMP]), ALU.subtract).then_inc(
                *od.done(*at("cat_e", i + 1)))
            e.wait_ge(*at("cat_x", i + 1))
            e.tensor_tensor(a, a, c_01[:, i, :].unsqueeze(1).broadcast_to([P, 8, CMP]), ALU.mult).then_inc(*od.own())
            e.wait_ge(*od.latest())
            e.tensor_reduce(var[:, 0:8], a, AX.X, ALU.add).then_inc(*od.own())
            e.wait_ge(*od.latest())
            e.tensor_scalar(var[:, 0:8], var[:, 0:8], 1e-30, None, ALU.max).then_inc(*od.own())
            e.wait_ge(*od.latest())
            e.reciprocal(var[:, 0:8], var[:, 0:8]).then_inc(*od.own())
            e.wait_ge(*od.latest())
            e.tensor_tensor(a, a, var[:, 0:8].unsqueeze(2).broadcast_to([P, 8, CMP]), ALU.mult).then_inc(
                *od.done(*at("cat_p", i + 1)))
            e.wait_ge(*at("cat_tp", i + 1))
            e.tensor_copy(scratch[:, 1, 0:256], bank(5, 256)).then_inc(*od.done(*at("cat_pt", i + 1)))
            e.wait_ge(*at("cat_o", i + 1))
            g_c = gate[:, i, :].rearrange("p (h b) -> p h b", b=3)[:, :, 0:1].broadcast_to([P, 8, HD])
            e.tensor_tensor(o1[:, i, 0:W].rearrange("p (h d) -> p h d", d=HD),
                            bank(6).rearrange("p (h d) -> p h d", d=HD), g_c, ALU.mult).then_inc(
                *od.done(*at("cat_fin", i + 1)))

        def fin_nsa(j, k, r, free, value):
            hd, i = 2 * j + k // 4, 3 - k % 4
            hq, branch = hd % 8, hd // 8 + 1
            e.tensor_tensor(r, r, column(gate[:, i, :], 3 * hq + branch), ALU.mult).then_inc(*od.own())
            e.wait_ge(*od.latest())
            o = columns(o1, hq)(i)
            e.scalar_tensor_tensor(out=o, in0=bank(6 + k % 2, HD), scalar=r, in1=o, op0=ALU.mult,
                                   op1=ALU.add).then_inc(*od.done(free, value))

        def fin_to(dst):
            def fin(j, k, r, free, value):
                e.tensor_scalar(dst(2 * j + k // 4)(3 - k % 4), bank(6 + k % 2, HD), r, None, ALU.mult).then_inc(
                    *od.done(free, value))
            return fin

        dve_attend(e, od, att["nsa"], fin_nsa, 16)
        dve_attend(e, od, att["swa"], fin_to(lambda hd: columns(o1, hd + 8)), 24)
        dve_norm(e, od, "n1", 1, lambda t: o1[:, t, :], 2, lambda t: at("swa_ofree", 34))
        dve_post(e, od, "out1", 2)
        dve_norm(e, od, "n3", 3, lambda t: h[:, t, :], 1, lambda t: at("out1_res", t + 1))
        dve_up(e, od, "up1", True)
        dve_post(e, od, "down1", 4)

        dve_norm(e, od, "n5", 5, lambda t: h[:, t, :], 1, lambda t: at("down1_res", t + 1))
        plan = t_plan(T_IN2)
        e.wait_ge(*at("in2_copy", 4))
        e.tensor_scalar(var[:, 0:4], ss[:, 0:4], 1.0 / QR, EPS, ALU.mult, ALU.add).then_inc(*od.own())
        e.tensor_scalar(var[:, 4:8], ss[:, 4:8], 1.0 / KVR, EPS, ALU.mult, ALU.add).then_inc(
            *od.done(*at("in2_var", 1)))
        dve_refine(e, od, "in2", 1, 8)
        for t in range(NT):
            for x, (a, n, gn) in enumerate(((0, QR, g_qa), (QR, KVR, g_kva))):
                v = tok3[:, t, a:a + n]
                op = e.scalar_tensor_tensor(out=v, in0=v, scalar=rstd[:, 4 * x + t:4 * x + t + 1], in1=gn[:, :],
                                            op0=ALU.mult, op1=ALU.mult)
                if x:
                    op.then_inc(*od.done(*at("in2_tok", t + 1)))
                else:
                    op.then_inc(*od.own())
        for c in range(3):
            dve_turned(e, od, "in2", plan, c)
        plan = t_plan(T_MLA)
        for c in range(4):
            def rotate_tail(t, v):
                swapped_halves(e, od, v[:, :, HD:MQK], 4, ROPE // 2, m_cos[:, t, :], m_sin[:, t, :],
                               lambda: od.done(*at("mla_tok", 4 * c + t + 1)))
            head_norms(e, od, "mla", c, c + 1, 4, MQK, MQK, g_mq if c < 2 else g_mk, rotate_tail)
            dve_turned(e, od, "mla", plan, c)
        dve_attend(e, od, att["att2"], fin_to(lambda hd: columns(v2, hd)), 8)
        dve_stick(e, od, att["stk"])
        for i in range(8):
            dve_low(e, od, "x2", i)
        dve_residual(e, od, "out2")
        dve_norm(e, od, "n6", 6, lambda t: h[:, t, :], 1, lambda t: at("out2_res", t + 1))
        dve_up(e, od, "up2", False)
        dve_residual(e, od, "down2")

        dve_norm(e, od, "n7", 7, lambda t: h[:, t, :], 1, lambda t: at("down2_res", t + 1))
        e.wait_ge(*at("in3_copy", 4))
        x = decay[:, :, :]
        e.tensor_tensor(x, logf[:, :, :], f_bias[:, :].unsqueeze(1).broadcast_to([P, NT, 16]), ALU.add).then_inc(
            *od.own())
        e.wait_ge(*od.latest())
        e.scalar_tensor_tensor(out=logf[:, :, :], in0=x, scalar=-1.0, in1=x, op0=ALU.mult, op1=ALU.max).then_inc(
            *od.done(*at("fox_abs", 1)))
        e.wait_ge(*at("fox_ln", 1))
        e.scalar_tensor_tensor(out=logf[:, :, :], in0=x, scalar=0.0, in1=logf[:, :, :], op0=ALU.min,
                               op1=ALU.subtract).then_inc(*od.done(*at("fox_logf", 1)))
        e.wait_ge(*at("fox_decay", 1))
        e.tensor_copy(decay[:, :, :].rearrange("p a b -> p (a b)"), bank(7, 64)).then_inc(
            *od.done(*at("fox_dec_out", 1)))
        plan = t_plan(T_IN3)
        for c in range(1, 5):
            def decays_beside(t, v):
                two = tok3[:, t, :].rearrange("p (h d) -> p h d", d=66)
                dec = decay[:, t, 8 * ((c - 1) % 2):8 * ((c - 1) % 2) + 8].unsqueeze(2)
                is_k = c > 2
                e.memset(two[:, :, HD:HD + 1] if is_k else two[:, :, HD + 1:HD + 2], 1.0).then_inc(*od.own())
                e.tensor_scalar(two[:, :, HD + 1:HD + 2] if is_k else two[:, :, HD:HD + 1], dec,
                                -1.0 if is_k else 1.0, None, ALU.mult).then_inc(
                    *od.done(*at("in3_tok", 4 * (c - 1) + t + 1)))
            head_norms(e, od, "in3", c, c, 8, HD, 66, g_fk if c > 2 else g_fq, decays_beside)
            dve_turned(e, od, "in3", plan, c)
        dve_attend(e, od, att["fox"], fin_to(lambda hd: columns(v3, hd)), 8)
        for i in range(8):
            dve_low(e, od, "x3", i)
        dve_residual(e, od, "out3")
        dve_norm(e, od, "n8", 8, lambda t: h[:, t, :], 1, lambda t: at("out3_res", t + 1))
        dve_up(e, od, "up3", False)
        dve_residual(e, od, "down3")

    top.close()


def shape_constants():
    import numpy as np
    half = HD // 2
    inv = (np.float32(10000.0) ** (-np.arange(half, dtype=np.float32) / np.float32(half))).astype(np.float32)
    ang = np.arange(SEQ, dtype=np.float32)[:, None] * inv[None, :]
    cos, sin = np.cos(ang).astype(np.float32), np.sin(ang).astype(np.float32)
    mh = ROPE // 2
    inv_m = (np.float32(10000.0) ** (-np.arange(mh, dtype=np.float32) / np.float32(mh))).astype(np.float32)
    return {"rope_cos": np.concatenate([cos, cos], 1), "rope_sin": np.concatenate([-sin, sin], 1),
            "inv_freq": inv_m}


def kernel(**inputs):
    import numpy as np
    from concourse import bacc
    from concourse.bass_utils import run_bass_kernel_spmd

    nc = bacc.Bacc("TRN2", target_bir_lowering=False, num_devices=1)
    arrays, aps = {}, {}
    for name, value in {**inputs, **shape_constants()}.items():
        a = np.ascontiguousarray(value)
        arrays[f"in_{name}"] = a
        aps[name] = nc.dram_tensor(f"in_{name}", a.shape, mybir.dt.from_np(a.dtype), kind="ExternalInput").ap()
    out = nc.dram_tensor("out_dram", (1, SEQ, D), F32, kind="ExternalOutput").ap()
    build(nc, aps, out)
    r = run_bass_kernel_spmd(nc, [arrays], core_ids=[0])
    return r.results[0]["out_dram"]
```

```python
from contextlib import ExitStack

import concourse.bass as bass
from concourse import mybir

P = 128
SEQ = 512
D = 1024
NT = SEQ // P
KD = D // P
DFF = 2816
KF = DFF // P
HD = 64
EPS = 1e-6
NEG = -1e30
W = 512
SLAB = 1024
TOKW = 528
QR, KVR, ROPE = 256, 128, 32
MQK = 96
CMP, CMPS = 32, 16
SMALLS = 18
NCB = SEQ // CMPS - 1
FILL = 8

F32 = mybir.dt.float32
F32R = mybir.dt.float32r
BF16 = mybir.dt.bfloat16
I32 = mybir.dt.int32
ALU = mybir.AluOpType
ACT = mybir.ActivationFunctionType
AX = mybir.AxisListType
EXP_LN = "natural_log_exp_and_others"

TWO_PI_HI = 6.28125
TWO_PI_MID = 0.0019350051879882812
TWO_PI_LO = 3.019916050561e-07
PI = 3.1415925


class Order:

    def __init__(self, sem):
        self.sem, self.n, self.base, self.before, self.newest = sem, 0, 0, 0, None

    def own(self):
        self.n += 1
        self.newest = (self.sem, self.base + self.n)
        return self.sem, 1

    def done(self, sem, value):
        self.newest = (sem, value)
        return sem, 1

    def latest(self):
        return self.newest

    def enter(self, j, per):
        self.before, self.n = self.n, 0
        self.base = self.before + j * per

    def leave(self, count, per):
        assert self.n == per, f"{self.n} steps in the loop's body"
        self.n, self.base = self.before + count * per, 0


def build(nc, A, out):
    top = ExitStack()
    sems = {}

    def sem(name):
        name = shared.get(name, (name, 0))[0]
        if name not in sems:
            sems[name] = top.enter_context(nc.semaphore(name))
        return sems[name]

    shared = {}

    def share(kind, what, counts, start=0):
        for phase, n in counts:
            shared[f"{phase}_{what}"] = (f"{kind}_{what}", start)
            start += n

    NORMS = ["n0", "n1", "n3", "n5", "x2", "n6", "n7", "x3", "n8"]
    RMS = [p for p in NORMS if p[0] == "n"]
    WHOLE = ("n0", "n3", "n5")
    for what in ("tp", "hi", "lo"):
        share("norm", what, [(p, 2 * NT) for p in NORMS])
    share("norm", "sq", [(p, NT if p in WHOLE else 2 * NT) for p in RMS])
    share("norm", "var", [(p, NT) for p in RMS])
    share("norm", "y", [(p, NT) for p in RMS])
    share("norm", "xn", [(p, NT) for p in RMS])
    UPS, OUTS = ["up1", "up2", "up3"], ["out1", "down1", "out2", "down2", "out3", "down3"]
    share("up", "acc", [(p, 33) for p in UPS])
    share("up", "s", [(p, 4 * 11 if p == "up1" else 2 * 11) for p in UPS])
    share("up", "h", [(p, KF) for p in UPS], 2)
    for what in ("hi", "lo"):
        share("up", what, [(p, KF) for p in UPS])
    share("out", "acc", [(p, 6) for p in OUTS])
    POSTS = ("out1", "down1")
    share("out", "res", [(p, NT if p in POSTS else 2 * NT) for p in OUTS])
    share("out", "sq", [(p, 2 * NT) for p in POSTS])
    share("out", "var", [(p, NT) for p in POSTS])
    share("out", "y", [(p, NT) for p in POSTS])

    def at(name, value):
        name, start = shared.get(name, (name, 0))
        return sem(name), value + start

    def sb(name, shape, dt=F32, ctx=top):
        return ctx.enter_context(nc.sbuf_tensor(name, shape, dt))

    ps = top.enter_context(nc.psum_tensor("ps", [P, 8 * W], F32))

    def bank(b, n=W, at=0, rows=P):
        return ps[0:rows, b * W + at:b * W + at + n]

    h = sb("h", [P, NT, D])
    raw = sb("raw", [P, 2, SLAB])
    w_hi = sb("w_hi", [P, 4, SLAB], F32R)
    w_lo = sb("w_lo", [P, 4, SLAB], F32R)
    gains = sb("gains", [P, 2, D])
    tok = sb("tok", [P, NT * TOKW])
    scratch = sb("scratch", [P, 2, W])
    ident = sb("ident", [P, P])
    ident_b = sb("ident_b", [P, P], BF16)
    causal = sb("causal", [P, P], BF16)
    strict = sb("strict", [P, P], BF16)
    band = sb("band", [P, P], BF16)
    one = sb("one", [P, 1])
    conv = sb("conv", [P, 4, 2 * KF])
    pe_t = sb("pe_t", [HD, 2, 2, CMPS])
    sink = sb("sink", [P, 8])
    neg_sink = sb("neg_sink", [P, 8])
    g_qa = sb("g_qa", [P, QR])
    g_kva = sb("g_kva", [P, KVR])
    g_mq = sb("g_mq", [P, MQK])
    g_mk = sb("g_mk", [P, MQK])
    g_col = sb("g_col", [P, 4])
    rot = sb("rot", [P, 4 * ROPE])
    m_table = sb("m_table", [P, 2, 2, NT, ROPE])
    f_bias = sb("f_bias", [P, 16])
    k_rope = sb("k_rope", [P, NT, ROPE])
    m_cos = sb("m_cos", [P, NT, ROPE])
    m_sin = sb("m_sin", [P, NT, ROPE])
    ss = sb("ss", [P, 32])
    var = sb("var", [P, 32])
    rstd = sb("rstd", [P, 32])
    sq_a = sb("sq_a", [P, 32])
    nmax = sb("nmax", [P, 8])
    den = sb("den", [P, 8])
    esink = sb("esink", [P, 8])
    dump = sb("dump", [P, D], BF16)
    rg = sb("rg", [P, 2])

    lay = ExitStack()
    xt_hi = sb("xt_hi", [P, KD, SEQ], F32R, lay)
    xt_lo = sb("xt_lo", [P, KD, SEQ], F32R, lay)
    lay.close()
    lay = ExitStack()
    q_st = sb("q_st", [P, 2, SEQ], F32, lay)
    prob = sb("prob", [P, 4, SEQ], F32, lay)
    prob_t = sb("prob_t", [P, 2, SEQ], F32, lay)
    sb_ln = sb("sb_ln", [P, 4, SEQ], F32, lay)
    lay.close()
    lay = ExitStack()
    f_hi = sb("f_hi", [P, 2, CMPS, 62], F32R, lay)
    f_lo = sb("f_lo", [P, 2, CMPS, 62], F32R, lay)
    f_raw = sb("f_raw", [P, 2, CMPS, 62], F32, lay)
    cat_e = sb("cat_e", [P, NT, 8 * CMP], F32, lay)
    cat_t = sb("cat_t", [P, NT, 8 * CMP], F32, lay)
    lay.close()
    lay = ExitStack()
    x_hold = sb("x_hold", [P, 2 * KD, SEQ], F32, lay)
    u = ExitStack()
    hid_hi = sb("hid_hi", [P, KF, SEQ], F32R, u)
    hid_lo = sb("hid_lo", [P, KF, SEQ], F32R, u)
    u.close()
    u = ExitStack()
    qt1 = sb("qt1", [HD, 16, SEQ], F32, u)
    kt1 = sb("kt1", [HD, 8, SEQ], F32, u)
    vct = sb("vct", [HD, 2, SEQ], F32, u)
    v1 = sb("v1", [P, NT, 6 * HD], F32, u)
    o1 = sb("o1", [P, NT, D], F32, u)
    rope_c = sb("rope_c", [P, NT, HD], F32, u)
    rope_s = sb("rope_s", [P, NT, HD], F32, u)
    gate = sb("gate", [P, NT, 24], F32, u)
    c_add = sb("c_add", [P, NT, CMP], F32, u)
    c_01 = sb("c_01", [P, NT, CMP], F32, u)
    w2_sb = sb("w2_sb", [P, 2, 2, HD], F32, u)
    kct = sb("kct", [HD, 2, CMP], F32, u)
    vbd = sb("vbd", [P, 2, 4 * HD], F32, u)
    chid = sb("chid", [P, 2, 256], F32, u)
    chid_t = sb("chid_t", [P, 2, 2, 62], F32, u)
    u.close()
    u = ExitStack()
    qm = sb("qm", [MQK, 8, SEQ], F32, u)
    qs = sb("qs", [HD, 8, SEQ], F32, u)
    ksb = sb("ksb", [HD, 8, SEQ], F32, u)
    v2 = sb("v2", [P, NT, D], F32, u)
    ckv_hi = sb("ckv_hi", [P, SEQ], F32R, u)
    ckv_lo = sb("ckv_lo", [P, SEQ], F32R, u)
    kk = ExitStack()
    km = sb("km", [MQK, 8, SEQ], F32, kk)
    kk.close()
    cq_hi = sb("cq_hi", [P, 2, SEQ], F32R, kk)
    cq_lo = sb("cq_lo", [P, 2, SEQ], F32R, kk)
    kk.close()
    u.close()
    u = ExitStack()
    qf = sb("qf", [HD + 2, 16, SEQ], F32, u)
    kf = sb("kf", [HD + 2, 16, SEQ], F32, u)
    v3 = sb("v3", [P, NT, D], F32, u)
    tri = sb("tri", [P, P], F32, u)
    ones = sb("ones", [P, P], F32, u)
    logf = sb("logf", [P, NT, 16], F32, u)
    logit_t = sb("logit_t", [16, SEQ], F32, u)
    decay = sb("decay", [P, NT, 16], F32, u)
    u.close()
    u = ExitStack()
    c_raw = sb("c_raw", [2 * KF, 4, P], F32, u)
    pe_raw = sb("pe_raw", [CMPS, 2, P], F32, u)
    pos_i = sb("pos_i", [P, NT], I32, u)
    pos_f = sb("pos_f", [P, NT], F32, u)
    inv_f = sb("inv_f", [P, ROPE // 2], F32, u)
    ang = sb("ang", [P, NT, ROPE // 2], F32, u)
    turn = sb("turn", [P, NT, ROPE // 2], F32, u)
    turn_i = sb("turn_i", [P, NT, ROPE // 2], I32, u)
    red = sb("red", [P, NT, ROPE // 2], F32, u)
    u.close()
    u_hold = sb("u_hold", [P, 2 * KF * SEQ], F32, lay)
    top.push(lay.pop_all())

    tok3 = tok[:, :].rearrange("p (t n) -> p t n", t=NT)
    tok_b = gains[:, :, :].rearrange("p a n -> p (a n)")[:, 0:NT * 4 * MQK].rearrange("p (t n) -> p t n", t=NT)
    xn = tok[:, 0:2 * D].rearrange("p (s n) -> p s n", s=2)
    half_u = tok[:, 0:4 * W].rearrange("p (s n) -> p s n", s=4)

    def cols(w, c0, n, kts):
        return w.rearrange("(k p) c -> p k c", p=P)[:, kts, c0:c0 + n] if isinstance(c0, int) else \
            w.rearrange("(k p) c -> p k c", p=P)[:, kts, bass.ds(c0, n)]

    class Phase:

        def __init__(self, name, g0, groups):
            self.name, self.g0, self.groups = name, g0, groups

    IN1 = [(0, 512), (512, 512), (1024, 280), (1304, 512), (1816, 256)]
    IN2 = [(416, 0, 4, 2), (512, 4, 4, 2), (384, 8, 1, 2), (512, 9, 4, 2), (384, 13, 1, 2), (512, 14, 1, 1),
           (512, 15, 4, 2), (512, 19, 1, 1)]
    CQ, SQ, Q0, SK, Q1, K0, SV, K1 = range(8)
    HEAD_CHUNKS = {Q0: 0, Q1: 1, K0: 2, K1: 3}
    g = 0
    phases = {}
    for name, n in (("in1", 5), ("cmp", 2), ("out1", 2), ("up1", 11), ("down1", 6), ("in2", 5),
                    ("out2", 2), ("up2", 11), ("down2", 6), ("in3", 7), ("out3", 2), ("up3", 11), ("down3", 6)):
        phases[name] = Phase(name, g, n)
        g += n
    split, slab_used = sem("split"), sem("slab_used")
    raw_full = [sem(f"raw_full{i}") for i in range(2)]

    block = top.enter_context(nc.Block())

    def sp_slab(e, n, parts):
        if not isinstance(n, int) or n >= 2:
            e.wait_ge(split, 2 * n - 2)
        for off, src in parts:
            k, c = src.shape[1], src.shape[2]
            dst = raw[:, n_slot(n), off:off + (k - 1) * STRIDE[0] + c]
            if k > 1:
                dst = raw[:, n_slot(n), :].rearrange("p (k c) -> p k c", c=STRIDE[0])[:, 0:k, off:off + c]
            else:
                dst = raw[:, n_slot(n), off:off + c].rearrange("p (k c) -> p k c", k=1)
            e.dma_start(dst, src).then_inc(raw_full[n_slot(n)], 32 // len(parts))

    STRIDE = [W]
    SLOT = [0]

    def n_slot(n):
        return SLOT[0] % 2

    def sp_group(e, grp, slabs, stride=W):
        STRIDE[0] = stride
        for s, parts in enumerate(slabs):
            SLOT[0] = s
            sp_slab(e, 4 * grp + s, parts)

    def gain_load(e, n, wait=None):
        if wait:
            e.wait_ge(*wait)
        rows = GAINS[n]
        col = 0
        for r in rows:
            w = r.shape[-1]
            e.dma_start(gains[:, n % 2, col:col + w], r.partition_broadcast(P)).then_inc(
                sem(f"gain_full{n % 2}"), 32 // len(rows))
            col += w

    GAINS = [[A["attn_pre_norm"][0]], [A["nsa_out_norm"][0], A["swa_out_norm"][0]], [A["attn_post_norm"][0]],
             [A["ffn_pre_norm"][0]], [A["ffn_post_norm"][0]], [A["l0_attn_norm_2"]], [A["l0_ffn_norm_2"]],
             [A["l1_attn_norm_2"]], [A["l1_ffn_norm_2"]]]

    def wait_apart(e, s, value):
        e.wait_ge(s, value)
        e.sem_inc(sem("passed"), 1)

    def gain_ready(e, n):
        e.wait_ge(*at(f"gain_full{n % 2}", 32 * (n // 2 + 1)))

    def two_kt(w, c0, n):
        return [[(0, cols(w, c0, n, slice(2 * s, 2 * s + 2)))] for s in range(4)]

    def up_slabs(wg, wu, off_u, gi):
        return [[(0, cols(wg, gi * 256, 256, slice(2 * s, 2 * s + 2))),
                 (256, cols(wu, gi * 256 + off_u, 256, slice(2 * s, 2 * s + 2)))] for s in range(4)]

    def down_slabs(w, c0):
        kts = [slice(2 * s, 2 * s + 2) for s in range(10)] + [slice(20, 21), slice(21, 22)]
        return [[(0, cols(w, c0, W, k))] for k in kts]

    def sp_ffn(e, up, down, wg, wu, off_u, wd, mid):
        with e.Fori(0, up.groups) as gi:
            sp_group(e, gi + up.g0, up_slabs(wg, wu, off_u, gi))
        mid()
        with e.Fori(0, 2) as c:
            slabs = down_slabs(wd, c * W)
            for q in range(3):
                sp_group(e, 3 * c + (down.g0 + q), slabs[4 * q:4 * q + 4])

    @block.sync
    def _(e):
        ph = phases
        for t in range(NT):
            e.dma_start(h[:, t, :], A["x"][0, t * P:(t + 1) * P, :]).then_inc(sem(f"h_full{t}"), 16)
        gain_load(e, 0)
        for i, (c0, n) in enumerate(IN1):
            sp_group(e, ph["in1"].g0 + i, two_kt(A["w_in"][0], c0, n))
            if i == 0:
                gain_load(e, 1)
        gain_load(e, 2, at("n0_xn", NT))
        for kv in range(2):
            w1 = A["cmp_w1"][0, kv]
            sp_group(e, ph["cmp"].g0 + kv,
                     [[(0, cols(w1, 0, 256, slice(4 * s, 4 * s + 4)))] for s in range(4)], 256)
        with e.Fori(0, 2) as c:
            sp_group(e, c + ph["out1"].g0, two_kt(A["w_out"][0], c * W, W))
        gain_load(e, 3, at("n1_xn", NT))

        def mid1():
            gain_load(e, 4, at("out1_res", NT))
            gain_load(e, 5, at("n3_xn", NT))

        sp_ffn(e, ph["up1"], ph["down1"], A["w_up"][0], A["w_up"][0], DFF, A["w_down"][0], mid1)
        qw, kw, iw = A["l0_mla_w_q_up_2"], A["l0_mla_w_kv_up_2"], A["l0_w_in_2"]
        slabs = (two_kt(iw, 0, 416) + two_kt(iw, 416, W) + [[(0, cols(qw, 0, 384, slice(0, 2)))]] + two_kt(iw, 928, W)
                 + [[(0, cols(qw, 384, 384, slice(0, 2)))], [(0, cols(kw, 0, W, slice(0, 1)))]]
                 + two_kt(iw, 1440, W) + [[(0, cols(kw, W, W, slice(0, 1)))]])
        for i in range(ph["in2"].groups):
            sp_group(e, ph["in2"].g0 + i, slabs[4 * i:4 * i + 4])
        gain_load(e, 6, at("in2_tp", 35))
        gain_load(e, 7)
        with e.Fori(0, 2) as c:
            sp_group(e, c + ph["out2"].g0, two_kt(A["l0_w_o_2"], c * W, W))
        sp_ffn(e, ph["up2"], ph["down2"], A["l0_w_gate_2"], A["l0_w_up_2"], 0, A["l0_w_down_2"], lambda: None)
        sp_group(e, ph["in3"].g0, two_kt(A["l1_w_in_2"], 0, W))
        sp_group(e, ph["in3"].g0 + 1, two_kt(A["l1_w_in_2"], 3 * D, 16))
        with e.Fori(1, 6) as c:
            sp_group(e, c + (ph["in3"].g0 + 1), two_kt(A["l1_w_in_2"], c * W, W))
        gain_load(e, 8, at("n6_xn", NT))
        with e.Fori(0, 2) as c:
            sp_group(e, c + ph["out3"].g0, two_kt(A["l1_w_o_2"], c * W, W))
        sp_ffn(e, ph["up3"], ph["down3"], A["l1_w_gate_2"], A["l1_w_up_2"], 0, A["l1_w_down_2"], lambda: None)
        for t in range(NT):
            e.wait_ge(*at("down3_res", NT + t + 1))
            e.dma_start(out[0, t * P:(t + 1) * P, :], h[:, t, :]).then_inc(sem("stored"), 16)
        e.wait_ge(*at("stored", 16 * NT))

    def split_slab(e, grp, s, width):
        n = 4 * grp + s
        e.wait_ge(raw_full[s % 2], 64 * grp + 32 * (s // 2 + 1))
        free = n - 3
        wait_apart(e, slab_used, free)
        r = raw[:, s % 2, 0:width]
        e.tensor_scalar(w_hi[:, s, 0:width], r, 1.0, 0.0, ALU.mult, ALU.add).then_inc(split, 1)
        e.wait_ge(split, 2 * n + 1)
        e.tensor_tensor(w_lo[:, s, 0:width], r, w_hi[:, s, 0:width].bitcast(F32), ALU.subtract).then_inc(split, 1)

    def split_cols(e, grp, s, k, n):
        m = 4 * grp + s
        e.wait_ge(raw_full[s % 2], 64 * grp + 32 * (s // 2 + 1))
        if grp > 0:
            e.wait_ge(slab_used, m - 3)

        def view(x):
            return x.rearrange("p (k c) -> p k c", c=W)[:, 0:k, 0:n]

        e.tensor_scalar(view(w_hi[:, s, :]), view(raw[:, s % 2, :]), 1.0, 0.0, ALU.mult, ALU.add).then_inc(split, 1)
        e.wait_ge(split, 2 * m + 1)
        e.tensor_tensor(view(w_lo[:, s, :]), view(raw[:, s % 2, :]), view(w_hi[:, s, :].bitcast(F32)),
                        ALU.subtract).then_inc(split, 1)

    def split_all(e, phase, first=0, widths=(SLAB,) * 4):
        with e.Fori(first, phase.groups) as gi:
            for s in range(4):
                split_slab(e, gi + phase.g0, s, widths[s])

    def split_down(e, phase):
        with e.Fori(0, 2) as c:
            for q in range(3):
                for s in range(4):
                    split_slab(e, 3 * c + (phase.g0 + q), s, W if q == 2 and s >= 2 else SLAB)

    def stage_queries(e, ph, q_src, rows, iters, ready, before=None):
        for s, v in ready:
            e.wait_ge(s, v)

        def one_head(hd, hh):
            e.tensor_copy(q_st[0:rows, hh, :], q_src(hd)).then_inc(sem(f"{ph}_q"), 1)

        for hh in range(2):
            if before:
                e.wait_ge(*at(f"{before[0]}_qk", before[1] - 4 + 4 * hh))
            one_head(hh, hh)
        with e.Fori(1, iters) as j:
            for hh in range(2):
                e.wait_ge(*at(f"{ph}_qk", 8 * j + (4 * hh - 4)))
                one_head(2 * j + hh, hh)

    def heads(t, hd, off=0, m=None):
        if isinstance(hd, int):
            return t[:, hd, :]
        return t[:, bass.ds(hd, 1), :].rearrange("p a s -> p (a s)")

    @block.gpsimd
    def _(e):
        consts = sem("consts")
        e.memset(ident[:, :], 0.0).then_inc(consts, 1)
        e.memset(one[:, :], 1.0).then_inc(consts, 1)
        for m in (causal, strict, band):
            e.memset(m[:, :], 0.0).then_inc(consts, 1)
        e.memset(c_add[:, :, :], 0.0).then_inc(consts, 1)
        e.memset(c_01[:, :, :], 1.0).then_inc(consts, 1)
        e.memset(kct[:, :, :], 0.0).then_inc(consts, 1)
        e.memset(vbd[:, :, :], 0.0).then_inc(consts, 1)
        e.memset(g_col[:, :], 1.0).then_inc(consts, 1)
        e.wait_ge(consts, 10)
        sel = lambda t, op, fill, base, pat, ch: e.affine_select(
            out=t, in_=t, compare_op=op, fill=fill, base=base, pattern=pat, channel_multiplier=ch).then_inc(consts, 1)
        sel(ident[:, :], ALU.not_equal, 1.0, 0, [[-1, P]], 1)
        sel(causal[:, :], ALU.is_ge, NEG, 0, [[-1, P]], 1)
        sel(strict[:, :], ALU.is_ge, NEG, -1, [[-1, P]], 1)
        sel(band[:, :], ALU.is_ge, NEG, -1, [[1, P]], -1)
        sel(c_add[:, :, :], ALU.is_ge, NEG, -(CMP - 1), [[P, NT], [-CMPS, CMP]], 1)
        sel(c_01[:, :, :], ALU.is_ge, 0.0, -(CMP - 1), [[P, NT], [-CMPS, CMP]], 1)
        e.wait_ge(consts, 11)
        e.tensor_copy(ident_b[:, :], ident[:, :]).then_inc(consts, 1)
        ph = phases
        for i, (c0, n) in enumerate(IN1):
            for s in range(4):
                split_cols(e, ph["in1"].g0 + i, s, 2, n)
        split_all(e, ph["cmp"])
        stage_queries(e, "nsa", lambda hd: heads(qt1, hd if isinstance(hd, int) else hd % 8), HD, 8,
                      [at("in1_tpa", 13), at("in1_tpd", 13), (slab_used, 4 * (ph["cmp"].g0 + 2)), at("cat_s", 1)])
        stage_queries(e, "swa", lambda hd: heads(qt1, hd + 8), HD, 4, [], ("nsa", 64))
        split_all(e, ph["out1"])
        split_all(e, ph["up1"])
        split_down(e, ph["down1"])
        for n, slab0, slabs, k in IN2:
            for i in range(slab0, slab0 + slabs):
                split_cols(e, ph["in2"].g0 + i // 4, i % 4, k, n)
        stage_queries(e, "att2", lambda hd: heads(qm, hd), MQK, 4,
                      [at("in2_tpa", 16), at("in2_tpd", 19)])
        stage_queries(e, "stk", lambda hd: heads(qs, hd), HD, 4, [], ("att2", 32))
        split_all(e, ph["out2"])
        split_all(e, ph["up2"])
        split_down(e, ph["down2"])
        for s in range(4):
            split_cols(e, ph["in3"].g0, s, 2, W)
        e.memset(tri[:, :], 1.0).then_inc(consts, 1)
        e.memset(ones[:, :], 1.0).then_inc(consts, 1)
        e.wait_ge(consts, 19)
        sel(tri[:, :], ALU.is_ge, 0.0, 0, [[1, P]], -1)
        for s in range(4):
            split_cols(e, ph["in3"].g0 + 1, s, 2, 16)
        split_all(e, ph["in3"], 2)
        stage_queries(e, "fox", lambda hd: heads(qf, hd), HD + 2, 8,
                      [at("in3_tpa", 16), at("in3_tpd", 16), (slab_used, 4 * (ph["in3"].g0 + 7))])
        split_all(e, ph["out3"])
        split_all(e, ph["up3"])
        split_down(e, ph["down3"])

    def staged(name, c):
        return tok_b if name == "in2" and c == K0 else tok3

    def alternate(items, scale=None):
        return [(off, w, (dst, scale), "ad"[i % 2]) for i, (off, w, dst) in enumerate(items)]

    T_IN1 = [
        alternate([(64 * i, HD, qt1[:, i, :]) for i in range(8)]),
        alternate([(0, HD, kt1[:, 0, :]), (64, HD, kt1[:, 1, :]), (128, HD, vct[:, 0, :]), (192, HD, vct[:, 1, :]),
                   (256, HD, kt1[:, 2, :]), (320, HD, kt1[:, 3, :])]),
        alternate([(64 * i, HD, kt1[:, 4 + i, :]) for i in range(2)]),
        alternate([(64 * i, HD, qt1[:, 8 + i, :]) for i in range(8)]),
        alternate([(64 * i, HD, kt1[:, 6 + i, :]) for i in range(2)]),
    ]
    def mla_heads(dst, h0, which):
        return alternate([(MQK * i, MQK, dst[:, h0 + i, :]) for i in range(4)], g_col[0:MQK, which:which + 1])

    T_IN2 = [
        [(0, P, (cq_hi[:, 0, :], cq_lo[:, 0, :]), "s"), (P, P, (cq_hi[:, 1, :], cq_lo[:, 1, :]), "s"),
         (QR, P, (ckv_hi[:, :], ckv_lo[:, :]), "s")],
        alternate([(64 * i, HD, qs[:, i, :]) for i in range(8)]),
        mla_heads(qm, 0, 0),
        alternate([(64 * i, HD, ksb[:, i, :]) for i in range(8)]),
        mla_heads(qm, 4, 0),
        mla_heads(km, 0, 1),
        [],
        mla_heads(km, 4, 1),
    ]
    T_IN3 = [alternate([(66 * i, 66, (qf, kf)[c // 2][:, 8 * (c % 2) + i, :]) for i in range(8)],
                       g_col[0:66, 2 + c // 2:3 + c // 2]) for c in range(4)] + [[], []]
    T_IN3.insert(1, [])
    FOX_CHUNKS = {0: 0, 2: 1, 3: 2, 4: 3}

    def t_plan(t_lists):
        plan, n = [], {"a": 0, "d": 0}
        for c, units in enumerate(t_lists):
            for un in units:
                k = "a" if un[3] == "a" else "d"
                n[k] += 1
                plan.append((c, un, k, n[k]))
        return plan

    def emptied(e, name, plan, i):
        _, _, k, count = plan[i]
        e.wait_ge(*at(f"{name}_tp{k}", count))

    def mm3(e, o, s_hi, s_lo, m_hi, m_lo, start, stop):
        e.matmul(o, s_hi, m_hi, start=start, stop=False)
        e.matmul(o, s_hi, m_lo, start=False, stop=False)
        return e.matmul(o, s_lo, m_hi, start=False, stop=stop)

    def pe_turn(e, name, plan, c, tok_waits):
        if any(p[0] == c for p in plan):
            for s, v in tok_waits:
                e.wait_ge(s, v)
        for i, (cc, (off, w, _, _), _, _) in enumerate(plan):
            if cc != c:
                continue
            if i >= 4:
                emptied(e, name, plan, i - 4)
            for t in range(NT):
                m = e.transpose(bank(ODD[i % 4], P, t * P, w), staged(name, c)[:, t, off:off + w], ident[:, :])
            m.then_inc(sem(f"{name}_tp"), 1)

    def pe_project(e, name, chunks, plan, turns, tok_waits, xt, turn, hooks={}):
        g0 = phases[name].g0

        def tile(c, s, t):
            n, s0, slabs, ks, x_of = chunks[c]
            slot = (s0 + s) % 4
            for k in range(ks):
                hi, lo = x_of(ks * s + k, t)
                m = mm3(e, bank(EVEN[t], n), hi, lo, w_hi[:, slot, k * W:k * W + n], w_lo[:, slot, k * W:k * W + n],
                        s == 0 and k == 0, s == slabs - 1 and k == ks - 1)
            if s == slabs - 1 and t < 3:
                m.then_inc(sem(f"{name}_acc"), 1)
            return m

        def narrow(c, s):
            if s == 0:
                e.wait_ge(*at(f"{name}_copy", 4 * wide(name, c)))
            for k in range(2):
                kt = 2 * s + k
                m = mm3(e, bank(EVEN[0], SEQ, 0, 16), w_hi[:, s, k * W:k * W + 16], w_lo[:, s, k * W:k * W + 16],
                        xt_hi[:, kt, :], xt_lo[:, kt, :], kt == 0, kt == KD - 1)
            m.then_inc(slab_used, 1)

        def slab_there(c, s):
            e.wait_ge(split, 2 * (4 * g0 + chunks[c][1] + s + 1))

        def input_there(t):
            e.wait_ge(*at(f"{xt}_lo", 2 * t + 2))

        if name == "in1":
            first_chunk(e, g0, turn, input_there, lambda s, t: tile(0, s, t))
        else:
            for pair in ((0, 1), (2, 3)):
                for s in range(4):
                    if pair[0] == 0:
                        slab_there(0, s)
                    for t in pair:
                        if s == 0:
                            input_there(t)
                        m = tile(0, s, t)
                    if pair[0] == 2:
                        m.then_inc(slab_used, 1)
                    elif s % 2:
                        turn(2 + s // 2)
        for c in range(1, len(chunks)):
            for s in range(chunks[c][2]):
                slab_there(c, s)
                if chunks[c][0] == 16:
                    narrow(c, s)
                    continue
                if c == 2 and name == "in2":
                    emptied(e, name, plan, 2)
                for t in range(NT):
                    if s == 0:
                        e.wait_ge(*at(f"{name}_copy", 4 * wide(name, c) - 3 + t))
                        if chunks[c - 1][0] == 16 and t == 0:
                            e.wait_ge(*at("fox_logits", 1))
                    m = tile(c, s, t)
                m.then_inc(slab_used, 1)
                for x in turns.get((c, s), ()):
                    pe_turn(e, name, plan, x, tok_waits(x))
                if (c, s) in hooks:
                    hooks[c, s]()
        pe_turn(e, name, plan, len(chunks) - 1, tok_waits(len(chunks) - 1))

    def x_model(k, t):
        return xt_hi[:, k, t * P:(t + 1) * P], xt_lo[:, k, t * P:(t + 1) * P]

    def x_hidden(k, t):
        return hid_hi[:, k, t * P:(t + 1) * P], hid_lo[:, k, t * P:(t + 1) * P]

    def wide(name, c):
        return c - 1 if name == "in3" and c > 1 else c

    def tile_done(e, name, c, t, slabs_end):
        if t == 3:
            e.wait_ge(slab_used, slabs_end)
        else:
            e.wait_ge(*at(f"{name}_acc", 3 * wide(name, c) + t + 1))

    EVEN, ODD = (0, 4, 1, 5), (2, 6, 3, 7)

    def turn_bank(name, i):
        t, q = i // 2, i % 2
        if name in ("n3", "n6", "n8"):
            return out_bank("out", q, t)
        if name in ("n0", "n5", "n7"):
            return out_bank("down", q, t)
        return 4 + i % 4

    def out_bank(name, c, t):
        if name.startswith("down"):
            return (ODD, EVEN)[c][t]
        return 4 * c + t

    def pe_to_xt(e, name, src, ready, t):
        e.wait_ge(*ready(t))
        for q in range(2):
            i = 2 * t + q
            if i >= 4 and name in ("n1", "x2", "x3"):
                e.wait_ge(*at(f"{name}_lo", i - 3))
            for k in range(4):
                m = e.transpose(bank(turn_bank(name, i), P, k * P), src(t)[:, (4 * q + k) * P:(4 * q + k + 1) * P],
                                ident[:, :])
            m.then_inc(sem(f"{name}_tp"), 1)

    def first_chunk(e, g0, before, there, tile):
        before(0)
        for t in range(2):
            before(t + 1)
            for s in range(4):
                if t == 0:
                    e.wait_ge(split, 2 * (4 * g0 + s) + 2)
                elif s == 0:
                    before(NT - 1)
                if s == 0:
                    there(t)
                tile(s, t)
        for s in range(4):
            for t in (2, 3):
                if s == 0:
                    there(t)
                m = tile(s, t)
            m.then_inc(slab_used, 1)

    def slab_tile(e, name, c, s, kt, x_of, last, t):
        for i, k in enumerate(kt):
            hi, lo = x_of(k, t)
            m = mm3(e, bank(out_bank(name, c, t)), hi, lo, w_hi[:, s % 4, i * W:(i + 1) * W],
                    w_lo[:, s % 4, i * W:(i + 1) * W], k == 0, k == last)
        if k == last and t < 3:
            m.then_inc(sem(f"{name}_acc"), 1)
        return m

    def pe_slabs(e, name, c, s0, kts, x_of, hid=None):
        phase = phases[name]
        per = phase.groups // 2
        last = DOWN_KTS[-1][-1] if hid else KD - 1
        for s, kt in enumerate(kts, s0):
            e.wait_ge(split, 2 * (4 * (per * c + phase.g0) + s) + 2)
            if hid and c == 0:
                e.wait_ge(*at(f"{hid}_lo", 2 * (kt[-1] // 2) + 2))
            for t in range(NT):
                m = slab_tile(e, name, c, s, kt, x_of, last, t)
            m.then_inc(slab_used, 1)

    def pe_pairs(e, name, c, s0, kts, x_of, last, turn, when):
        phase = phases[name]
        per = phase.groups // 2
        for pair in ((0, 1), (2, 3)):
            for s, kt in enumerate(kts, s0):
                if pair[0] == 0:
                    e.wait_ge(split, 2 * (4 * (per * c + phase.g0) + s) + 2)
                for t in pair:
                    m = slab_tile(e, name, c, s, kt, x_of, last, t)
                if pair[0] == 2:
                    m.then_inc(slab_used, 1)
                    for t in when.get(s - s0, ()) if turn else ():
                        turn(t)

    def pe_out(e, name, xt, turn_in, turn_next, when):
        def there(t):
            e.wait_ge(*at(xt, 2 * t + 2))

        first_chunk(e, phases[name].g0, turn_in, there, lambda s, t: slab_tile(e, name, 0, s, OUT_KTS[s], x_model, KD - 1, t))
        pe_pairs(e, name, 1, 0, OUT_KTS, x_model, KD - 1, turn_next, when)

    def pe_down(e, name, up, turn_next, when):
        e.wait_ge(*at(f"{up}_h", 20))
        for c in range(2):
            pe_slabs(e, name, c, 0, DOWN_KTS[:8] if c else DOWN_KTS, x_hidden, up)
        pe_pairs(e, name, 1, 8, DOWN_KTS[8:], x_hidden, KF - 1, turn_next, when)

    OUT_KTS = [(2 * s, 2 * s + 1) for s in range(4)]
    DOWN_KTS = [(2 * s, 2 * s + 1) for s in range(10)] + [(20,), (21,)]

    def pe_up(e, name, xt, turn):
        g0 = phases[name].g0

        def tile(odd, s, j, T):
            for k in range(2):
                kt = 2 * s + k
                m = mm3(e, bank((ODD if odd else EVEN)[j], T.stop - T.start, T.start),
                        w_hi[:, s, k * W + j * P:k * W + (j + 1) * P], w_lo[:, s, k * W + j * P:k * W + (j + 1) * P],
                        xt_hi[:, kt, T], xt_lo[:, kt, T], kt == 0, kt == KD - 1)
            return m

        def chunk(gi, odd):
            for s in range(4):
                e.wait_ge(split, 8 * (gi + g0) + (2 * s + 2))
                for j in range(4):
                    if s == 0 and j == 0:
                        e.wait_ge(*at(f"{name}_h", 2 * (gi - 1)))
                    m = tile(odd, s, j, slice(0, SEQ))
                    if s == 3 and j < 3:
                        m.then_inc(sem(f"{name}_acc"), 1)
                m.then_inc(slab_used, 1)

        for T, tiles in ((slice(0, SEQ // 2), 2), (slice(SEQ // 2, SEQ), 4)):
            e.wait_ge(*at(f"{xt}_lo", 2 * tiles))
            for s in range(4):
                if tiles == 2:
                    e.wait_ge(split, 8 * g0 + (2 * s + 2))
                for j in range(4):
                    m = tile(0, s, j, T)
                    if tiles == 4 and s == 3 and j < 3:
                        m.then_inc(sem(f"{name}_acc"), 1)
                if tiles == 4:
                    m.then_inc(slab_used, 1)
                elif s % 2:
                    turn(2 + s // 2)
        with e.Fori(0, 5) as j:
            chunk(2 * j + 1, 1)
            chunk(2 * j + 2, 0)

    def columns(ap3, hd):
        return lambda kt: (ap3[:, kt, hd * HD:(hd + 1) * HD] if isinstance(hd, int)
                           else ap3[:, kt, bass.ds(hd * HD, HD)])

    def span(cfg, i):
        return (max(0, i - 1) if cfg["band"] else 0), i + 1

    def ahead(stage, j, k, last):
        if k < 8:
            stage(j, k)
        elif not last:
            stage(j + 1, k - 8)

    def pe_attend(e, cfg):
        name, iters, look = cfg["name"], cfg["iters"], cfg["look"]

        def scores(j, k):
            hh, i = k // 4, 3 - k % 4
            k0, k1 = span(cfg, i)
            n = (k1 - k0) * P
            if k % 4 == 0:
                e.wait_ge(*at(f"{name}_q", 2 * j + (hh + 1)))
            o = bank(k % 4, n)
            e.matmul(o, q_st[0:cfg["dh"], hh, i * P:(i + 1) * P], cfg["k"](2 * j + hh)[:, k0 * P:k1 * P],
                     start=True, stop=False)
            last = k1 - k0 - 1
            if cfg["band"] and i > 0:
                e.matmul(bank(k % 4, P), ident_b[:, :], band[:, :], start=False, stop=False)
            e.matmul(bank(k % 4, P, last * P), ident_b[:, :], cfg["mask"][:, :], start=False, stop=True).then_inc(
                sem(f"{name}_qk"), 1)

        def turn_probs(j, k):
            k0, k1 = span(cfg, 3 - k % 4)
            e.wait_ge(*at(f"{name}_p", 8 * j + (k + 1)))
            for x in range(k1 - k0):
                m = e.transpose(bank(4 + k % 2, P, x * P), prob[:, k % 4, x * P:(x + 1) * P], ident[:, :])
            m.then_inc(sem(f"{name}_tp"), 1)

        def values(j, k):
            k0, k1 = span(cfg, 3 - k % 4)
            v = cfg["v"](2 * j + k // 4)
            e.wait_ge(*at(f"{name}_pt", 8 * j + (k + 1)))
            e.wait_ge(*at(f"{name}_ofree", 8 * j + (k + 1)))
            for x in range(k1 - k0):
                m = e.matmul(bank(6 + k % 2, HD), prob_t[:, k % 2, x * P:(x + 1) * P], v(k0 + x),
                             start=x == 0, stop=x == k1 - k0 - 1)
            m.then_inc(sem(f"{name}_pv"), 1)

        for s, v in cfg.get("start", ()):
            e.wait_ge(s, v)
        e.sem_inc(sem(f"{name}_pv"), 2)
        for k in range(look + 1):
            scores(0, k)
        for s, v in cfg["banks"]:
            e.wait_ge(s, v)
        for _ in range(FILL):
            e.matmul(bank(6), ident_b[:, :], dump[:, 0:W], start=True, stop=True)
        turn_probs(0, 0)

        def body(j, last):
            for k in range(1, 9):
                ahead(scores, j, k + look, last)
                ahead(turn_probs, j, k, last)
                values(j, k - 1)

        with e.Fori(0, iters - 1) as j:
            body(j, False)
        body(iters - 1, True)

    att = {
        "nsa": dict(name="nsa", iters=8, look=3, dh=HD, band=False, mask=causal,
                    k=lambda hd: heads(kt1, hd // 4 + 2), v=lambda hd: columns(v1, hd // 4),
                    banks=[at("cat_fin", NT)]),
        "swa": dict(name="swa", iters=4, look=3, dh=HD, band=True, mask=causal,
                    k=lambda hd: heads(kt1, hd // 4 + 6), v=lambda hd: columns(v1, hd // 4 + 4),
                    banks=[at("nsa_ofree", 66)]),
        "att2": dict(name="att2", iters=4, look=3, dh=MQK, band=False, mask=causal,
                     k=lambda hd: heads(km, hd), v=lambda hd: columns(v2, hd),
                     start=[at("in2_tpa", 16), at("in2_tpd", 19), at("in2_copy", 32)], banks=[]),
        "stk": dict(name="stk", iters=4, look=3, dh=HD, band=False, mask=strict,
                    k=lambda hd: heads(ksb, hd), v=lambda hd: columns(v2, hd + 8),
                    banks=[at("att2_ofree", 34)]),
        "fox": dict(name="fox", iters=8, look=3, dh=HD + 2, band=False, mask=causal,
                    k=lambda hd: heads(kf, hd), v=lambda hd: columns(v3, hd),
                    start=[at("in3_tpa", 16), at("in3_tpd", 16), at("in3_copy", 23)], banks=[at("in3_copy", 24)]),
    }

    @block.tensor
    def _(e):
        def turn_smalls():
            e.wait_ge(*at("small_full", 16 * SMALLS))
            for w in range(4):
                e.transpose(bank(7, 2 * KF, w * 2 * KF), c_raw[:, w, :], ident[0:2 * KF, 0:2 * KF])
            for kv in range(2):
                for par in range(2):
                    m = e.transpose(bank(6, CMPS, (2 * kv + par) * CMPS, HD), pe_raw[:, kv, par * HD:(par + 1) * HD],
                                    ident[0:CMPS, 0:CMPS])
            m.then_inc(sem("pre_tp"), 1)

        e.wait_ge(*at("consts", 17))
        xn_ready = lambda name: lambda t: at(f"{name}_xn", t + 1)
        xn_of = lambda t: xn[:, t % 2, :]
        def turn(name):
            return lambda t: pe_to_xt(e, name, xn_of, xn_ready(name), t)

        tokd = {0: 4, 1: 8, 2: 12, 3: 16, 4: 20}
        each = lambda widths: [(n, 4 * c, 4, 2, x_model) for c, n in enumerate(widths)]
        pe_project(e, "in1", each([n for _, n in IN1]), t_plan(T_IN1), {(c, 2): (c - 1,) for c in range(1, 5)},
                   lambda c: [at("in1_copy", 4 * c + 4), at("in1_tok", tokd[c]), at("pre_out", 1)], "n0", turn("n0"),
                   {(1, 0): turn_smalls})
        e.wait_ge(*at("in1_copy", 20))
        e.wait_ge(*at("in1_tpa", 13))
        e.wait_ge(*at("in1_tpd", 13))
        g0 = phases["cmp"].g0
        for kv in range(2):
            for s in range(4):
                e.wait_ge(split, 2 * (4 * (g0 + kv) + s + 1))
                if s == 0:
                    e.wait_ge(*at("cmp_f", kv + 1))
                for k in range(4):
                    pp = 4 * s + k
                    m = mm3(e, bank(kv, 256, 0, 62), f_hi[:, kv, pp, :], f_lo[:, kv, pp, :],
                            w_hi[:, s, k * 256:(k + 1) * 256], w_lo[:, s, k * 256:(k + 1) * 256],
                            pp == 0, pp == CMPS - 1)
                m.then_inc(slab_used, 1)
        for kv in range(2):
            e.wait_ge(*at("cmp_gelu", kv + 1))
            for x in range(2):
                m = e.transpose(bank(2, 62, (2 * kv + x) * 62), chid[0:62, kv, x * P:(x + 1) * P],
                                ident[0:62, 0:62])
            m.then_inc(sem("cmp_tp"), 1)
        e.wait_ge(*at("cmp_ht", 1))
        for x in range(2):
            m = e.matmul(bank(3, 62, 0, HD), w2_sb[:, 0, x, :], chid_t[:, 0, x, :], start=x == 0, stop=x == 1)
        m.then_inc(sem("cmp_kv"), 1)
        for hd in range(2):
            for x in range(2):
                m = e.matmul(bank(hd, HD, 0, NCB), chid_t[:, 1, x, hd * NCB:(hd + 1) * NCB], w2_sb[:, 1, x, :],
                             start=x == 0, stop=x == 1)
        m.then_inc(sem("cmp_kv"), 1)
        e.wait_ge(*at("cmp_out", 1))
        for i in range(NT):
            for hd in range(8):
                m = e.matmul(bank(4 + i // 2, CMP, i % 2 * 8 * CMP + hd * CMP), qt1[:, hd, i * P:(i + 1) * P],
                             kct[:, hd // 4, :], start=True, stop=True)
        m.then_inc(sem("cat_s"), 1)
        for i in range(NT):
            e.wait_ge(*at("cat_p", i // 2 + 1))
            for x in range(2):
                m = e.transpose(bank(6 + i // 2, P, (i % 2 * 2 + x) * P), cat_e[:, i, x * P:(x + 1) * P], ident[:, :])
            if i % 2:
                m.then_inc(sem("cat_tp"), 1)
        for i in range(NT):
            e.wait_ge(*at("cat_pt", 1 if i < 2 else 2))
            for x in range(2):
                m = e.matmul(bank(4 + i, 4 * HD, x * 4 * HD), cat_t[:, i, x * P:(x + 1) * P], vbd[:, x, :],
                             start=True, stop=True)
            m.then_inc(sem("cat_o"), 1)
        pe_attend(e, att["nsa"])
        pe_attend(e, att["swa"])
        pe_out(e, "out1", "n1_lo", turn("n1"), turn("n3"), {2: (0,), 3: (1,)})
        pe_up(e, "up1", "n3", turn("n3"))
        pe_down(e, "down1", "up1", turn("n5"), {3: (0, 1)})

        def x_cq(k, t):
            return cq_hi[:, k, t * P:(t + 1) * P], cq_lo[:, k, t * P:(t + 1) * P]

        def x_ckv(k, t):
            return ckv_hi[:, t * P:(t + 1) * P], ckv_lo[:, t * P:(t + 1) * P]

        x2 = {Q0: x_cq, Q1: x_cq, K0: x_ckv, K1: x_ckv}
        pe_project(e, "in2", [(*chunk, x2.get(c, x_model)) for c, chunk in enumerate(IN2)], t_plan(T_IN2),
                   {(SQ, 2): (CQ,), (Q0, 0): (SQ,), (SK, 2): (Q0,), (Q1, 0): (SK,), (SV, 1): (Q1,), (SV, 3): (K0,)},
                   lambda c: [at("in2_copy", 4 * c + 4)]
                   + ([at("in2_tok", 4 if c == CQ else 4 * HEAD_CHUNKS[c] + 8)] if c == CQ or c in HEAD_CHUNKS else []),
                   "n5", turn("n5"))
        pe_attend(e, att["att2"])
        pe_attend(e, att["stk"])
        pe_out(e, "out2", "x2_lo", lambda t: pe_to_xt(e, "x2", lambda t: v2[:, t, :], lambda t: at("stk_ofree", 34), t),
               turn("n6"), {1: (0,), 2: (1,)})
        pe_up(e, "up2", "n6", turn("n6"))
        pe_down(e, "down2", "up2", turn("n7"), {1: (0,), 3: (1,)})

        g3 = phases["in3"].g0
        plan = t_plan(T_IN3)

        def turn_logits():
            e.wait_ge(*at("fox_logits", 1))
            for t in range(NT):
                m = e.transpose(bank(7, 16, 64 + t * 16), logit_t[:, t * P:(t + 1) * P], ident[0:16, 0:16])
            m.then_inc(sem("fox_turned"), 1)

        def decays():
            e.wait_ge(*at("consts", 20))
            e.wait_ge(*at("fox_logf", 1))
            for t in range(NT):
                for x in range(t + 1):
                    m = e.matmul(bank(7, 16, t * 16), (tri if x == t else ones)[:, :], logf[:, x, :],
                                 start=x == 0, stop=x == t)
            m.then_inc(sem("fox_decay"), 1)

        def turn_first():
            e.wait_ge(*at("fox_dec_out", 1))
            pe_turn(e, "in3", plan, 0, [at("in3_copy", 4), at("in3_tok", 4)])

        pe_project(e, "in3", each([W, 16] + [W] * 5), plan, {(c, 2): (c - 1,) for c in (3, 4, 5)},
                   lambda c: [at("in3_copy", 4 * wide("in3", c) + 4), at("in3_tok", 4 * FOX_CHUNKS[c] + 4)] if c in FOX_CHUNKS else [],
                   "n7", turn("n7"), {(2, 0): turn_logits, (2, 1): decays, (2, 3): turn_first})
        pe_attend(e, att["fox"])
        pe_out(e, "out3", "x3_lo", lambda t: pe_to_xt(e, "x3", lambda t: v3[:, t, :], lambda t: at("fox_ofree", 66), t),
               turn("n8"), {1: (0,), 2: (1,)})
        pe_up(e, "up3", "n8", turn("n8"))
        pe_down(e, "down3", "up3", None, {})


    def small_loads(e):
        full = sem("small_full")
        ld = lambda dst, src: e.dma_start(dst, src).then_inc(full, 16)
        ld(c_raw[:, 0:3, :], A["conv_w"][0].rearrange("w (t p) -> t w p", p=P))
        ld(c_raw[:, 3, :], A["conv_b"][0].rearrange("(t p) -> t p", p=P))
        ld(pe_raw[:, :, :], A["cmp_pos"][0].rearrange("k (s r) d -> s k (r d)", r=2))
        ld(rope_c[:, :, :], A["rope_cos"].rearrange("(t p) d -> p t d", p=P))
        ld(rope_s[:, :, :], A["rope_sin"].rearrange("(t p) d -> p t d", p=P))
        with nc.allow_non_contiguous_dma(reason="512 positions"):
            ld(pos_i[:, :], A["positions_2"][0].rearrange("(t p) -> p t", p=P))
        for dst, src in ((inv_f, A["inv_freq"]), (sink, A["swa_sinks"][0]), (g_qa, A["l0_mla_q_a_norm_2"]),
                         (g_kva, A["l0_mla_kv_a_norm_2"]), (g_mq, A["l0_mla_q_norm_2"]),
                         (g_mk, A["l0_mla_k_norm_2"]), (f_bias, A["l1_fox_f_bias_2"])):
            ld(dst[:, :], src.partition_broadcast(P))
        e.wait_ge(sem("consts"), 17)
        with nc.allow_non_contiguous_dma(reason="64 gains each"):
            for i, src in enumerate((A["l0_mla_q_norm_2"], A["l0_mla_k_norm_2"], A["l1_fox_q_norm_2"],
                                     A["l1_fox_k_norm_2"])):
                ld(g_col[0:HD, i:i + 1], src[0:HD].rearrange("(p o) -> p o", o=1))
        ld(w2_sb[:, :, :, :].rearrange("p k x d -> p (k x) d"),
           A["cmp_w2"][0].rearrange("k (x p) d -> p (k x) d", p=P))

    def act_rstd(e, od, name, k, n, a=0):
        e.wait_ge(*at(f"{name}_var", k))
        e.activation(sq_a[:, a:a + n], var[:, a:a + n], ACT.Ln).then_inc(*od.own())
        e.wait_ge(*od.latest())
        e.activation(rstd[:, a:a + n], sq_a[:, a:a + n], ACT.Exp, scale=-0.5).then_inc(*od.done(*at(f"{name}_y", k)))

    def act_square(e, od, src, n, column, sq, value):
        if od.newest:
            e.wait_ge(*od.latest())
        e.activation(dump[:, 0:n], src, ACT.Square, accum_out=ss[:, column:column + 1]).then_inc(
            *od.done(*at(sq, value)))

    def act_high(e, od, name, t):
        for i in (2 * t, 2 * t + 1):
            q = i % 2
            e.wait_ge(*at(f"{name}_tp", i + 1))
            e.activation(xt_hi[:, 4 * q:4 * q + 4, t * P:(t + 1) * P],
                         bank(turn_bank(name, i)).rearrange("p (k s) -> p k s", k=4), ACT.Copy).then_inc(
                *od.done(*at(f"{name}_hi", i + 1)))

    def act_norm(e, od, name, src, parts, ready, lag):
        for t in range(NT):
            for x in range(parts):
                e.wait_ge(*ready(t, x))
                act_square(e, od, src(t)[:, x * D // parts:(x + 1) * D // parts], D // parts, 2 * t + x,
                           f"{name}_sq", parts * t + x + 1)
            if t >= lag:
                act_high(e, od, name, t - lag)
            act_rstd(e, od, name, t + 1, parts, 2 * t)
        for t in range(NT - lag, NT):
            act_high(e, od, name, t)

    def out_half(name, c, t):
        return bank(out_bank(name, c, t))

    def out_done(e, name, c, t):
        phase = phases[name]
        tile_done(e, name, c, t, 4 * (phase.g0 + phase.groups // 2 * (c + 1)))

    def act_out(e, od, name, norm, lag):
        post = name in POSTS
        for t in range(NT):
            if post:
                out_done(e, name, 0, t)
                act_square(e, od, out_half(name, 0, t), W, 8 + 2 * t, f"{name}_sq", t + 1)
            elif norm:
                e.wait_ge(*at(f"{name}_res", t + 1))
                act_square(e, od, h[:, t, 0:W], W, 2 * t, f"{norm}_sq", t + 1)
        for t in range(NT if norm else 0):
            if post:
                out_done(e, name, 1, t)
                act_square(e, od, out_half(name, 1, t), W, 9 + 2 * t, f"{name}_sq", NT + t + 1)
                act_rstd(e, od, name, t + 1, 1, 8 + 2 * t)
                e.wait_ge(*at(f"{name}_res", t + 1))
                act_square(e, od, h[:, t, :], D, 2 * t, f"{norm}_sq", t + 1)
            else:
                e.wait_ge(*at(f"{name}_res", NT + t + 1))
                act_square(e, od, h[:, t, W:D], W, 2 * t + 1, f"{norm}_sq", NT + t + 1)
            if t >= lag:
                act_high(e, od, norm, t - lag)
            act_rstd(e, od, norm, t + 1, 1, 2 * t)
        for t in range(NT - lag, NT) if norm else ():
            act_high(e, od, norm, t)

    def act_turned(e, od, name, plan, c):
        for i, (cc, (off, w, dst, kind), _, count) in enumerate(plan):
            if cc != c or kind == "d":
                continue
            e.wait_ge(*at(f"{name}_tp", i + 1))
            if kind == "s":
                e.activation(dst[0], bank(ODD[i % 4]), ACT.Copy).then_inc(*od.done(*at(f"{name}_tph", i + 1)))
            else:
                dst, scale = dst
                src = bank(ODD[i % 4], W, 0, w)
                if scale is None:
                    e.activation(dst, src, ACT.Copy).then_inc(*od.done(*at(f"{name}_tpa", count)))
                else:
                    e.activation(dst, src, ACT.Copy, scale=scale).then_inc(*od.done(*at(f"{name}_tpa", count)))

    def act_head_squares(e, od, name, nth, t, rows):
        i = 4 * nth + t
        if i >= 2:
            e.wait_ge(*at(f"{name}_red", i - 1))
        e.wait_ge(*od.latest())
        n = rows.shape[1] * (rows.shape[2] if len(rows.shape) == 3 else 1)
        s = scratch[:, t % 2, 0:n]
        if len(rows.shape) == 3:
            s = s.rearrange("p (h d) -> p h d", d=rows.shape[2])
        e.activation(s, rows, ACT.Square).then_inc(*od.done(*at(f"{name}_sqs", i + 1)))

    def act_copies(e, od, name, c, ends, copy, plan, uses_tok):
        for t in range(NT):
            tile_done(e, name, c, t, ends)
            if t == 0 and c == 0:
                e.wait_ge(*at({"in1": "n0", "in2": "n5", "in3": "n7"}[name] + "_tp", 2 * NT))
            if t == 0 and uses_tok:
                before = sum(p[0] < c for p in plan)
                if before:
                    e.wait_ge(*at(f"{name}_tp", before))
            copy(t)

    def act_up(e, od, name, conv_layer):
        g0 = phases[name].g0

        def chunk(gi, even):
            first = isinstance(gi, int) and gi == 0
            for j in range(4):
                if j == 3:
                    e.wait_ge(slab_used, 4 * (gi + g0) + 4)
                elif conv_layer or j < 2:
                    e.wait_ge(*at(f"{name}_acc", 3 * gi + (j + 1)))
                if conv_layer:
                    tile = 2 * gi + (j % 2 + (j // 2) * KF)
                    tap = (lambda w: conv[:, w, tile:tile + 1]) if isinstance(gi, int) else \
                        (lambda w: conv[:, w, bass.ds(tile, 1)])
                    scale, bias = tap(2), tap(3)
                    if not first:
                        wait_apart(e, *at(f"{name}_lo", 2 * gi + (j % 2 - 1)))
                    e.activation(half_u[:, 2 * (j % 2) + j // 2, :], bank((ODD, EVEN)[even][j]), ACT.Identity,
                                 scale=scale, bias=bias).then_inc(*od.done(*at(f"{name}_s", 4 * gi + (j + 1))))
                elif j < 2:
                    e.activation(half_u[:, 2 * j, :], bank((ODD, EVEN)[even][j]), ACT.Silu).then_inc(
                        *od.done(*at(f"{name}_s", 2 * gi + (j + 1))))
            if conv_layer:
                for k in range(2):
                    e.wait_ge(*at(f"{name}_c", 4 * gi + (k + 1)))
                    e.activation(half_u[:, 2 * k, :], half_u[:, 2 * k, :], ACT.Gelu_apprx_tanh).then_inc(
                        *od.done(*at(f"{name}_g", 2 * gi + (k + 1))))
            for k in range(2):
                src = half_u[:, 2 * k + (0 if conv_layer else 1), :]
                high = hid_tile(hid_hi, 2 * gi + k)
                wait_apart(e, *at(f"{name}_h", 2 * gi + (k + 1)))
                e.activation(high, src, ACT.Copy).then_inc(*od.done(*at(f"{name}_hi", 2 * gi + (k + 1))))

        e.preload_act_table(ACT.Gelu_apprx_tanh if conv_layer else ACT.Silu)
        chunk(0, 1)
        with e.Fori(0, 5) as j:
            chunk(2 * j + 1, 0)
            chunk(2 * j + 2, 1)
        e.preload_act_table_set(EXP_LN)

    def hid_tile(t, i):
        return t[:, i, :] if isinstance(i, int) else t[:, bass.ds(i, 1), :].rearrange("p a s -> p (a s)")

    def column(t, hd):
        return t[:, hd:hd + 1] if isinstance(hd, int) else t[:, bass.ds(hd, 1)]

    def steps(e, od, cfg, before, body, per):
        before()
        iters = cfg["iters"]
        with e.Fori(0, iters - 1) as j:
            od.enter(j, per)
            body(j, False)
        od.leave(iters - 1, per)
        body(iters - 1, True)

    def act_attend(e, od, cfg):
        name = cfg["name"]

        def probs(j, k):
            k0, k1 = span(cfg, 3 - k % 4)
            n = (k1 - k0) * P
            c, slot = k % 8, k % 4
            if cfg["band"]:
                its_sink = column(sink, 2 * j + k // 4)
                wait_apart(e, *at(f"{name}_nm", 8 * j + (k + 1)))
                e.activation(esink[:, c:c + 1], its_sink, ACT.Exp, bias=nmax[:, c:c + 1]).then_inc(*od.own())
            else:
                e.wait_ge(*at(f"{name}_nm", 8 * j + (k + 1)))
            e.activation(prob[:, slot, 0:n], bank(slot, n), ACT.Exp, bias=nmax[:, c:c + 1],
                         accum_out=den[:, c:c + 1]).then_inc(*od.done(*at(f"{name}_p", 8 * j + (k + 1))))

        def body(j, last):
            for k in range(1, 9):
                ahead(turned, j, k, last)
                ahead(probs, j, k + 3, last)

        def turned(j, k):
            k0, k1 = span(cfg, 3 - k % 4)
            n = (k1 - k0) * P
            e.wait_ge(*at(f"{name}_tp", 8 * j + (k + 1)))
            e.wait_ge(*at(f"{name}_pv", 8 * j + (k + 1)))
            e.activation(prob_t[:, k % 2, 0:n], bank(4 + k % 2, n), ACT.Copy).then_inc(
                *od.done(*at(f"{name}_pt", 8 * j + (k + 1))))

        steps(e, od, cfg, lambda: (probs(0, 0), probs(0, 1), probs(0, 2), turned(0, 0), probs(0, 3)), body,
              8 if cfg["band"] else 0)

    def act_stick(e, od, cfg):
        name = cfg["name"]

        def logs(j, k):
            n = (4 - k % 4) * P
            e.wait_ge(*at(f"{name}_qk", 8 * j + (k + 1)))
            a = sb_ln[:, k % 4, 0:n]
            e.activation(a, bank(k % 4, n), ACT.Abs).then_inc(*od.own())
            e.wait_ge(*od.latest())
            e.activation(a, a, ACT.Exp, scale=-1.0).then_inc(*od.own())
            e.wait_ge(*od.latest())
            e.activation(a, a, ACT.Ln, bias=1.0).then_inc(*od.done(*at(f"{name}_ln", 8 * j + (k + 1))))

        def probs(j, k):
            n = (4 - k % 4) * P
            e.wait_ge(*at(f"{name}_w", 8 * j + (k + 1)))
            a = prob[:, k % 4, 0:n]
            e.activation(a, a, ACT.Exp).then_inc(*od.done(*at(f"{name}_p", 8 * j + (k + 1))))

        def fin(j, k):
            o = cfg["v"](2 * j + k // 4)(3 - k % 4)
            wait_apart(e, *at(f"{name}_pv", 8 * j + (k + 3)))
            e.activation(o, bank(6 + k % 2, HD), ACT.Copy).then_inc(*od.done(*at(f"{name}_ofree", 8 * j + (k + 3))))

        def body(j, last):
            for k in range(1, 9):
                ahead(logs, j, k + 3, last)
                ahead(probs, j, k + 2, last)
                fin(j, k - 1)

        def before():
            e.sem_inc(*at(f"{name}_ofree", 2))
            for k in range(3):
                logs(0, k)
            probs(0, 0)
            probs(0, 1)
            logs(0, 3)
            probs(0, 2)

        steps(e, od, cfg, before, body, 16)

    @block.scalar
    def _(e):
        od = Order(sem("act_own"))
        e.preload_act_table_set(EXP_LN)
        act_norm(e, od, "n0", lambda t: h[:, t, :], 1, lambda t, x: at(f"h_full{t}", 16), 1)
        small_loads(e)
        for k in range(2):
            e.wait_ge(*at("angle", k + 1))
            halves = ((-1.0, 0), (1.0, 1)) if k == 0 else ((1.0, 0), (1.0, 1))
            dst = (m_sin, m_cos)[k]
            for sign, x in halves:
                op = e.activation(dst[:, :, 16 * x:16 * x + 16], red[:, :, :], ACT.Sin, scale=sign)
                if x:
                    op.then_inc(*od.done(*at("angle_out", k + 1)))
                else:
                    op.then_inc(*od.own())
        e.preload_act_table_set(EXP_LN)

        plan = t_plan(T_IN1)
        g0 = phases["in1"].g0

        def copy1(c):
            cp = sem("in1_copy")

            def put(t):
                last = 4 * c + t + 1
                if c in (0, 3):
                    e.activation(tok3[:, t, 0:W], bank(EVEN[t]), ACT.Copy, scale=0.125).then_inc(*od.done(cp, last))
                elif c == 1:
                    e.activation(tok3[:, t, 0:384], bank(EVEN[t], 384), ACT.Copy).then_inc(*od.own())
                    e.activation(v1[:, t, 0:P], bank(EVEN[t], P, 384), ACT.Copy).then_inc(*od.done(cp, last))
                else:
                    e.activation(tok3[:, t, 0:P], bank(EVEN[t], P), ACT.Copy).then_inc(*od.own())
                    if c == 2:
                        e.activation(gate[:, t, :], bank(EVEN[t], 24, 256), ACT.Exp, scale=-1.0).then_inc(*od.own())
                    v_at = P if c == 2 else 2 * P
                    e.activation(v1[:, t, v_at:v_at + P], bank(EVEN[t], P, P), ACT.Copy).then_inc(*od.done(cp, last))
            return put

        for c in range(5):
            act_copies(e, od, "in1", c, 4 * (g0 + c + 1), copy1(c), plan, True)
            act_turned(e, od, "in1", plan, c)
        for kv in range(2):
            e.wait_ge(*at("cmp_raw", kv + 1))
            e.activation(f_hi[:, kv, :, :], f_raw[:, kv, :, :], ACT.Copy).then_inc(*od.done(*at("cmp_fh", kv + 1)))
        for kv in range(2):
            e.wait_ge(slab_used, 4 * (phases["cmp"].g0 + kv + 1))
            e.activation(chid[0:62, kv, :], bank(kv, 256, 0, 62), ACT.Gelu_apprx_tanh).then_inc(
                *od.done(*at("cmp_gelu", kv + 1)))
        e.preload_act_table_set(EXP_LN)
        for i in range(2):
            e.wait_ge(*at("cat_e", i + 1))
            a = cat_e[:, 2 * i:2 * i + 2, :]
            e.activation(a, a, ACT.Exp).then_inc(*od.done(*at("cat_x", i + 1)))
        for i in range(2):
            e.wait_ge(*at("cat_tp", i + 1))
            e.activation(cat_t[:, 2 * i:2 * i + 2, :].rearrange("p a b -> p (a b)"), bank(6 + i), ACT.Copy).then_inc(
                *od.done(*at("cat_pt", i + 1)))
        act_attend(e, od, att["nsa"])
        act_attend(e, od, att["swa"])
        act_norm(e, od, "n1", lambda t: o1[:, t, :], 2, lambda t, x: at("swa_ofree", 34), 1)
        act_out(e, od, "out1", "n3", 1)
        act_up(e, od, "up1", True)
        act_out(e, od, "down1", "n5", 1)

        plan = t_plan(T_IN2)
        g2 = phases["in2"].g0

        def copy2(c):
            cp = sem("in2_copy")

            def put(t):
                last = 4 * c + t + 1
                if c == 0:
                    e.activation(tok3[:, t, 0:384], bank(EVEN[t], 384), ACT.Copy).then_inc(*od.own())
                    e.activation(k_rope[:, t, :], bank(EVEN[t], ROPE, 384), ACT.Copy).then_inc(*od.own())
                    if t:
                        e.wait_ge(*od.latest())
                    e.activation(dump[:, 0:QR], bank(EVEN[t], QR), ACT.Square, accum_out=ss[:, t:t + 1]).then_inc(
                        *od.own())
                    e.activation(dump[:, QR:QR + KVR], bank(EVEN[t], KVR, QR), ACT.Square,
                                 accum_out=ss[:, 4 + t:5 + t]).then_inc(*od.done(cp, last))
                elif c in (SQ, SK):
                    e.activation(tok3[:, t, 0:W], bank(EVEN[t]), ACT.Copy, scale=0.125 if c == SQ else 1.0).then_inc(
                        *od.done(cp, last))
                elif c == SV:
                    e.activation(v2[:, t, W:D], bank(EVEN[t]), ACT.Copy).then_inc(*od.done(cp, last))
                elif c in (Q0, Q1):
                    e.activation(tok3[:, t, 0:384], bank(EVEN[t], 384), ACT.Copy).then_inc(*od.done(cp, last))
                    act_head_squares(e, od, "in2", HEAD_CHUNKS[c], t, tok3[:, t, 0:384])
                else:
                    rows = staged("in2", c)[:, t, 0:384].rearrange("p (h d) -> p h d", d=MQK)
                    kv = bank(EVEN[t]).rearrange("p (h d) -> p h d", d=P)
                    e.activation(rows[:, :, 0:HD], kv[:, :, 0:HD], ACT.Copy).then_inc(*od.own())
                    e.activation(rows[:, :, HD:MQK], k_rope[:, t, :].unsqueeze(1).broadcast_to([P, 4, ROPE]),
                                 ACT.Copy).then_inc(*od.own())
                    a = (c == K1) * 4 * HD
                    e.activation(v2[:, t, a:a + 4 * HD].rearrange("p (h d) -> p h d", d=HD), kv[:, :, HD:P],
                                 ACT.Copy).then_inc(*od.done(cp, last))
                    act_head_squares(e, od, "in2", HEAD_CHUNKS[c], t, staged("in2", c)[:, t, 0:384])
            return put

        ends = [4 * g2 + s0 + slabs for _, s0, slabs, _ in IN2]
        for c in range(8):
            act_copies(e, od, "in2", c, ends[c], copy2(c), plan, c not in (K0, SV))
            if c == CQ or c in HEAD_CHUNKS:
                act_rstd(e, od, "in2", 1 if c == CQ else HEAD_CHUNKS[c] + 2, 8 if c == CQ else 16)
            for x in {Q1: (), K0: (Q1, K0), SV: ()}.get(c, (c,)):
                act_turned(e, od, "in2", plan, x)
        act_attend(e, od, att["att2"])
        act_stick(e, od, att["stk"])
        for t in range(NT):
            act_high(e, od, "x2", t)
        act_out(e, od, "out2", "n6", 1)
        act_up(e, od, "up2", False)
        act_out(e, od, "down2", "n7", 1)

        plan = t_plan(T_IN3)
        g3 = phases["in3"].g0

        def copy3(c):
            cp = sem("in3_copy")

            def put(t):
                last = 4 * wide("in3", c) + t + 1
                if c < 5:
                    rows = tok3[:, t, :].rearrange("p (h d) -> p h d", d=66)[:, :, 0:HD]
                    e.activation(rows, bank(EVEN[t]).rearrange("p (h d) -> p h d", d=HD), ACT.Copy).then_inc(
                        *od.done(cp, last))
                    act_head_squares(e, od, "in3", FOX_CHUNKS[c], t, rows)
                else:
                    e.activation(v3[:, t, (c - 5) * W:(c - 4) * W], bank(EVEN[t]), ACT.Copy).then_inc(*od.done(cp, last))
            return put

        for c in range(7):
            if c == 1:
                continue
            act_copies(e, od, "in3", c, 4 * (g3 + c + 1), copy3(c), plan, c < 5)
            if c == 0:
                e.wait_ge(slab_used, 4 * (g3 + 2))
                e.activation(logit_t[:, :], bank(EVEN[0], SEQ, 0, 16), ACT.Copy).then_inc(
                    *od.done(*at("fox_logits", 1)))
                e.wait_ge(*at("fox_abs", 1))
                a = logf[:, :, :]
                e.activation(a, a, ACT.Exp, scale=-1.0).then_inc(*od.own())
                e.wait_ge(*od.latest())
                e.activation(a, a, ACT.Ln, bias=1.0).then_inc(*od.done(*at("fox_ln", 1)))
            if c in FOX_CHUNKS:
                act_rstd(e, od, "in3", FOX_CHUNKS[c] + 1, 32)
            act_turned(e, od, "in3", plan, c)
        act_attend(e, od, att["fox"])
        for t in range(NT):
            act_high(e, od, "x3", t)
        act_out(e, od, "out3", "n8", 1)
        act_up(e, od, "up3", False)

    def dve_refine(e, od, name, k, n, a=0):
        r, v, q = rstd[:, a:a + n], var[:, a:a + n], sq_a[:, a:a + n]
        e.wait_ge(*at(f"{name}_y", k))
        e.tensor_tensor(q, r, r, ALU.mult).then_inc(*od.own())
        e.wait_ge(*od.latest())
        e.scalar_tensor_tensor(out=q, in0=q, scalar=-0.5, in1=v, op0=ALU.mult, op1=ALU.mult).then_inc(*od.own())
        e.wait_ge(*od.latest())
        e.scalar_tensor_tensor(out=r, in0=q, scalar=1.5, in1=r, op0=ALU.add, op1=ALU.mult).then_inc(*od.own())
        e.wait_ge(*od.latest())

    def dve_rstd(e, od, name, k, n, count, a=0):
        e.tensor_scalar(var[:, a:a + n], ss[:, a:a + n], 1.0 / count, EPS, ALU.mult, ALU.add).then_inc(
            *od.done(*at(f"{name}_var", k)))
        dve_refine(e, od, name, k, n, a)

    def dve_low(e, od, name, t):
        for i in (2 * t, 2 * t + 1):
            q = i % 2
            e.wait_ge(*at(f"{name}_hi", i + 1))
            hi = xt_hi[:, 4 * q:4 * q + 4, t * P:(t + 1) * P].bitcast(F32)
            e.tensor_tensor(xt_lo[:, 4 * q:4 * q + 4, t * P:(t + 1) * P],
                            bank(turn_bank(name, i)).rearrange("p (k s) -> p k s", k=4), hi, ALU.subtract).then_inc(
                *od.done(*at(f"{name}_lo", i + 1)))

    def dve_norm_tile(e, od, name, gain, src, parts, t, lag):
        a = 2 * t
        if t >= lag:
            dve_low(e, od, name, t - lag)
        if parts == 2:
            e.wait_ge(*at(f"{name}_sq", 2 * t + 2))
            dve_rstd(e, od, name, t + 1, 2, D // 2, a)
        else:
            e.wait_ge(*at(f"{name}_sq", t + 1 if name in WHOLE else NT + t + 1))
            if name not in WHOLE:
                e.tensor_tensor(ss[:, a:a + 1], ss[:, a:a + 1], ss[:, a + 1:a + 2], ALU.add).then_inc(*od.own())
                e.wait_ge(*od.latest())
            dve_rstd(e, od, name, t + 1, 1, D, a)
        if t == 0:
            gain_ready(e, gain)
        if t >= 2:
            e.wait_ge(*at(f"{name}_tp", 2 * t - 2))
        for x in range(parts):
            cs = slice(x * D // parts, (x + 1) * D // parts)
            e.scalar_tensor_tensor(out=xn[:, t % 2, cs], in0=src[:, cs], scalar=rstd[:, a + x:a + x + 1],
                                   in1=gains[:, gain % 2, cs], op0=ALU.mult, op1=ALU.mult).then_inc(
                *(od.done(*at(f"{name}_xn", t + 1)) if x == parts - 1 else od.own()))

    def dve_norm(e, od, name, gain, src, parts, lag):
        for t in range(NT):
            dve_norm_tile(e, od, name, gain, src(t), parts, t, lag)
        for t in range(NT - lag, NT):
            dve_low(e, od, name, t)

    def dve_out(e, od, name, post_gain, norm, gain, lag):
        y = scratch[:, :, :]
        if name not in POSTS:
            for t in range(NT):
                out_done(e, name, 0, t)
                e.tensor_tensor(h[:, t, 0:W], out_half(name, 0, t), h[:, t, 0:W], ALU.add).then_inc(
                    *od.done(*at(f"{name}_res", t + 1)))
        for t in range(NT):
            if name in POSTS:
                a = 8 + 2 * t
                e.wait_ge(*at(f"{name}_sq", NT + t + 1))
                e.tensor_tensor(ss[:, a:a + 1], ss[:, a:a + 1], ss[:, a + 1:a + 2], ALU.add).then_inc(*od.own())
                e.wait_ge(*od.latest())
                dve_rstd(e, od, name, t + 1, 1, D, a)
                if t == 0:
                    gain_ready(e, post_gain)
                for c in range(2):
                    e.scalar_tensor_tensor(out=y[:, c, :], in0=out_half(name, c, t), scalar=rstd[:, a:a + 1],
                                           in1=gains[:, post_gain % 2, c * W:(c + 1) * W], op0=ALU.mult,
                                           op1=ALU.mult).then_inc(*od.own())
                e.wait_ge(*od.latest())
                e.tensor_tensor(h[:, t, :], h[:, t, :], y.rearrange("p a b -> p (a b)"), ALU.add).then_inc(
                    *od.done(*at(f"{name}_res", t + 1)))
            else:
                out_done(e, name, 1, t)
                e.tensor_tensor(h[:, t, W:D], out_half(name, 1, t), h[:, t, W:D], ALU.add).then_inc(
                    *od.done(*at(f"{name}_res", NT + t + 1)))
            if norm:
                dve_norm_tile(e, od, norm, gain, h[:, t, :], 1, t, lag)
        for t in range(NT - lag, NT) if norm else ():
            dve_low(e, od, norm, t)

    def dve_turned(e, od, name, plan, c):
        for i, (cc, (off, w, dst, kind), _, count) in enumerate(plan):
            if cc != c or kind == "a":
                continue
            if kind == "s":
                e.wait_ge(*at(f"{name}_tph", i + 1))
                e.tensor_tensor(dst[1], bank(ODD[i % 4]), dst[0].bitcast(F32), ALU.subtract).then_inc(
                    *od.done(*at(f"{name}_tpd", count)))
            else:
                e.wait_ge(*at(f"{name}_tp", i + 1))
                dst, scale = dst
                src = bank(ODD[i % 4], W, 0, w)
                if scale is None:
                    e.tensor_copy(dst, src).then_inc(*od.done(*at(f"{name}_tpd", count)))
                else:
                    e.tensor_scalar(dst, src, scale, None, ALU.mult).then_inc(*od.done(*at(f"{name}_tpd", count)))

    def swapped_halves(e, od, x, nh, half, cos, sin, room, done):
        v = x if len(x.shape) == 3 else x.rearrange("p (h d) -> p h d", h=nh)
        v4 = v.rearrange("p h (a b) -> p h a b", a=2)
        s = room[:, 0:nh * 2 * half].rearrange("p (h d) -> p h d", h=nh)
        s4 = s.rearrange("p h (a b) -> p h a b", a=2)
        sn = sin.rearrange("p (a b) -> p a b", a=2).unsqueeze(1).broadcast_to([P, nh, 2, half])
        e.tensor_tensor(s4, v4[:, :, ::-1, :], sn, ALU.mult).then_inc(*od.own())
        e.wait_ge(*od.latest())
        e.tensor_tensor(v, v, cos.unsqueeze(1).broadcast_to([P, nh, 2 * half]), ALU.mult).then_inc(*od.own())
        e.wait_ge(*od.latest())
        e.tensor_tensor(v, v, s, ALU.add).then_inc(*done())

    def head_norms(e, od, name, c, nth, k, nh, dh, stride, after, between=None):
        def view(t):
            return staged(name, c)[:, t, 0:nh * stride].rearrange("p (h d) -> p h d", d=stride)[:, :, 0:dh]
        for t in range(NT):
            i = 4 * nth + t
            e.wait_ge(*at(f"{name}_sqs", i + 1))
            s = scratch[:, t % 2, 0:nh * dh].rearrange("p (h d) -> p h d", h=nh)
            e.tensor_reduce(ss[:, nh * t:nh * (t + 1)], s, AX.X, ALU.add).then_inc(*od.done(*at(f"{name}_red", i + 1)))
        if between:
            between()
        e.wait_ge(*od.latest())
        dve_rstd(e, od, name, k, nh * NT, dh)
        for t in range(NT):
            r = rstd[:, nh * t:nh * (t + 1)].unsqueeze(2).broadcast_to([P, nh, dh])
            e.tensor_tensor(view(t), view(t), r, ALU.mult).then_inc(*od.own())
            e.wait_ge(*od.latest())
            after(t, view(t))

    def dve_up(e, od, name, conv_layer):
        g0 = phases[name].g0
        per = 4 if conv_layer else 0

        def chunk(gi, even):
            if conv_layer:
                for j in range(4):
                    tile = 2 * gi + (j % 2 + (j // 2) * KF)
                    tap = (lambda w: conv[:, w, tile:tile + 1]) if isinstance(gi, int) else \
                        (lambda w: conv[:, w, bass.ds(tile, 1)])
                    y = half_u[:, 2 * (j % 2) + j // 2, :]
                    e.wait_ge(*at(f"{name}_s", 4 * gi + (j + 1)))
                    e.scalar_tensor_tensor(out=y[:, 1:], in0=bank((ODD, EVEN)[even][j], W - 1), scalar=tap(1),
                                           in1=y[:, 1:], op0=ALU.mult, op1=ALU.add).then_inc(*od.own())
                    e.wait_ge(*od.latest())
                    e.scalar_tensor_tensor(out=y[:, 2:], in0=bank((ODD, EVEN)[even][j], W - 2), scalar=tap(0),
                                           in1=y[:, 2:], op0=ALU.mult, op1=ALU.add).then_inc(
                        *od.done(*at(f"{name}_c", 4 * gi + (j + 1))))
                e.wait_ge(*od.latest())
                for k in range(2):
                    e.wait_ge(*at(f"{name}_g", 2 * gi + (k + 1)))
                    e.tensor_tensor(half_u[:, 2 * k, :], half_u[:, 2 * k, :], half_u[:, 2 * k + 1, :],
                                    ALU.mult).then_inc(*od.done(*at(f"{name}_h", 2 * gi + (k + 1))))
            else:
                for k in range(2):
                    e.wait_ge(*at(f"{name}_s", 2 * gi + (k + 1)))
                    if not (isinstance(gi, int) and gi == 0):
                        e.wait_ge(*at(f"{name}_lo", 2 * gi + (k - 1)))
                    if k == 1:
                        e.wait_ge(slab_used, 4 * (gi + g0) + 4)
                    else:
                        e.wait_ge(*at(f"{name}_acc", 3 * gi + 3))
                    e.tensor_tensor(half_u[:, 2 * k + 1, :], bank((ODD, EVEN)[even][2 + k]), half_u[:, 2 * k, :],
                                    ALU.mult).then_inc(*od.done(*at(f"{name}_h", 2 * gi + (k + 1))))
            for k in range(2):
                e.wait_ge(*at(f"{name}_hi", 2 * gi + (k + 1)))
                src = half_u[:, 2 * k + (0 if conv_layer else 1), :]
                e.tensor_tensor(hid_tile(hid_lo, 2 * gi + k), src,
                                hid_tile(hid_hi, 2 * gi + k).bitcast(F32), ALU.subtract).then_inc(
                    *od.done(*at(f"{name}_lo", 2 * gi + (k + 1))))

        chunk(0, 1)
        with e.Fori(0, 5) as j:
            od.enter(j, 2 * per)
            chunk(2 * j + 1, 0)
            chunk(2 * j + 2, 1)
        od.leave(5, 2 * per)
        od.newest = at(f"{name}_lo", 22)

    def dve_attend(e, od, cfg, fin_steps, per):
        name = cfg["name"]

        def maxima(j, k):
            k0, k1 = span(cfg, 3 - k % 4)
            c = k % 8
            e.wait_ge(*at(f"{name}_qk", 8 * j + (k + 1)))
            op = e.tensor_reduce(nmax[:, c:c + 1], bank(k % 4, (k1 - k0) * P), AX.X, ALU.max, negate=True)
            if cfg["band"]:
                op.then_inc(*od.own())
                e.wait_ge(*od.latest())
                op = e.tensor_tensor(nmax[:, c:c + 1], nmax[:, c:c + 1], column(neg_sink, 2 * j + k // 4), ALU.min)
            op.then_inc(*od.done(*at(f"{name}_nm", 8 * j + (k + 1))))

        def body(j, last):
            for k in range(1, 9):
                ahead(maxima, j, k + 3, last)
                fin(j, k - 1)

        def fin(j, k):
            e.wait_ge(*at(f"{name}_pv", 8 * j + (k + 3)))
            c = k % 8
            r = rg[:, k % 2:k % 2 + 1]
            if cfg["band"]:
                e.tensor_tensor(r, den[:, c:c + 1], esink[:, c:c + 1], ALU.add).then_inc(*od.own())
                e.wait_ge(*od.latest())
                e.reciprocal(r, r).then_inc(*od.own())
            else:
                e.reciprocal(r, den[:, c:c + 1]).then_inc(*od.own())
            e.wait_ge(*od.latest())
            fin_steps(j, k, r, *at(f"{name}_ofree", 8 * j + (k + 3)))

        def before():
            e.sem_inc(*at(f"{name}_ofree", 2))
            for k in range(4):
                maxima(0, k)

        steps(e, od, cfg, before, body, per)

    def dve_stick(e, od, cfg):
        name = cfg["name"]

        def weights(j, k):
            n = (4 - k % 4) * P
            e.wait_ge(*at(f"{name}_ln", 8 * j + (k + 1)))
            sp, r, z = sb_ln[:, k % 4, 0:n], prob[:, k % 4, 0:n], bank(k % 4, n)
            e.scalar_tensor_tensor(out=sp, in0=z, scalar=0.0, in1=sp, op0=ALU.max, op1=ALU.add).then_inc(*od.own())
            e.wait_ge(*od.latest())
            e.tensor_tensor_scan(r[:, ::-1], one[:, 0:1].broadcast_to([P, n]), sp[:, ::-1], 0.0,
                                 ALU.mult, ALU.add).then_inc(*od.own())
            e.wait_ge(*od.latest())
            e.tensor_tensor(r, z, r, ALU.subtract).then_inc(*od.done(*at(f"{name}_w", 8 * j + (k + 1))))

        def body(j, last):
            for k in range(1, 9):
                ahead(weights, j, k + 2, last)
                ahead(turned, j, k, last)

        def turned(j, k):
            n = (4 - k % 4) * P
            e.wait_ge(*at(f"{name}_tp", 8 * j + (k + 1)))
            e.wait_ge(*at(f"{name}_pv", 8 * j + (k + 1)))
            e.tensor_copy(prob_t[:, k % 2, 0:n], bank(4 + k % 2, n)).then_inc(
                *od.done(*at(f"{name}_pt", 8 * j + (k + 1))))

        steps(e, od, cfg, lambda: (weights(0, 0), weights(0, 1), weights(0, 2), turned(0, 0)), body, 16)

    @block.vector
    def _(e):
        od = Order(sem("dve_own"))
        e.sem_inc(sem("up1_h"), 2)
        dve_norm(e, od, "n0", 0, lambda t: h[:, t, :], 1, 1)
        e.wait_ge(*at("small_full", 16 * SMALLS))
        e.tensor_scalar(neg_sink[:, :], sink[:, :], -1.0, None, ALU.mult).then_inc(*od.own())
        e.tensor_scalar(g_col[0:HD, 2:3], g_col[0:HD, 2:3], 0.125, None, ALU.mult).then_inc(*od.own())
        e.tensor_scalar(g_col[0:HD, 0:1], g_col[0:HD, 0:1], MQK ** -0.5, None, ALU.mult).then_inc(*od.own())
        e.tensor_scalar(g_mq[:, :], g_mq[:, :], MQK ** -0.5, None, ALU.mult).then_inc(*od.own())
        e.tensor_copy(pos_f[:, :], pos_i[:, :]).then_inc(*od.own())
        e.wait_ge(*od.latest())
        for t in range(NT):
            e.tensor_scalar(ang[:, t, :], inv_f[:, :], pos_f[:, t:t + 1], None, ALU.mult).then_inc(*od.own())
        e.wait_ge(*od.latest())
        for k in range(2):
            e.tensor_scalar(turn[:, :, :], ang[:, :, :], 0.15915494309189535, 0.25 * k, ALU.mult, ALU.add).then_inc(
                *od.own())
            e.wait_ge(*od.latest())
            e.tensor_copy(turn_i[:, :, :], turn[:, :, :]).then_inc(*od.own())
            e.wait_ge(*od.latest())
            e.tensor_copy(turn[:, :, :], turn_i[:, :, :]).then_inc(*od.own())
            e.wait_ge(*od.latest())
            if k:
                e.wait_ge(*at("angle_out", 1))
            for part, src in ((TWO_PI_HI, ang), (TWO_PI_MID, red), (TWO_PI_LO, red)):
                e.scalar_tensor_tensor(out=red[:, :, :], in0=turn[:, :, :], scalar=-part, in1=src[:, :, :],
                                       op0=ALU.mult, op1=ALU.add).then_inc(*od.own())
                e.wait_ge(*od.latest())
            if k:
                e.tensor_scalar(red[:, :, :], red[:, :, :], 1.5707963267948966, None, ALU.add).then_inc(*od.own())
                e.wait_ge(*od.latest())
            e.tensor_scalar(red[:, :, :], red[:, :, :], PI, -PI, ALU.min, ALU.max).then_inc(
                *od.done(*at("angle", k + 1)))
        e.wait_ge(*at("angle_out", 2))
        for i, g in enumerate((g_mq, g_mk)):
            tail = g[:, HD:MQK]
            swapped = tail.rearrange("p (a b) -> p a b", a=2)[:, ::-1, :].unsqueeze(1).broadcast_to(
                [P, NT, 2, ROPE // 2])
            e.tensor_tensor(m_table[:, i, 0, :, :], m_cos[:, :, :], tail.unsqueeze(1).broadcast_to([P, NT, ROPE]),
                            ALU.mult).then_inc(*od.own())
            e.tensor_tensor(m_table[:, i, 1, :, :].rearrange("p t (a b) -> p t a b", a=2),
                            m_sin[:, :, :].rearrange("p t (a b) -> p t a b", a=2), swapped, ALU.mult).then_inc(*od.own())

        e.wait_ge(*at("pre_tp", 1))
        e.tensor_copy(conv[:, :, :].rearrange("p a b -> p (a b)"), bank(7, 8 * KF)).then_inc(*od.own())
        e.tensor_copy(pe_t[:, :, :, :].rearrange("p a b c -> p (a b c)"), bank(6, 4 * CMPS, 0, HD)).then_inc(
            *od.done(*at("pre_out", 1)))

        plan = t_plan(T_IN1)
        for c in range(5):
            for t in range(NT):
                e.wait_ge(*at("in1_copy", 4 * c + t + 1))
                pieces = {0: [(0, 8)], 1: [(0, 2), (256, 2)], 2: [(0, 2)], 3: [(0, 8)], 4: [(0, 2)]}[c]
                for x, (off, nh) in enumerate(pieces):
                    if x or t:
                        e.wait_ge(*od.latest())
                    done = (lambda: od.done(*at("in1_tok", 4 * c + t + 1))) if x == len(pieces) - 1 else od.own
                    swapped_halves(e, od, tok3[:, t, off:off + nh * HD], nh, HD // 2, rope_c[:, t, :],
                                   rope_s[:, t, :], scratch[:, 1, :], done)
            if c == 2:
                e.tensor_scalar(gate[:, :, :], gate[:, :, :], 1.0, None, ALU.add).then_inc(*od.own())
                e.wait_ge(*od.latest())
                e.reciprocal(gate[:, :, :], gate[:, :, :]).then_inc(*od.own())
            dve_turned(e, od, "in1", plan, c)

        e.wait_ge(*at("in1_tpa", 13))
        e.wait_ge(*at("in1_tpd", 13))
        for kv in range(2):
            for hd in range(2):
                src = (vct[:, hd, :] if kv else kt1[:, hd, :]).rearrange("d (c s) -> d c s", s=CMPS)
                for par in range(2):
                    for hf in range(2):
                        op = e.tensor_tensor(
                            f_raw[par * HD:(par + 1) * HD, kv, 8 * hf:8 * hf + 8, hd * NCB:(hd + 1) * NCB],
                            src[:, hf:hf + NCB, par::2].rearrange("d c s -> d s c"),
                            pe_t[:, kv, par, 8 * hf:8 * hf + 8].unsqueeze(2).broadcast_to([HD, 8, NCB]), ALU.add)
                        if hd and par and hf:
                            op.then_inc(*od.done(*at("cmp_raw", kv + 1)))
                        else:
                            op.then_inc(*od.own())
        for kv in range(2):
            e.wait_ge(*at("cmp_fh", kv + 1))
            e.tensor_tensor(f_lo[:, kv, :, :], f_raw[:, kv, :, :], f_hi[:, kv, :, :].bitcast(F32),
                            ALU.subtract).then_inc(*od.done(*at("cmp_f", kv + 1)))
        e.wait_ge(*at("cmp_tp", 2))
        e.tensor_copy(chid_t[:, :, :, :].rearrange("p a b c -> p (a b c)"), bank(2, 4 * 62)).then_inc(
            *od.done(*at("cmp_ht", 1)))
        e.wait_ge(*at("cmp_kv", 2))
        e.tensor_copy(kct[:, :, 0:NCB], bank(3, 62, 0, HD).rearrange("p (h c) -> p h c", h=2)).then_inc(*od.own())
        for gq in range(2):
            for x in range(4):
                op = e.tensor_copy(vbd[32 * x:32 * x + NCB, gq, HD * x:HD * (x + 1)], bank(gq, HD, 0, NCB))
                if gq and x == 3:
                    op.then_inc(*od.done(*at("cmp_out", 1)))
                else:
                    op.then_inc(*od.own())
        e.wait_ge(*at("cat_s", 1))
        halves = [cat_e[:, 2 * i:2 * i + 2, :].rearrange("p t (h c) -> p t h c", h=8) for i in range(2)]
        shape = [P, 2, 8, CMP]
        rows = [ss[:, 16 * i:16 * i + 16].rearrange("p (t h) -> p t h", t=2) for i in range(2)]
        sums = [var[:, 16 * i:16 * i + 16].rearrange("p (t h) -> p t h", t=2) for i in range(2)]
        for i, a in enumerate(halves):
            e.tensor_tensor(a, bank(4 + i).rearrange("p (t h c) -> p t h c", t=2, h=8),
                            c_add[:, 2 * i:2 * i + 2, :].unsqueeze(2).broadcast_to(shape), ALU.add).then_inc(*od.own())
            e.wait_ge(*od.latest())
            e.tensor_reduce(rows[i], a, AX.X, ALU.max).then_inc(*od.own())
            e.wait_ge(*od.latest())
            e.tensor_tensor(a, a, rows[i].unsqueeze(3).broadcast_to(shape), ALU.subtract).then_inc(
                *od.done(*at("cat_e", i + 1)))
        for i, a in enumerate(halves):
            e.wait_ge(*at("cat_x", i + 1))
            e.tensor_tensor(a, a, c_01[:, 2 * i:2 * i + 2, :].unsqueeze(2).broadcast_to(shape), ALU.mult).then_inc(
                *od.own())
            e.wait_ge(*od.latest())
            e.tensor_reduce(sums[i], a, AX.X, ALU.add).then_inc(*od.own())
            e.wait_ge(*od.latest())
            e.tensor_scalar(sums[i], sums[i], 1e-30, None, ALU.max).then_inc(*od.own())
            e.wait_ge(*od.latest())
            e.reciprocal(sums[i], sums[i]).then_inc(*od.own())
            e.wait_ge(*od.latest())
            e.tensor_tensor(a, a, sums[i].unsqueeze(3).broadcast_to(shape), ALU.mult).then_inc(
                *od.done(*at("cat_p", i + 1)))
        for i in range(NT):
            e.wait_ge(*at("cat_o", i + 1))
            g_c = gate[:, i, :].rearrange("p (h b) -> p h b", b=3)[:, :, 0:1].broadcast_to([P, 8, HD])
            e.tensor_tensor(o1[:, i, 0:W].rearrange("p (h d) -> p h d", d=HD),
                            bank(4 + i).rearrange("p (h d) -> p h d", d=HD), g_c, ALU.mult).then_inc(
                *od.done(*at("cat_fin", i + 1)))

        def fin_nsa(j, k, r, free, value):
            hd, i = 2 * j + k // 4, 3 - k % 4
            hq, branch = hd % 8, hd // 8 + 1
            e.tensor_tensor(r, r, column(gate[:, i, :], 3 * hq + branch), ALU.mult).then_inc(*od.own())
            e.wait_ge(*od.latest())
            o = columns(o1, hq)(i)
            e.scalar_tensor_tensor(out=o, in0=bank(6 + k % 2, HD), scalar=r, in1=o, op0=ALU.mult,
                                   op1=ALU.add).then_inc(*od.done(free, value))

        def fin_to(dst):
            def fin(j, k, r, free, value):
                e.tensor_scalar(dst(2 * j + k // 4)(3 - k % 4), bank(6 + k % 2, HD), r, None, ALU.mult).then_inc(
                    *od.done(free, value))
            return fin

        dve_attend(e, od, att["nsa"], fin_nsa, 16)
        dve_attend(e, od, att["swa"], fin_to(lambda hd: columns(o1, hd + 8)), 24)
        dve_norm(e, od, "n1", 1, lambda t: o1[:, t, :], 2, 1)
        dve_out(e, od, "out1", 2, "n3", 3, 1)
        dve_up(e, od, "up1", True)
        dve_out(e, od, "down1", 4, "n5", 5, 1)

        plan = t_plan(T_IN2)
        e.wait_ge(*at("in2_copy", 4))
        e.tensor_scalar(var[:, 0:4], ss[:, 0:4], 1.0 / QR, EPS, ALU.mult, ALU.add).then_inc(*od.own())
        e.tensor_scalar(var[:, 4:8], ss[:, 4:8], 1.0 / KVR, EPS, ALU.mult, ALU.add).then_inc(
            *od.done(*at("in2_var", 1)))
        dve_refine(e, od, "in2", 1, 8)
        for t in range(NT):
            for x, (a, n, gn) in enumerate(((0, QR, g_qa), (QR, KVR, g_kva))):
                v = tok3[:, t, a:a + n]
                op = e.scalar_tensor_tensor(out=v, in0=v, scalar=rstd[:, 4 * x + t:4 * x + t + 1], in1=gn[:, :],
                                            op0=ALU.mult, op1=ALU.mult)
                if x:
                    op.then_inc(*od.done(*at("in2_tok", t + 1)))
                else:
                    op.then_inc(*od.own())

        def mla_norms(c):
            nth = HEAD_CHUNKS[c]
            table = m_table[:, nth // 2, :, :, :]

            def rotate_tail(t, v):
                swapped_halves(e, od, v[:, :, HD:MQK], 4, ROPE // 2, table[:, 0, t, :], table[:, 1, t, :], rot,
                               lambda: od.done(*at("in2_tok", 4 * nth + t + 5)))
            head_norms(e, od, "in2", c, nth, nth + 2, 4, MQK, MQK, rotate_tail)

        for step in (CQ, SQ, (Q0,), Q0, SK, (Q1,), (K0,), Q1, K0, (K1,), K1):
            if isinstance(step, tuple):
                mla_norms(step[0])
            else:
                dve_turned(e, od, "in2", plan, step)
        dve_attend(e, od, att["att2"], fin_to(lambda hd: columns(v2, hd)), 8)
        dve_stick(e, od, att["stk"])
        for t in range(NT):
            dve_low(e, od, "x2", t)
        dve_out(e, od, "out2", None, "n6", 6, 1)
        dve_up(e, od, "up2", False)
        dve_out(e, od, "down2", None, "n7", 7, 1)

        def forget_gates():
            e.wait_ge(*at("fox_turned", 1))
            x = decay[:, :, :]
            e.tensor_tensor(x, bank(7, 64, 64).rearrange("p (t h) -> p t h", t=NT),
                            f_bias[:, :].unsqueeze(1).broadcast_to([P, NT, 16]), ALU.add).then_inc(*od.own())
            e.wait_ge(*od.latest())
            e.scalar_tensor_tensor(out=logf[:, :, :], in0=x, scalar=-1.0, in1=x, op0=ALU.mult, op1=ALU.max).then_inc(
                *od.done(*at("fox_abs", 1)))
            e.wait_ge(*at("fox_ln", 1))
            e.scalar_tensor_tensor(out=logf[:, :, :], in0=x, scalar=0.0, in1=logf[:, :, :], op0=ALU.min,
                                   op1=ALU.subtract).then_inc(*od.done(*at("fox_logf", 1)))
            e.wait_ge(*at("fox_decay", 1))
            e.tensor_copy(decay[:, :, :].rearrange("p a b -> p (a b)"), bank(7, 64)).then_inc(
                *od.done(*at("fox_dec_out", 1)))

        plan = t_plan(T_IN3)
        for c, nth in FOX_CHUNKS.items():
            def decays_beside(t, v):
                two = tok3[:, t, :].rearrange("p (h d) -> p h d", d=66)
                dec = decay[:, t, 8 * (nth % 2):8 * (nth % 2) + 8].unsqueeze(2)
                is_k = nth > 1
                e.memset(two[:, :, HD:HD + 1] if is_k else two[:, :, HD + 1:HD + 2], 1.0).then_inc(*od.own())
                e.tensor_scalar(two[:, :, HD + 1:HD + 2] if is_k else two[:, :, HD:HD + 1], dec,
                                -1.0 if is_k else 1.0, None, ALU.mult).then_inc(
                    *od.done(*at("in3_tok", 4 * nth + t + 1)))
            head_norms(e, od, "in3", c, nth, nth + 1, 8, HD, 66, decays_beside, None if nth else forget_gates)
            dve_turned(e, od, "in3", plan, c)
        dve_attend(e, od, att["fox"], fin_to(lambda hd: columns(v3, hd)), 8)
        for t in range(NT):
            dve_low(e, od, "x3", t)
        dve_out(e, od, "out3", None, "n8", 8, 1)
        dve_up(e, od, "up3", False)
        dve_out(e, od, "down3", None, None, None, 0)

    top.close()


def shape_constants():
    import numpy as np
    half = HD // 2
    inv = (np.float32(10000.0) ** (-np.arange(half, dtype=np.float32) / np.float32(half))).astype(np.float32)
    ang = np.arange(SEQ, dtype=np.float32)[:, None] * inv[None, :]
    cos, sin = np.cos(ang).astype(np.float32), np.sin(ang).astype(np.float32)
    mh = ROPE // 2
    inv_m = (np.float32(10000.0) ** (-np.arange(mh, dtype=np.float32) / np.float32(mh))).astype(np.float32)
    return {"rope_cos": np.concatenate([cos, cos], 1), "rope_sin": np.concatenate([-sin, sin], 1),
            "inv_freq": inv_m}


def kernel(**inputs):
    import numpy as np
    from concourse import bacc
    from concourse.bass_utils import run_bass_kernel_spmd

    nc = bacc.Bacc("TRN2", target_bir_lowering=False, num_devices=1)
    arrays, aps = {}, {}
    for name, value in {**inputs, **shape_constants()}.items():
        a = np.ascontiguousarray(value)
        arrays[f"in_{name}"] = a
        aps[name] = nc.dram_tensor(f"in_{name}", a.shape, mybir.dt.from_np(a.dtype), kind="ExternalInput").ap()
    out = nc.dram_tensor("out_dram", (1, SEQ, D), F32, kind="ExternalOutput").ap()
    build(nc, aps, out)
    r = run_bass_kernel_spmd(nc, [arrays], core_ids=[0])
    return r.results[0]["out_dram"]
```
